# Optimizing a Trainium2 kernel written in Bass

```python
import jax
import jax.numpy as jnp
from jax import lax
import numpy as np

D_MODEL = 1024
BATCH = 1
SEQ = 512
DEPTH = 2

N_A_LAYERS = DEPTH // 2
N_B_LAYERS = DEPTH - N_A_LAYERS
A_HEADS = 8
A_HEAD_DIM = D_MODEL // A_HEADS
MOBA_BLOCK = 256
MOBA_TOPK = 3
MOBA_Q_CHUNK = 64
B_HEADS = 8
QK_NOPE_DIM = 128
QK_ROPE_DIM = 64
V_HEAD_DIM = D_MODEL // B_HEADS
Q_LORA_RANK = D_MODEL // 2
KV_LORA_RANK = D_MODEL // 4
MLA_Q_BLOCK = 128
D_FF = ((8 * D_MODEL // 3 + 255) // 256) * 256
ROPE_THETA = 10000.0
NORM_EPS = 1e-6
N_SUBLAYER_NORMS = 6

kernel_name = "yoco_moba_mla_macaron_sandwich"

def rms_norm(x, g):
    xf = x.astype(jnp.float32)
    y = xf * lax.rsqrt(jnp.mean(xf * xf, axis=-1, keepdims=True) + NORM_EPS)
    return (y * g.astype(jnp.float32)).astype(x.dtype)

def rope_tables(seq_len, dim):
    inv_freq = 1.0 / (ROPE_THETA ** (jnp.arange(0, dim, 2, dtype=jnp.float32) / dim))
    ang = jnp.arange(seq_len, dtype=jnp.float32)[:, None] * inv_freq[None, :]
    return jnp.cos(ang), jnp.sin(ang)

def apply_rope(x, cos, sin):
    half = x.shape[-1] // 2
    xf = x.astype(jnp.float32)
    x1, x2 = xf[..., :half], xf[..., half:]
    return jnp.concatenate([x1 * cos - x2 * sin, x1 * sin + x2 * cos], axis=-1).astype(x.dtype)

def swiglu(h, w1, w3, w2):
    return (jax.nn.silu(h @ w1) * (h @ w3)) @ w2

def moba_attention(q, k, v):
    bsz, nh, s_len, dh = q.shape
    nb = -(-s_len // MOBA_BLOCK)
    pad = nb * MOBA_BLOCK - s_len
    k_blk = jnp.pad(k, ((0, 0), (0, 0), (0, pad), (0, 0))).reshape(bsz, nh, nb, MOBA_BLOCK, dh)
    v_blk = jnp.pad(v, ((0, 0), (0, 0), (0, pad), (0, 0))).reshape(bsz, nh, nb, MOBA_BLOCK, dh)
    k_mean = jnp.mean(k_blk.astype(jnp.float32), axis=3)
    k_sel = min(MOBA_TOPK, nb - 1)
    scale = dh ** -0.5
    key_off = jnp.arange(MOBA_BLOCK)
    n_chunks = s_len // MOBA_Q_CHUNK
    gather = jax.vmap(jax.vmap(lambda blocks, idx: blocks[idx]))

    def chunk(c):
        start = c * MOBA_Q_CHUNK
        qc = lax.dynamic_slice_in_dim(q, start, MOBA_Q_CHUNK, axis=2)
        qpos = start + jnp.arange(MOBA_Q_CHUNK)
        own = start // MOBA_BLOCK
        logits = []
        top_i = None
        if k_sel > 0:
            gate = jnp.einsum('bhqd,bhnd->bhqn', qc.astype(jnp.float32), k_mean)
            gate = jnp.where(jnp.arange(nb) < own, gate, -jnp.inf)
            _, top_i = lax.top_k(gate, k_sel)
            valid = jnp.arange(k_sel) < own
            for s in range(k_sel):
                kg = gather(k_blk, top_i[..., s])
                l = jnp.einsum('bhqd,bhqkd->bhqk', qc, kg).astype(jnp.float32) * scale
                logits.append(jnp.where(valid[s], l, -jnp.inf))
        k_own = lax.dynamic_index_in_dim(k_blk, own, axis=2, keepdims=False)
        v_own = lax.dynamic_index_in_dim(v_blk, own, axis=2, keepdims=False)
        l_own = jnp.einsum('bhqd,bhkd->bhqk', qc, k_own).astype(jnp.float32) * scale
        causal = (own * MOBA_BLOCK + key_off)[None, :] <= qpos[:, None]
        logits.append(jnp.where(causal, l_own, -jnp.inf))
        p = jax.nn.softmax(jnp.concatenate(logits, axis=-1), axis=-1).astype(v.dtype)
        out = jnp.einsum('bhqk,bhkd->bhqd', p[..., k_sel * MOBA_BLOCK:], v_own)
        for s in range(k_sel):
            vg = gather(v_blk, top_i[..., s])
            out = out + jnp.einsum('bhqk,bhqkd->bhqd', p[..., s * MOBA_BLOCK:(s + 1) * MOBA_BLOCK], vg)
        return out

    outs = lax.map(chunk, jnp.arange(n_chunks))
    return outs.transpose(1, 2, 0, 3, 4).reshape(bsz, nh, s_len, dh)

def moba_mixer(h, w_qkv, w_o, cos_h, sin_h):
    bsz, s_len, _ = h.shape
    qkv = (h @ w_qkv).reshape(bsz, s_len, 3, A_HEADS, A_HEAD_DIM)
    q = apply_rope(qkv[:, :, 0], cos_h, sin_h).transpose(0, 2, 1, 3)
    k = apply_rope(qkv[:, :, 1], cos_h, sin_h).transpose(0, 2, 1, 3)
    v = qkv[:, :, 2].transpose(0, 2, 1, 3)
    o = moba_attention(q, k, v)
    return o.transpose(0, 2, 1, 3).reshape(bsz, s_len, A_HEADS * A_HEAD_DIM) @ w_o

def mla_shared_kv(h, kv_in_norm, w_dkv_kr, kv_norm, w_ukv, cos_r, sin_r):
    bsz, s_len, _ = h.shape
    ckr = rms_norm(h, kv_in_norm) @ w_dkv_kr
    c_kv = rms_norm(ckr[..., :KV_LORA_RANK], kv_norm)
    k_rope = apply_rope(ckr[..., KV_LORA_RANK:], cos_r, sin_r)
    kv = (c_kv @ w_ukv).reshape(bsz, s_len, B_HEADS, QK_NOPE_DIM + V_HEAD_DIM)
    return kv[..., :QK_NOPE_DIM], k_rope, kv[..., QK_NOPE_DIM:]

def mla_mixer(h, w_dq, q_norm, w_uq, w_o, k_nope, k_rope, v, cos_rh, sin_rh):
    bsz, s_len, _ = h.shape
    cq = rms_norm(h @ w_dq, q_norm)
    q = (cq @ w_uq).reshape(bsz, s_len, B_HEADS, QK_NOPE_DIM + QK_ROPE_DIM)
    q_nope = q[..., :QK_NOPE_DIM]
    q_rope = apply_rope(q[..., QK_NOPE_DIM:], cos_rh, sin_rh)
    scale = (QK_NOPE_DIM + QK_ROPE_DIM) ** -0.5
    kpos = jnp.arange(s_len)

    def block(i):
        s0 = i * MLA_Q_BLOCK
        qn = lax.dynamic_slice_in_dim(q_nope, s0, MLA_Q_BLOCK, axis=1)
        qr = lax.dynamic_slice_in_dim(q_rope, s0, MLA_Q_BLOCK, axis=1)
        logits = (jnp.einsum('bqhd,bkhd->bhqk', qn, k_nope)
                  + jnp.einsum('bqhd,bkd->bhqk', qr, k_rope)).astype(jnp.float32) * scale
        qpos = s0 + jnp.arange(MLA_Q_BLOCK)
        logits = jnp.where(kpos[None, :] <= qpos[:, None], logits, -jnp.inf)
        p = jax.nn.softmax(logits, axis=-1).astype(v.dtype)
        return jnp.einsum('bhqk,bkhd->bqhd', p, v)

    o = lax.map(block, jnp.arange(s_len // MLA_Q_BLOCK))
    o = o.transpose(1, 0, 2, 3, 4).reshape(bsz, s_len, B_HEADS * V_HEAD_DIM)
    return o @ w_o

def setup_inputs(seed: int = 0) -> dict:
    key = jax.random.key(seed)
    ks = jax.random.split(key, 20)

    def w(k, shape, fan_in):
        return jax.random.normal(k, shape, jnp.float32) * fan_in ** -0.5

    def gain(k, shape):
        return 1.0 + 0.02 * jax.random.normal(k, shape, jnp.float32)

    return {
        'x': jax.random.normal(ks[0], (BATCH, SEQ, D_MODEL), jnp.float32),
        'norm_gains': gain(ks[1], (DEPTH, N_SUBLAYER_NORMS, D_MODEL)),
        'ffn_w1': w(ks[2], (DEPTH, 2, D_MODEL, D_FF), D_MODEL),
        'ffn_w3': w(ks[3], (DEPTH, 2, D_MODEL, D_FF), D_MODEL),
        'ffn_w2': w(ks[4], (DEPTH, 2, D_FF, D_MODEL), D_FF),
        'moba_w_qkv': w(ks[5], (N_A_LAYERS, D_MODEL, 3 * A_HEADS * A_HEAD_DIM), D_MODEL),
        'moba_w_o': w(ks[6], (N_A_LAYERS, A_HEADS * A_HEAD_DIM, D_MODEL), A_HEADS * A_HEAD_DIM),
        'mla_w_dq': w(ks[7], (N_B_LAYERS, D_MODEL, Q_LORA_RANK), D_MODEL),
        'mla_q_norm': gain(ks[8], (N_B_LAYERS, Q_LORA_RANK)),
        'mla_w_uq': w(ks[9], (N_B_LAYERS, Q_LORA_RANK, B_HEADS * (QK_NOPE_DIM + QK_ROPE_DIM)), Q_LORA_RANK),
        'mla_w_o': w(ks[10], (N_B_LAYERS, B_HEADS * V_HEAD_DIM, D_MODEL), B_HEADS * V_HEAD_DIM),
        'kv_in_norm': gain(ks[11], (D_MODEL,)),
        'w_dkv_kr': w(ks[12], (D_MODEL, KV_LORA_RANK + QK_ROPE_DIM), D_MODEL),
        'kv_norm': gain(ks[13], (KV_LORA_RANK,)),
        'w_ukv': w(ks[14], (KV_LORA_RANK, B_HEADS * (QK_NOPE_DIM + V_HEAD_DIM)), KV_LORA_RANK),
    }

def reference(x, norm_gains, ffn_w1, ffn_w3, ffn_w2, moba_w_qkv, moba_w_o, mla_w_dq, mla_q_norm,
              mla_w_uq, mla_w_o, kv_in_norm, w_dkv_kr, kv_norm, w_ukv):
    s_len = x.shape[1]
    cos_a, sin_a = rope_tables(s_len, A_HEAD_DIM)
    cos_r, sin_r = rope_tables(s_len, QK_ROPE_DIM)
    k_nope = k_rope = v_sh = None
    for l in range(DEPTH):
        g = norm_gains[l]
        x = x + 0.5 * rms_norm(swiglu(rms_norm(x, g[0]), ffn_w1[l, 0], ffn_w3[l, 0], ffn_w2[l, 0]), g[1])
        hn = rms_norm(x, g[2])
        if l < N_A_LAYERS:
            mix = moba_mixer(hn, moba_w_qkv[l], moba_w_o[l], cos_a[:, None, :], sin_a[:, None, :])
        else:
            j = l - N_A_LAYERS
            mix = mla_mixer(hn, mla_w_dq[j], mla_q_norm[j], mla_w_uq[j], mla_w_o[j],
                            k_nope, k_rope, v_sh, cos_r[:, None, :], sin_r[:, None, :])
        x = x + rms_norm(mix, g[3])
        x = x + 0.5 * rms_norm(swiglu(rms_norm(x, g[4]), ffn_w1[l, 1], ffn_w3[l, 1], ffn_w2[l, 1]), g[5])
        if l == N_A_LAYERS - 1:
            k_nope, k_rope, v_sh = mla_shared_kv(x, kv_in_norm, w_dkv_kr, kv_norm, w_ukv, cos_r, sin_r)
    return x


_drawn_inputs = setup_inputs


def setup_inputs(seed=0):
    import zlib

    import numpy as np

    out = dict(_drawn_inputs(seed))
    spreads = {}
    factors = {'mla_q_norm': 8.0, 'kv_in_norm': 5.434, 'kv_norm': 5.03}
    for name, (base, spread) in spreads.items():
        noise = np.random.default_rng([zlib.crc32(name.encode()), seed]).standard_normal(out[name].shape)
        drawn = base * np.exp(spread * noise) if base else spread * noise
        out[name] = jnp.asarray(drawn.astype(out[name].dtype))
    for name, factor in factors.items():
        out[name] = (out[name] * factor).astype(out[name].dtype)
    return out
```

```python
from contextlib import ExitStack

import concourse.bass as bass
from concourse import mybir

ALU = mybir.AluOpType
ACT = mybir.ActivationFunctionType
F32 = mybir.dt.float32
F32R = mybir.dt.float32r
AX_X = mybir.AxisListType.X

P = 128
SLOTS = 4
UT = 8
NEG = -3.0e38


def yoco_kernel(nc: bass.Bass, x, norm_gains, ffn_w1, ffn_w3, ffn_w2, moba_w_qkv, moba_w_o, mla_w_dq,
                mla_q_norm, mla_w_uq, mla_w_o, kv_in_norm, w_dkv_kr, kv_norm, w_ukv,
                rope_a, rope_r, out):
    _, S, D = x.shape
    L, _, _, FF = ffn_w1.shape
    KD = D // P
    KF = FF // P
    TS = S // P
    HEADS = moba_w_o.shape[1] // P
    QR = mla_w_dq.shape[2]
    KQ = QR // P
    KVR = kv_norm.shape[0]
    KK = KVR // P
    ROPE = w_dkv_kr.shape[1] - KVR
    HQ = P + ROPE
    A_SCALE = float(P) ** -0.5
    B_SCALE = float(HQ) ** -0.5
    EPS = 1e-6
    DOWN = [min(UT, KF - s) for s in range(0, KF, UT)]
    ND = len(DOWN)
    assert KD == UT and KF == 22 and ND == 3 and TS == 4 and HEADS == 8 and ROPE == 64 and KQ == 4 and KK == 2

    FFN_U = [(UT, 1)] * (2 * KF) + [(n, 1) for n in DOWN] * KD
    MOBA_U = [(UT, 1)] * (3 * HEADS + KD)
    KV_U = [(UT, 1)] * KK + [(UT // 2, 2)] * 2
    MLA_U = [(UT, 1)] * KQ + [(KQ, 2), (UT, 3), (UT, 3)] * (HEADS // 2) + [(UT, 1)] * KD
    stages = [FFN_U, MOBA_U, FFN_U, KV_U, FFN_U, MLA_U, FFN_U]
    results = [2 * KF + KD, 3 * HEADS + KD, 2 * KF + KD, KK + 1, 2 * KF + KD,
               KQ + 7 * (HEADS // 2) + KD, 2 * KF + KD]
    units = [u for s in stages for u in s]
    NU = len(units)
    U0 = [sum(len(s) for s in stages[:i]) for i in range(len(stages))]
    R0 = [sum(results[:i]) for i in range(len(stages))]
    assert all(u % SLOTS == 0 for u in U0)
    landed = []
    for u, (_, dmas) in enumerate(units):
        landed.append((landed[u - SLOTS] if u >= SLOTS else 0) + 16 * dmas)
    FFN_STAGE = {0: 0, 2: 1, 4: 2, 6: 3}

    NORM_TILES = [KD, KD, KD, KD, KD, KD, KD, KD, KD, KK, KQ, KD, KD, KD]
    A0 = [sum(n + 1 for n in NORM_TILES[:i]) for i in range(len(NORM_TILES) + 1)]
    X_LOAD, X_F0, X_MOBA, X_F1, X_F2, X_MLA, X_F3 = range(7)
    XG0 = [KD * i for i in (0, 1, 2, 3, 5, 6, 7)]

    def gain(layer, s, k):
        return (layer * 6 + s) * KD + k
    G_KVIN = L * 6 * KD
    G_Q = G_KVIN + KD
    G_KV = G_Q + KQ
    NG = G_KV + KK

    with ExitStack() as ctx:
        base = [(nc.sbuf_base + 63) // 64 * 64]

        def at(name, shape, dt, offset):
            return nc.alloc_sbuf_tensor_at(name, shape, dt, offset=offset)

        def sb(name, shape, dt=F32):
            n = 4
            for d in shape[1:]:
                n *= d
            o = base[0]
            base[0] += (n + 31) // 32 * 32
            return at(name, shape, dt, o)

        xT = sb("xT", [P, KD, S])
        xg_base = base[0]
        xg = sb("xg", [P, 2, KD, S], F32R)
        y = at("y", [P, KD, S], F32, xg_base + 4 * KD * S)
        raw = sb("raw", [P, SLOTS, UT, P])
        wh = sb("wh", [P, SLOTS, UT, P], F32R)
        wl = sb("wl", [P, SLOTS, UT, P], F32R)
        h_base = base[0]
        hT = sb("hT", [P, 2, KF, S], F32R)
        ck = sb("ck", [P, KK + 1, S])
        Rb = sb("Rb", [P, S])
        sumsq = sb("sumsq", [P, S])
        T = [sb(f"tmp{i}", [P, S]) for i in range(4)]
        gains = sb("gains", [P, P])
        ident = sb("ident", [P, P])
        ones = sb("ones", [P, P])
        mean_w = {n: sb(f"mean_w{n}", [P, 1]) for n in (D, QR, KVR)}
        var = sb("var", [P, TS])
        neghalf = sb("neghalf", [P, TS])
        rtok = sb("rtok", [P, TS])
        mx = sb("mx", [P, TS])
        nmx = sb("nmx", [P, TS])
        psums = sb("psums", [P, TS])
        rsums = sb("rsums", [P, TS])
        assert base[0] <= nc.sbuf_usable_end, base[0]

        spot = [h_base]

        def over(name, shape, dt=F32):
            n = 4
            for d in shape[1:]:
                n *= d
            o = spot[0]
            spot[0] += n
            assert spot[0] <= h_base + 4 * 2 * KF * S
            return at(name, shape, dt, o)

        xin = at("xin", [P, TS, D], F32, h_base)
        gin = at("gin", [P, P], F32, h_base + 4 * TS * D)
        xout = at("xout", [P, KD, TS, P], F32, h_base)
        cosT = over("cosT", [P, S])
        sinT = over("sinT", [P, S])
        xkv = at("xkv", [P, 2, KD, S], F32R, spot[0])
        cosR = over("cosR", [P, S])
        sinR = over("sinR", [P, S])
        qh = over("qh", [P, 2, S], F32R)
        kh = over("kh", [P, 2, S], F32R)
        vh = over("vh", [P, 2, TS, P], F32R)
        POFF = [P * c * (c + 1) // 2 for c in range(TS + 1)]
        prob = over("prob", [P, POFF[TS]])
        TOFF = [sum((TS - i) * P for i in range(j)) for j in range(TS + 1)]
        probT = over("probT", [P, 2, TOFF[TS]], F32R)
        oT_at = spot[0]
        oT = over("oT", [P, 2, HEADS, S], F32R)
        cq = at("cq", [P, KQ, S], F32, oT_at)
        mask = over("mask", [P, P])
        Rq = over("Rq", [P, S])
        Rkv = over("Rkv", [P, S])
        krT = over("krT", [P, 2, S], F32R)
        qrT = over("qrT", [P, 2, S], F32R)
        ckT = over("ckT", [P, 2, KK, S], F32R)

        BANK = [(0, 0), (0, P), (1, 0), (2, 0)]
        TBANK = [(TOFF[0], TOFF[1]), (TOFF[1], TOFF[2]), (TOFF[2], TOFF[4])]

        acc = [ctx.enter_context(nc.psum_tensor(f"acc{i}", [P, S], F32)) for i in range(4)]
        aux = ctx.enter_context(nc.psum_tensor("aux", [P, S], F32))
        sco = [ctx.enter_context(nc.psum_tensor(f"sco{i}", [P, S], F32)) for i in range(3)]

        def sem(name):
            return ctx.enter_context(nc.semaphore(name))

        raw_full = [sem(f"raw_full{i}") for i in range(SLOTS)]
        w_hi = sem("w_hi")
        w_lo = sem("w_lo")
        unit_done = sem("unit_done")
        evacuated = sem("evacuated")
        const_ready = sem("const_ready")
        gains_in = sem("gains_in")
        gains_psum = sem("gains_psum")
        gains_ready = sem("gains_ready")
        x_in = [sem(f"x_in{k}") for k in range(KD)]
        x_psum = sem("x_psum")
        x_ready = sem("x_ready")
        xhi_ready = sem("xhi_ready")
        xg_ready = sem("xg_ready")
        yr_ready = sem("yr_ready")
        sq_ready = sem("sq_ready")
        sumsq_added = sem("sumsq_added")
        var_psum = sem("var_psum")
        var_ready = sem("var_ready")
        rtok_ready = sem("rtok_ready")
        diag_ready = sem("diag_ready")
        r_psum = sem("r_psum")
        r_ready = sem("r_ready")
        silu_ready = sem("silu_ready")
        hid_ready = sem("hid_ready")
        hid_hi = sem("hid_hi")
        hid_lo = sem("hid_lo")
        table_in = sem("table_in")
        mask_ready = sem("mask_ready")
        table_ready = sem("table_ready")
        swapped = sem("swapped")
        roped = sem("roped")
        part_hi = sem("part_hi")
        part_lo = sem("part_lo")
        vT_psum = sem("vT_psum")
        v_hi = sem("v_hi")
        v_lo = sem("v_lo")
        score_psum = sem("score_psum")
        softmax_step = sem("softmax_step")
        nmx_ready = sem("nmx_ready")
        exp_ready = sem("exp_ready")
        prob_ready = sem("prob_ready")
        probT_psum = sem("probT_psum")
        probT_hi = sem("probT_hi")
        probT_lo = sem("probT_lo")
        pv_psum = sem("pv_psum")
        o_hi = sem("o_hi")
        o_lo = sem("o_lo")
        cq_hi = sem("cq_hi")
        cq_lo = sem("cq_lo")
        out_copied = sem("out_copied")
        stored = sem("stored")

        block = ctx.enter_context(nc.Block())

        def f32(ap):
            return ap.bitcast(F32)

        def fresh(u):
            return u % SLOTS, units[u][0]

        @block.sync
        def _(sp):
            def slot_free(u):
                if isinstance(u, int) and u < SLOTS:
                    return
                sp.wait_ge(w_lo, u - SLOTS + 1)

            def load(slot, j, src):
                n = src.shape[1]
                w = src.shape[2]
                sp.dma_start(raw[:, slot, j:j + n, 0:w], src).then_inc(raw_full[slot], 16)

            def kpn(w):
                return w.rearrange("(k p) n -> p k n", p=P)

            def ffn(st, layer, i):
                w1, w3 = kpn(ffn_w1[layer, i]), kpn(ffn_w3[layer, i])
                w2 = kpn(ffn_w2[layer, i])

                def up(it):
                    for j in range(2):
                        for a, w in enumerate((w1, w3)):
                            slot_free(U0[st] + 4 * it + 2 * j + a)
                            load(2 * j + a, 0, w[:, :, bass.ds((2 * it + j) * P, P)])

                up(0)
                with sp.Fori(1, KF // 2) as it:
                    up(it)
                with sp.Fori(0, KD // 4) as it:
                    for m in range(4):
                        for s in range(ND):
                            u = ND * m + s
                            slot_free(U0[st] + 2 * KF + 4 * ND * it + u)
                            load(u % SLOTS, 0, w2[:, UT * s:UT * s + DOWN[s], bass.ds((4 * it + m) * P, P)])

            def plain(u0, w, cols):
                for n, c in enumerate(cols):
                    slot_free(u0 + n)
                    load((u0 + n) % SLOTS, 0, w[:, :, c:c + P])

            ffn(0, 0, 0)
            qkv = kpn(moba_w_qkv[0])
            plain(U0[1], qkv, [HEADS * P * a + P * h for h in range(HEADS) for a in range(3)])
            plain(U0[1] + 3 * HEADS, kpn(moba_w_o[0]), range(0, D, P))
            ffn(2, 0, 1)
            dkv = kpn(w_dkv_kr)
            plain(U0[3], dkv, range(0, KVR, P))
            for half in range(2):
                u = U0[3] + KK + half
                slot_free(u)
                for c in range(2):
                    sp.dma_start(raw[:, u % SLOTS, 0:UT // 2, c * ROPE:(c + 1) * ROPE],
                                 dkv[:, half * UT // 2:(half + 1) * UT // 2, KVR:KVR + ROPE]
                                 ).then_inc(raw_full[u % SLOTS], 16)
            ffn(4, 1, 0)
            plain(U0[5], kpn(mla_w_dq[0]), range(0, QR, P))
            uq, ukv = kpn(mla_w_uq[0]), kpn(w_ukv)
            u = U0[5] + KQ
            for g in range(HEADS // 2):
                slot_free(u)
                for c in range(2):
                    r = HQ * (2 * g + c) + P
                    sp.dma_start(raw[:, u % SLOTS, 0:KQ, c * ROPE:(c + 1) * ROPE],
                                 uq[:, :, r:r + ROPE]).then_inc(raw_full[u % SLOTS], 16)
                u += 1
                for h in (2 * g, 2 * g + 1):
                    slot_free(u)
                    load(u % SLOTS, 0, uq[:, :, HQ * h:HQ * h + P])
                    load(u % SLOTS, KQ, ukv[:, :, 2 * P * h:2 * P * h + P])
                    load(u % SLOTS, KQ + KK, ukv[:, :, 2 * P * h + P:2 * P * (h + 1)])
                    u += 1
            plain(u, kpn(mla_w_o[0]), range(0, D, P))
            ffn(6, 1, 1)
            ov = out[0].rearrange("(c p) (k f) -> p k c f", p=P, f=P)
            for k in range(KD):
                sp.wait_ge(out_copied, k + 1)
                sp.dma_start(ov[:, k], xout[:, k]).then_inc(stored, 16)
            sp.wait_ge(stored, 16 * KD)

        @block.gpsimd
        def _(pool):
            g = nc.gpsimd
            g.memset(ident[:], 0.0).then_inc(const_ready, 1)
            pool.wait_ge(const_ready, 1)
            g.affine_select(out=ident[:], in_=ident[:], compare_op=ALU.not_equal, fill=1.0, base=0,
                            pattern=[[-1, P]], channel_multiplier=1).then_inc(const_ready, 1)
            g.memset(ones[:], 1.0)
            for n, t in mean_w.items():
                g.memset(t[:], 1.0 / n)
            g.memset(neghalf[:], -0.5).then_inc(const_ready, 1)

            def norm(n):
                pool.wait_ge(var_ready, n + 1)
                g.tensor_tensor(rtok[:], var[:], neghalf[:], ALU.pow).then_inc(rtok_ready, 1)

            def scale_y(n):
                pool.wait_ge(r_ready, n + 1)
                for m in range(KD):
                    g.tensor_tensor(y[:, m], y[:, m], Rb[:], ALU.mult).then_inc(yr_ready, 1)

            def rope_add(count, dst):
                pool.wait_ge(swapped, count)
                g.tensor_tensor(dst, T[0][:], T[2][:], ALU.add).then_inc(roped, 1)

            def causal_mask(count, free_after):
                pool.wait_ge(unit_done, free_after)
                g.memset(mask[:], 0.0).then_inc(mask_ready, 1)
                pool.wait_ge(mask_ready, count)
                g.affine_select(out=mask[:], in_=mask[:], compare_op=ALU.is_ge, fill=NEG, base=0,
                                pattern=[[-1, P]], channel_multiplier=1).then_inc(mask_ready, 1)

            norm(0)
            norm(1)
            scale_y(1)
            causal_mask(1, U0[1])
            norm(2)
            for h in range(HEADS):
                rope_add(4 * h + 2, T[3][:])
                rope_add(4 * h + 4, T[3][:])
            norm(3)
            scale_y(3)
            norm(4)
            norm(5)
            scale_y(5)
            norm(6)
            rope_add(4 * HEADS + 4, ck[:, KK])
            norm(7)
            scale_y(7)
            causal_mask(3, U0[5])
            norm(8)
            norm(9)
            norm(10)
            for gg in range(HEADS // 2):
                rope_add(4 * HEADS + 4 * (gg + 2), T[3][:])
            norm(11)
            scale_y(11)
            norm(12)
            norm(13)
            scale_y(13)

        @block.scalar
        def _(act):
            s = nc.scalar
            COPY, SQUARE, EXP, SILU = ACT.Copy, ACT.Square, ACT.Exp, ACT.Silu

            def split_hi(slot, tiles, u, count):
                act.wait_ge(raw_full[slot], count)
                if not (isinstance(u, int) and u < SLOTS):
                    act.wait_ge(unit_done, u - SLOTS + 1)
                s.activation(wh[:, slot, 0:tiles], raw[:, slot, 0:tiles], COPY).then_inc(w_hi, 1)

            def split(u):
                if u < NU:
                    slot, tiles = fresh(u)
                    split_hi(slot, tiles, u, landed[u])

            def square(n, i, src):
                if i >= 2:
                    act.wait_ge(sumsq_added, A0[n] + i)
                elif n:
                    act.wait_ge(sumsq_added, A0[n])
                s.activation(T[i % 2][:], src, SQUARE).then_inc(sq_ready, 1)

            def x_update(t, targets):
                for a, (gcol, dst) in enumerate(targets):
                    for m in range(KD):
                        act.wait_ge(x_ready, KD * t + m + 1)
                        s.activation(dst[:, 0, m], xT[:, m], COPY, scale=gains[:, gcol + m:gcol + m + 1]
                                     ).then_inc(xhi_ready, 1)

            def x_squares(n):
                for m in range(KD):
                    square(n, m, xT[:, m])

            def ffn(st, n_post):
                F0 = KF * FFN_STAGE[st]
                sq0 = sum(NORM_TILES[:n_post])

                def up(it):
                    for j in range(2):
                        for a in range(2):
                            v = 2 * j + a + 2
                            split_hi(v % SLOTS, UT, U0[st] + 4 * it + v, landed[U0[st] + v] + 16 * it)
                        act.wait_ge(evacuated, R0[st] + 4 * it + 2 * j + 1)
                        s.activation(T[1][:], T[0][:], SILU).then_inc(silu_ready, 1)
                        act.wait_ge(hid_ready, F0 + 2 * it + j + 1)
                        s.activation(hT[:, 0, bass.ds(2 * it + j, 1)].rearrange("p a s -> p (a s)"),
                                     T[3][:], COPY).then_inc(hid_hi, 1)

                up(0)
                with act.Fori(1, KF // 2) as it:
                    up(it)

                def down(it, last=False):
                    for m in range(4):
                        for v in range(ND * m + 2, ND * m + 2 + ND):
                            if last and v >= 4 * ND:
                                continue
                            tiles = DOWN[v % ND]
                            split_hi(v % SLOTS, tiles, U0[st] + 2 * KF + 4 * ND * it + v,
                                     landed[U0[st] + 2 * KF + v] + 16 * ND * it)
                        act.wait_ge(evacuated, R0[st] + 2 * KF + 4 * it + m + 1)
                        act.wait_ge(sumsq_added, A0[n_post] + 4 * it + m + 1)
                        s.activation(T[0][:], y[:, bass.ds(4 * it + m, 1)].rearrange("p a s -> p (a s)"),
                                     SQUARE).then_inc(sq_ready, 1)

                if st == len(stages) - 1:
                    down(0)
                    down(1, last=True)
                else:
                    with act.Fori(0, KD // 4) as it:
                        down(it)

            def exchange(r, width):
                act.wait_ge(evacuated, r + 1)
                for b in range(0, P, 2 * width):
                    for i, o in ((b + width, b), (b, b + width)):
                        s.activation(T[2][o:o + width], T[1][i:i + width], COPY).then_inc(swapped, 1)

            def part(n, dst):
                s.activation(dst, T[3][:], COPY).then_inc(part_hi, 1)

            def softmax_exp(h, scale):
                act.wait_ge(nmx_ready, h + 1)
                for c in range(TS):
                    bank, o = BANK[c]
                    s.activation(prob[:, POFF[c]:POFF[c + 1]], sco[bank][:, o:o + (c + 1) * P], EXP,
                                 bias=nmx[:, c:c + 1], scale=scale, accum_out=psums[:, c:c + 1]
                                 ).then_inc(exp_ready, 1)

            def probT_split(h):
                for b, (lo, hi) in enumerate(TBANK):
                    act.wait_ge(probT_psum, 3 * h + b + 1)
                    s.activation(probT[:, 0, lo:hi], sco[b][:, 0:hi - lo], COPY).then_inc(probT_hi, 1)

            def o_split(h):
                act.wait_ge(pv_psum, h + 1)
                s.activation(oT[:, 0, h % HEADS], aux[:], COPY).then_inc(o_hi, 1)

            def v_split(h):
                act.wait_ge(vT_psum, h + 1)
                s.activation(vh[:, 0], sco[2][:].rearrange("p (t d) -> p t d", d=P), COPY).then_inc(v_hi, 1)

            def out_proj(st, u, r, n):
                for m in range(KD):
                    split(u + m + 2)
                    act.wait_ge(evacuated, r + m + 1)
                    square(n, m, y[:, m])

            for k in range(2):
                s.dma_start(xin[:, :, k * P:(k + 1) * P],
                            x[0].rearrange("(c p) d -> p c d", p=P)[:, :, k * P:(k + 1) * P]
                            ).then_inc(x_in[k], 16)
            s.dma_start(gin[0:G_KVIN], norm_gains.rearrange("l s (k f) -> (l s k) f", f=P)).then_inc(gains_in, 16)
            s.dma_start(gin[G_KVIN:G_Q], kv_in_norm.rearrange("(k f) -> k f", f=P)).then_inc(gains_in, 16)
            s.dma_start(gin[G_Q:G_KV], mla_q_norm.rearrange("a (k f) -> (a k) f", f=P)).then_inc(gains_in, 16)
            s.dma_start(gin[G_KV:NG], kv_norm.rearrange("(k f) -> k f", f=P)).then_inc(gains_in, 16)
            for k in range(2, KD):
                s.dma_start(xin[:, :, k * P:(k + 1) * P],
                            x[0].rearrange("(c p) d -> p c d", p=P)[:, :, k * P:(k + 1) * P]
                            ).then_inc(x_in[k], 16)
            split(0)
            split(1)
            act.wait_ge(gains_ready, 1)
            x_update(X_LOAD, [(gain(0, 0, 0), xg)])
            x_squares(0)
            ffn(0, 1)

            act.wait_ge(unit_done, U0[1])
            s.dma_start(cosT[:], rope_a[0]).then_inc(table_in, 16)
            s.dma_start(sinT[:], rope_a[1]).then_inc(table_in, 16)
            x_update(X_F0, [(gain(0, 2, 0), xg)])
            x_squares(2)
            u, r = U0[1], R0[1]

            def qk(h, i):
                split(u + 3 * h + i + 2)
                exchange(r + 3 * h + i, P // 2)
                act.wait_ge(roped, 2 * h + i + 1)
                part(2 * h + i, (qh, kh)[i][:, 0])

            qk(0, 0)
            qk(0, 1)
            split(u + 4)
            v_split(0)
            for h in range(HEADS):
                nxt = h + 1 < HEADS
                if nxt:
                    split(u + 3 * h + 5)
                softmax_exp(h, A_SCALE)
                if nxt:
                    exchange(r + 3 * h + 3, P // 2)
                    act.wait_ge(roped, 2 * h + 3)
                    part(2 * h + 2, qh[:, 0])
                    qk(h + 1, 1)
                probT_split(h)
                if nxt:
                    split(u + 3 * h + 7)
                o_split(h)
                if nxt:
                    v_split(h + 1)
            out_proj(1, U0[1] + 3 * HEADS, R0[1] + 3 * HEADS, 3)
            x_update(X_MOBA, [(gain(0, 4, 0), xg)])
            x_squares(4)
            ffn(2, 5)

            act.wait_ge(unit_done, U0[3])
            s.dma_start(cosT[:], rope_r[0]).then_inc(table_in, 16)
            s.dma_start(sinT[:], rope_r[1]).then_inc(table_in, 16)
            x_update(X_F1, [(G_KVIN, xkv), (gain(1, 0, 0), xg)])
            x_squares(6)
            u, r = U0[3], R0[3]
            for m in range(KK):
                split(u + m + 2)
            split(u + KK + 2)
            split(u + KK + 3)
            exchange(r + KK, ROPE // 2)
            ffn(4, 7)

            act.wait_ge(unit_done, U0[5])
            s.dma_start(cosT[:], rope_r[0]).then_inc(table_in, 16)
            s.dma_start(sinT[:], rope_r[1]).then_inc(table_in, 16)
            x_update(X_F2, [(gain(1, 2, 0), xg)])
            x_squares(8)
            u, r = U0[5], R0[5]
            for i in range(KK):
                square(9, i, ck[:, i])
            for i in range(KK):
                s.activation(ckT[:, 0, i], ck[:, i], COPY, scale=gains[:, G_KV + i:G_KV + i + 1]
                             ).then_inc(cq_hi, 1)
            s.activation(krT[:, 0], ck[:, KK], COPY).then_inc(cq_hi, 1)
            for m in range(KQ):
                split(u + m + 2)
            for m in range(KQ):
                act.wait_ge(evacuated, r + m + 1)
                square(10, m, cq[:, m])
            act.wait_ge(unit_done, u + KQ)
            for m in range(KQ):
                s.activation(xg[:, 0, m], cq[:, m], COPY, scale=gains[:, G_Q + m:G_Q + m + 1]
                             ).then_inc(cq_hi, 1)

            def rotated(gg, pn):
                exchange(r + KQ + 7 * gg, ROPE // 2)
                act.wait_ge(roped, 2 * HEADS + 2 + gg)
                part(pn, qrT[:, 0])

            def plain_part(rr, pn, dst):
                act.wait_ge(evacuated, rr + 1)
                part(pn, dst)

            split(u + KQ + 2)
            rotated(0, 0)
            split(u + KQ + 3)
            r1 = r + KQ + 1
            plain_part(r1, 1, qh[:, 0])
            plain_part(r1 + 1, 2, kh[:, 0])
            v_split(HEADS)
            for h in range(HEADS):
                nxt = h + 1 < HEADS
                gg = (h + 1) // 2
                nu = u + KQ + 3 * gg + 1 + (h + 1) % 2
                r1 = r + KQ + 7 * gg + 1 + 3 * ((h + 1) % 2)
                if nxt and h % 2:
                    split(nu + 1)
                softmax_exp(HEADS + h, B_SCALE)
                if nxt:
                    if h % 2:
                        rotated(gg, 0)
                    split(nu + 2)
                    plain_part(r1, 1, qh[:, 0])
                    plain_part(r1 + 1, 2, kh[:, 0])
                probT_split(HEADS + h)
                o_split(HEADS + h)
                if nxt:
                    v_split(HEADS + h + 1)
            out_proj(5, u + KQ + 12, r + KQ + 28, 11)
            x_update(X_MLA, [(gain(1, 4, 0), xg)])
            x_squares(12)
            ffn(6, 13)

        @block.vector
        def _(dve):
            v = nc.vector

            def split_lo(slot, tiles, u):
                dve.wait_ge(w_hi, u + 1)
                v.tensor_tensor(wl[:, slot, 0:tiles], raw[:, slot, 0:tiles], f32(wh[:, slot, 0:tiles]),
                                ALU.subtract).then_inc(w_lo, 1)

            def split(u):
                if u < NU:
                    slot, tiles = fresh(u)
                    split_lo(slot, tiles, u)

            def clear_sumsq(n):
                v.memset(sumsq[:], 0.0).then_inc(sumsq_added, 1)

            def add_square(n, i, buf):
                dve.wait_ge(sq_ready, sum(NORM_TILES[:n]) + i + 1)
                dve.wait_ge(sumsq_added, A0[n] + i + 1)
                v.tensor_tensor(sumsq[:], sumsq[:], T[buf][:], ALU.add).then_inc(sumsq_added, 1)

            def norm(n, factor, dst):
                dve.wait_ge(var_psum, n + 1)
                v.tensor_scalar(var[:], aux[:, 0:TS], EPS, None, ALU.add).then_inc(var_ready, 1)
                dve.wait_ge(rtok_ready, n + 1)
                v.scalar_tensor_tensor(out=T[3][:].rearrange("p (t q) -> p t q", q=P),
                                       in0=ident[:].unsqueeze(1).broadcast_to([P, TS, P]), scalar=factor,
                                       in1=rtok[:].unsqueeze(2).broadcast_to([P, TS, P]),
                                       op0=ALU.mult, op1=ALU.mult).then_inc(diag_ready, 1)
                dve.wait_ge(r_psum, n + 1)
                v.tensor_copy(dst[:], aux[:]).then_inc(r_ready, 1)

            def gated_split(t, a, m, gcol, dst):
                dve.wait_ge(xhi_ready, XG0[t] + KD * a + m + 1)
                v.scalar_tensor_tensor(out=dst[:, 1, m], in0=xT[:, m], scalar=gains[:, gcol + m:gcol + m + 1],
                                       in1=f32(dst[:, 0, m]), op0=ALU.mult, op1=ALU.subtract
                                       ).then_inc(xg_ready, 1)

            def x_update(t, n_post, g_post, targets):
                for m in range(KD + 1):
                    if m < KD:
                        dve.wait_ge(yr_ready, KD * (t - 1) + m + 1)
                        v.scalar_tensor_tensor(out=xT[:, m], in0=y[:, m], scalar=gains[:, g_post + m:g_post + m + 1],
                                               in1=xT[:, m], op0=ALU.mult, op1=ALU.add).then_inc(x_ready, 1)
                    if m and targets:
                        dve.wait_ge(x_ready, KD * t + m)
                        gated_split(t, 0, m - 1, *targets[0])
                for a in range(1, len(targets)):
                    for m in range(KD):
                        gated_split(t, a, m, *targets[a])

            def x_squares(n):
                clear_sumsq(n)
                for m in range(KD):
                    add_square(n, m, m % 2)

            def ffn(st, n_pre, n_post, factor_pre=1.0):
                F0 = KF * FFN_STAGE[st]
                sq0 = sum(NORM_TILES[:n_post])

                def up(it, pre=False):
                    for j in range(2):
                        for a in range(2):
                            w = 2 * j + a + 2
                            split_lo(w % SLOTS, UT, U0[st] + 4 * it + w)
                        if pre and j == 0:
                            norm(n_pre, 1.0, Rb)
                            dve.wait_ge(r_ready, n_pre + 1)
                        f = F0 + 2 * it + j
                        dve.wait_ge(unit_done, U0[st] + 4 * it + 2 * j + 1)
                        v.tensor_tensor(T[0][:], acc[2 * j][:], Rb[:], ALU.mult).then_inc(evacuated, 1)
                        dve.wait_ge(unit_done, U0[st] + 4 * it + 2 * j + 2)
                        v.tensor_tensor(T[2][:], acc[2 * j + 1][:], Rb[:], ALU.mult).then_inc(evacuated, 1)
                        dve.wait_ge(evacuated, R0[st] + 4 * it + 2 * j + 2)
                        dve.wait_ge(silu_ready, f + 1)
                        v.tensor_tensor(T[3][:], T[1][:], T[2][:], ALU.mult).then_inc(hid_ready, 1)
                        dve.wait_ge(hid_ready, f + 1)
                        dve.wait_ge(hid_hi, f + 1)
                        at_ = bass.ds(2 * it + j, 1)
                        v.tensor_tensor(hT[:, 1, at_].rearrange("p a s -> p (a s)"), T[3][:],
                                        f32(hT[:, 0, at_].rearrange("p a s -> p (a s)")),
                                        ALU.subtract).then_inc(hid_lo, 1)

                up(0, pre=n_pre is not None)
                with dve.Fori(1, KF // 2) as it:
                    up(it)
                clear_sumsq(n_post)

                def down(it, last=False):
                    for m in range(4):
                        for w in range(ND * m + 2, ND * m + 2 + ND):
                            if last and w >= 4 * ND:
                                continue
                            split_lo(w % SLOTS, DOWN[w % ND], U0[st] + 2 * KF + 4 * ND * it + w)
                        dve.wait_ge(unit_done, U0[st] + 2 * KF + 4 * ND * it + ND * (m + 1))
                        v.tensor_copy(y[:, bass.ds(4 * it + m, 1)].rearrange("p a s -> p (a s)"), acc[m][:]
                                      ).then_inc(evacuated, 1)
                        dve.wait_ge(sq_ready, sq0 + 4 * it + m + 1)
                        dve.wait_ge(sumsq_added, A0[n_post] + 4 * it + m + 1)
                        v.tensor_tensor(sumsq[:], sumsq[:], T[0][:], ALU.add).then_inc(sumsq_added, 1)

                if st == len(stages) - 1:
                    down(0)
                    down(1, last=True)
                else:
                    with dve.Fori(0, KD // 4) as it:
                        down(it)
                norm(n_post, 0.5, Rb)

            def rope_products(u_count, bank, cos, sin):
                dve.wait_ge(unit_done, u_count)
                v.tensor_tensor(T[1][:], bank, sin[:], ALU.mult)
                v.tensor_tensor(T[0][:], bank, cos[:], ALU.mult).then_inc(evacuated, 1)

            def part(n, dst):
                dve.wait_ge(part_hi, n + 1)
                v.tensor_tensor(dst[:, 1], T[3][:], f32(dst[:, 0]), ALU.subtract).then_inc(part_lo, 1)

            steps = [0]

            def step(ins):
                steps[0] += 1
                ins.then_inc(softmax_step, 1)
                dve.wait_ge(softmax_step, steps[0])

            def softmax_max(h, scale):
                dve.wait_ge(score_psum, 3 * (h + 1))
                if h % HEADS == 0:
                    dve.wait_ge(mask_ready, 2 * (h // HEADS + 1))
                for c in range(TS):
                    bank, o = BANK[c]
                    diag = sco[bank][:, o + c * P:o + (c + 1) * P]
                    ins = v.tensor_tensor(diag, diag, mask[:], ALU.add)
                step(ins)
                for c in range(TS):
                    bank, o = BANK[c]
                    ins = v.tensor_reduce(mx[:, c:c + 1], sco[bank][:, o:o + (c + 1) * P], AX_X, ALU.max)
                step(ins)
                v.tensor_scalar(nmx[:], mx[:], -scale, None, ALU.mult).then_inc(nmx_ready, 1)

            def softmax_norm(h):
                dve.wait_ge(exp_ready, TS * (h + 1))
                step(v.reciprocal(rsums[:], psums[:]))
                for c in range(TS):
                    pc = prob[:, POFF[c]:POFF[c + 1]]
                    v.tensor_scalar(pc, pc, rsums[:, c:c + 1], None, ALU.mult).then_inc(prob_ready, 1)

            def probT_split(h):
                for b, (lo, hi) in enumerate(TBANK):
                    dve.wait_ge(probT_hi, 3 * h + b + 1)
                    v.tensor_tensor(probT[:, 1, lo:hi], sco[b][:, 0:hi - lo], f32(probT[:, 0, lo:hi]),
                                    ALU.subtract).then_inc(probT_lo, 1)

            def o_split(h):
                dve.wait_ge(o_hi, h + 1)
                v.tensor_tensor(oT[:, 1, h % HEADS], aux[:], f32(oT[:, 0, h % HEADS]),
                                ALU.subtract).then_inc(o_lo, 1)

            def v_split(h):
                dve.wait_ge(v_hi, h + 1)
                v.tensor_tensor(vh[:, 1], sco[2][:].rearrange("p (t d) -> p t d", d=P), f32(vh[:, 0]),
                                ALU.subtract).then_inc(v_lo, 1)

            def out_proj(st, u, r, n):
                clear_sumsq(n)
                for m in range(KD):
                    split(u + m + 2)
                    dve.wait_ge(unit_done, u + m + 1)
                    v.tensor_copy(y[:, m], acc[(r - R0[st] + m) % 4][:]).then_inc(evacuated, 1)
                    add_square(n, m, m % 2)
                norm(n, 1.0, Rb)

            split(0)
            split(1)
            dve.wait_ge(gains_psum, 1)
            v.tensor_copy(gains[:, 0:NG], aux[:, 0:NG]).then_inc(gains_ready, 1)
            for m in range(KD + 1):
                if m < KD:
                    dve.wait_ge(x_psum, m + 1)
                    v.tensor_copy(xT[:, m], (sco + acc)[m % 7][:]).then_inc(x_ready, 1)
                if m:
                    dve.wait_ge(x_ready, m)
                    if m == 1:
                        dve.wait_ge(gains_ready, 1)
                    gated_split(X_LOAD, 0, m - 1, gain(0, 0, 0), xg)
            x_squares(0)
            ffn(0, 0, 1)
            x_update(X_F0, 1, gain(0, 1, 0), [(gain(0, 2, 0), xg)])
            x_squares(2)

            u, r = U0[1], R0[1]
            split(u + 2)
            norm(2, 1.0, Rb)
            dve.wait_ge(r_ready, 3)
            dve.wait_ge(table_in, 32)
            v.tensor_tensor(cosR[:], cosT[:], Rb[:], ALU.mult).then_inc(table_ready, 1)
            v.tensor_tensor(sinR[:], sinT[:], Rb[:], ALU.mult).then_inc(table_ready, 1)
            dve.wait_ge(table_ready, 2)

            def bank_of(rr):
                return acc[rr % 4][:]

            def evac_v(u_count, bank, R):
                dve.wait_ge(unit_done, u_count)
                v.tensor_tensor(T[0][:], bank, R[:], ALU.mult).then_inc(evacuated, 1)

            rope_products(u + 1, bank_of(0), cosR, sinR)
            part(0, qh)
            split(u + 3)
            rope_products(u + 2, bank_of(1), cosR, sinR)
            part(1, kh)
            split(u + 4)
            evac_v(u + 3, bank_of(2), Rb)
            v_split(0)
            for h in range(HEADS):
                nxt = h + 1 < HEADS
                r1 = 3 * h + 3
                softmax_max(h, A_SCALE)
                if nxt:
                    split(u + 3 * h + 5)
                softmax_norm(h)
                if nxt:
                    rope_products(u + r1 + 1, bank_of(r1), cosR, sinR)
                    part(2 * h + 2, qh)
                    split(u + 3 * h + 6)
                    rope_products(u + r1 + 2, bank_of(r1 + 1), cosR, sinR)
                    part(2 * h + 3, kh)
                probT_split(h)
                if nxt:
                    split(u + 3 * h + 7)
                    evac_v(u + r1 + 3, bank_of(r1 + 2), Rb)
                o_split(h)
                if nxt:
                    v_split(h + 1)
            out_proj(1, u + 3 * HEADS, r + 3 * HEADS, 3)
            x_update(X_MOBA, 3, gain(0, 3, 0), [(gain(0, 4, 0), xg)])
            x_squares(4)
            ffn(2, 4, 5)

            x_update(X_F1, 5, gain(0, 5, 0), [(G_KVIN, xkv), (gain(1, 0, 0), xg)])
            x_squares(6)
            u, r = U0[3], R0[3]
            for m in range(KK):
                split(u + m + 2)
            norm(6, 1.0, Rb)
            dve.wait_ge(r_ready, 7)
            for m in range(KK):
                dve.wait_ge(unit_done, u + m + 1)
                v.tensor_tensor(ck[:, m], acc[m][:], Rb[:], ALU.mult).then_inc(evacuated, 1)
            split(u + KK + 2)
            split(u + KK + 3)
            dve.wait_ge(table_in, 64)
            v.tensor_tensor(sinT[:], sinT[:], Rb[:], ALU.mult).then_inc(table_ready, 1)
            v.tensor_tensor(cosT[:], cosT[:], Rb[:], ALU.mult).then_inc(table_ready, 1)
            dve.wait_ge(table_ready, 4)
            rope_products(u + KK + 2, acc[KK][:], cosT, sinT)
            dve.wait_ge(roped, 2 * HEADS + 1)
            ffn(4, None, 7)
            x_update(X_F2, 7, gain(1, 1, 0), [(gain(1, 2, 0), xg)])
            x_squares(8)

            u, r = U0[5], R0[5]
            for m in range(2):
                split(u + m + 2)
            norm(8, 1.0, Rb)
            dve.wait_ge(r_ready, 9)
            clear_sumsq(9)
            for i in range(KK):
                add_square(9, i, i % 2)
            for i in range(KK):
                dve.wait_ge(cq_hi, i + 1)
                v.scalar_tensor_tensor(out=ckT[:, 1, i], in0=ck[:, i], scalar=gains[:, G_KV + i:G_KV + i + 1],
                                       in1=f32(ckT[:, 0, i]), op0=ALU.mult, op1=ALU.subtract).then_inc(cq_lo, 1)
            dve.wait_ge(cq_hi, KK + 1)
            v.tensor_tensor(krT[:, 1], ck[:, KK], f32(krT[:, 0]), ALU.subtract).then_inc(cq_lo, 1)
            for m in range(2, KQ):
                split(u + m + 2)
            for m in range(KQ):
                dve.wait_ge(unit_done, u + m + 1)
                v.tensor_tensor(cq[:, m], acc[m][:], Rb[:], ALU.mult).then_inc(evacuated, 1)
            norm(9, 1.0, Rkv)
            clear_sumsq(10)
            for m in range(KQ):
                add_square(10, m, m % 2)
            dve.wait_ge(evacuated, r + KQ)
            for m in range(KQ):
                dve.wait_ge(cq_hi, KK + 1 + m + 1)
                v.scalar_tensor_tensor(out=xg[:, 1, m], in0=cq[:, m], scalar=gains[:, G_Q + m:G_Q + m + 1],
                                       in1=f32(xg[:, 0, m]), op0=ALU.mult, op1=ALU.subtract).then_inc(cq_lo, 1)
            norm(10, 1.0, Rq)
            dve.wait_ge(r_ready, 11)
            dve.wait_ge(table_in, 96)
            v.tensor_tensor(cosR[:], cosT[:], Rq[:], ALU.mult).then_inc(table_ready, 1)
            v.tensor_tensor(sinR[:], sinT[:], Rq[:], ALU.mult).then_inc(table_ready, 1)
            dve.wait_ge(table_ready, 6)
            PB = 2 * HEADS

            def evac_part(rr, u_count, R, pn, dst):
                dve.wait_ge(unit_done, u_count)
                dve.wait_ge(part_lo, pn)
                v.tensor_tensor(T[3][:], bank_of(rr), R[:], ALU.mult).then_inc(evacuated, 1)
                dve.wait_ge(evacuated, r + rr + 1)
                part(pn, dst)

            pn = PB
            split(u + KQ + 2)
            rope_products(u + KQ + 1, bank_of(KQ), cosR, sinR)
            part(pn, qrT)
            split(u + KQ + 3)
            evac_part(KQ + 1, u + KQ + 2, Rq, pn + 1, qh)
            evac_part(KQ + 2, u + KQ + 2, Rkv, pn + 2, kh)
            evac_v(u + KQ + 2, bank_of(KQ + 3), Rkv)
            v_split(HEADS)
            pn += 3
            for h in range(HEADS):
                nxt = h + 1 < HEADS
                gg = (h + 1) // 2
                nu = u + KQ + 3 * gg + 1 + (h + 1) % 2
                r1 = KQ + 7 * gg + 1 + 3 * ((h + 1) % 2)
                softmax_max(HEADS + h, B_SCALE)
                if nxt and h % 2:
                    split(nu + 1)
                softmax_norm(HEADS + h)
                if nxt:
                    if h % 2:
                        rope_products(nu, bank_of(r1 - 1), cosR, sinR)
                        part(pn, qrT)
                        pn += 1
                    split(nu + 2)
                    evac_part(r1, nu + 1, Rq, pn, qh)
                    evac_part(r1 + 1, nu + 1, Rkv, pn + 1, kh)
                    pn += 2
                probT_split(HEADS + h)
                if nxt:
                    evac_v(nu + 1, bank_of(r1 + 2), Rkv)
                o_split(HEADS + h)
                if nxt:
                    v_split(HEADS + h + 1)
            out_proj(5, u + KQ + 12, r + KQ + 28, 11)
            x_update(X_MLA, 11, gain(1, 3, 0), [(gain(1, 4, 0), xg)])
            x_squares(12)
            ffn(6, 12, 13)
            x_update(X_F3, 13, gain(1, 5, 0), [])
            for m in range(KD):
                dve.wait_ge(x_psum, KD + m + 1)
                v.tensor_copy(xout[:, m].rearrange("p c f -> p (c f)"), (sco + acc)[m % 7][:]
                              ).then_inc(out_copied, 1)

        @block.tensor
        def _(pe):
            t = nc.tensor

            def product(dst, w_h, w_l, m_h, m_l, start, stop, **kw):
                t.matmul(dst, w_h, m_h, start=start, stop=False, **kw)
                t.matmul(dst, w_h, m_l, start=False, stop=False, **kw)
                return t.matmul(dst, w_l, m_h, start=False, stop=stop, **kw)

            def tiles(dst, slot, first, n, moving, start=True, stop=True, wait=None):
                for k in range(n):
                    if wait is not None:
                        wait(k)
                    m_h, m_l = moving(k)
                    ins = product(dst, wh[:, slot, first + k], wl[:, slot, first + k], m_h, m_l,
                                  start and k == 0, stop and k == n - 1)
                return ins

            def from_x(buf):
                return lambda k: (buf[:, 0, k], buf[:, 1, k])

            def norm_mean(n, width):
                pe.wait_ge(sumsq_added, A0[n + 1])
                if n:
                    pe.wait_ge(r_ready, n)
                for c in range(TS):
                    ins = t.matmul(aux[:, c:c + 1], sumsq[:, c * P:(c + 1) * P], mean_w[width][:],
                                   start=True, stop=True)
                ins.then_inc(var_psum, 1)

            def norm_spread(n):
                pe.wait_ge(diag_ready, n + 1)
                t.matmul(aux[:], ones[:], T[3][:], start=True, stop=True).then_inc(r_psum, 1)

            def pair(u, xg0, buf, bank=(0, 1)):
                pe.wait_ge(w_lo, u + 2)
                for k in range(UT):
                    pe.wait_ge(xg_ready, xg0 + k + 1)
                    for a in range(2):
                        ins = product(acc[a][:], wh[:, a, k], wl[:, a, k], buf[:, 0, k], buf[:, 1, k],
                                      k == 0, k == UT - 1)
                        if k == UT - 1:
                            ins.then_inc(unit_done, 1)

            def ffn(st, xg0, n_pre, n_post):
                F0 = KF * FFN_STAGE[st]
                u, r = U0[st], R0[st]
                if r:
                    pe.wait_ge(evacuated, r)
                pair(u, xg0, xg)
                if n_pre is not None:
                    norm_mean(n_pre, D)
                for a in (2, 3):
                    pe.wait_ge(w_lo, u + a + 1)
                    tiles(acc[a][:], a, 0, UT, from_x(xg)).then_inc(unit_done, 1)
                    if a == 2 and n_pre is not None:
                        norm_spread(n_pre)
                with pe.Fori(1, KF // 2) as it:
                    for a in range(4):
                        pe.wait_ge(w_lo, u + 4 * it + a + 1)
                        pe.wait_ge(evacuated, r + 4 * it + a - 3)
                        tiles(acc[a][:], a, 0, UT, from_x(xg)).then_inc(unit_done, 1)
                with pe.Fori(0, KD // 4) as it:
                    for m in range(4):
                        for s in range(ND):
                            w = ND * m + s
                            pe.wait_ge(w_lo, u + 2 * KF + 4 * ND * it + w + 1)
                            if s == 0:
                                pe.wait_ge(evacuated, r + 2 * KF + 4 * it + m - 3)
                            if m == 0 and s < ND - 1:
                                pe.wait_ge(hid_lo, F0 + UT * (s + 1))

                            def late(k, m=m, s=s):
                                if m == 0 and s == ND - 1:
                                    pe.wait_ge(hid_lo, F0 + UT * s + k + 1)
                            tiles(acc[m][:], w % SLOTS, 0, DOWN[s],
                                  lambda k, s=s: (hT[:, 0, UT * s + k], hT[:, 1, UT * s + k]),
                                  start=s == 0, stop=s == ND - 1, wait=late).then_inc(unit_done, 1)
                norm_mean(n_post, D)
                norm_spread(n_post)

            def bank_for(st, rr):
                pe.wait_ge(evacuated, R0[st] + max(rr - 3, 0))
                return acc[rr % 4][:]

            def scores(h, rope_rows=None):
                pe.wait_ge(part_lo, PARTS[h])
                for c in range(TS):
                    bank, o = BANK[c]
                    if c == TS - 1:
                        pe.wait_ge(v_lo, h + 1)
                    dst = sco[bank][:, o:o + (c + 1) * P]
                    ins = product(dst, qh[:, 0, c * P:(c + 1) * P], qh[:, 1, c * P:(c + 1) * P],
                                  kh[:, 0, 0:(c + 1) * P], kh[:, 1, 0:(c + 1) * P], True, rope_rows is None)
                    if rope_rows is not None:
                        rr = slice(rope_rows, rope_rows + ROPE)
                        ins = product(dst, qrT[rr, 0, c * P:(c + 1) * P], qrT[rr, 1, c * P:(c + 1) * P],
                                      krT[rr, 0, 0:(c + 1) * P], krT[rr, 1, 0:(c + 1) * P], False, True)
                    if c:
                        ins.then_inc(score_psum, 1)

            def prob_transposes(h):
                for b, js in enumerate(((0,), (1,), (2, 3))):
                    if b == 0:
                        pe.wait_ge(prob_ready, TS * (h + 1))
                    for j in js:
                        for c in range(j, TS):
                            o = TOFF[j] - TBANK[b][0] + (c - j) * P
                            ins = t.transpose(sco[b][:, o:o + P], prob[:, POFF[c] + j * P:POFF[c] + (j + 1) * P],
                                              ident[:])
                    ins.then_inc(probT_psum, 1)

            def values(h):
                if h:
                    pe.wait_ge(o_lo, h)
                for j in range(TS):
                    if j < 3:
                        pe.wait_ge(probT_lo, 3 * h + j + 1)
                    ins = product(aux[:, j * P:S], vh[:, 0, j], vh[:, 1, j], probT[:, 0, TOFF[j]:TOFF[j + 1]],
                                  probT[:, 1, TOFF[j]:TOFF[j + 1]], j == 0, j == TS - 1)
                ins.then_inc(pv_psum, 1)

            def value_transposes(h, r_count):
                pe.wait_ge(evacuated, r_count)
                if h:
                    pe.wait_ge(probT_lo, 3 * h)
                for j in range(TS):
                    ins = t.transpose(sco[2][:, j * P:(j + 1) * P], T[0][:, j * P:(j + 1) * P], ident[:])
                ins.then_inc(vT_psum, 1)

            def out_proj(st, u, rr):
                for m in range(KD):
                    pe.wait_ge(w_lo, u + m + 1)
                    if m == 0:
                        pe.wait_ge(o_lo, HEADS * (1 if st == 1 else 2))
                    tiles(bank_for(st, rr + m), (u + m) % SLOTS, 0, UT, from_x(oT)).then_inc(unit_done, 1)

            PARTS = [2 * (h + 1) for h in range(HEADS)]
            PARTS += [2 * HEADS + 2 * (h + 1) + h // 2 + 1 for h in range(HEADS)]

            pe.wait_ge(const_ready, 3)
            pe.wait_ge(gains_in, 64)
            t.transpose(aux[:, 0:NG], gin[0:NG, :], ident[0:NG, 0:NG]).then_inc(gains_psum, 1)
            for k in range(KD):
                pe.wait_ge(x_in[k], 16)
                if k == 7:
                    pe.wait_ge(x_ready, 1)
                for c in range(TS):
                    ins = t.transpose((sco + acc)[k % 7][:, c * P:(c + 1) * P], xin[:, c, k * P:(k + 1) * P],
                                      ident[:])
                ins.then_inc(x_psum, 1)
            pe.wait_ge(x_ready, KD)
            ffn(0, XG0[X_LOAD], 0, 1)

            u, r = U0[1], R0[1]
            pe.wait_ge(evacuated, r)
            pair(u, XG0[X_F0], xg)
            norm_mean(2, D)
            pe.wait_ge(w_lo, u + 3)
            tiles(acc[2][:], 2, 0, UT, from_x(xg)).then_inc(unit_done, 1)
            norm_spread(2)
            value_transposes(0, r + 3)

            def qkv_unit(n):
                pe.wait_ge(w_lo, u + n + 1)
                tiles(bank_for(1, n), (u + n) % SLOTS, 0, UT, from_x(xg)).then_inc(unit_done, 1)

            for h in range(HEADS):
                nxt = h + 1 < HEADS
                scores(h)
                if nxt:
                    qkv_unit(3 * h + 3)
                    qkv_unit(3 * h + 4)
                prob_transposes(h)
                if nxt:
                    qkv_unit(3 * h + 5)
                if h == 0:
                    pe.wait_ge(r_ready, 3)
                values(h)
                if nxt:
                    value_transposes(h + 1, r + 3 * h + 6)
            out_proj(1, u + 3 * HEADS, 3 * HEADS)
            norm_mean(3, D)
            norm_spread(3)
            ffn(2, XG0[X_MOBA], 4, 5)

            u, r = U0[3], R0[3]
            pe.wait_ge(evacuated, r)
            pair(u, XG0[X_F1], xkv)
            norm_mean(6, D)
            pe.wait_ge(w_lo, u + 3)
            tiles(acc[2][:], 2, 0, UT // 2, from_x(xkv), stop=False).then_inc(unit_done, 1)
            norm_spread(6)
            pe.wait_ge(w_lo, u + 4)
            tiles(acc[2][:], 3, 0, UT // 2, lambda k: (xkv[:, 0, UT // 2 + k], xkv[:, 1, UT // 2 + k]),
                  start=False).then_inc(unit_done, 1)
            ffn(4, XG0[X_F1] + KD, None, 7)

            u, r = U0[5], R0[5]
            pe.wait_ge(evacuated, r)
            pair(u, XG0[X_F2], xg)
            norm_mean(8, D)
            pe.wait_ge(w_lo, u + 3)
            tiles(acc[2][:], 2, 0, UT, from_x(xg)).then_inc(unit_done, 1)
            norm_spread(8)
            pe.wait_ge(w_lo, u + 4)
            tiles(acc[3][:], 3, 0, UT, from_x(xg)).then_inc(unit_done, 1)
            norm_mean(9, KVR)
            norm_spread(9)

            def rope_unit(gg):
                n = KQ + 3 * gg
                pe.wait_ge(w_lo, u + n + 1)
                tiles(bank_for(5, KQ + 7 * gg), (u + n) % SLOTS, 0, KQ, from_x(xg),
                      wait=(lambda k: pe.wait_ge(cq_lo, KK + 1 + k + 1)) if gg == 0 else None
                      ).then_inc(unit_done, 1)

            def head_qk(h):
                gg = h // 2
                n, rr = KQ + 3 * gg + 1 + h % 2, KQ + 7 * gg + 1 + 3 * (h % 2)
                pe.wait_ge(w_lo, u + n + 1)
                tiles(bank_for(5, rr), (u + n) % SLOTS, 0, KQ, from_x(xg))
                tiles(bank_for(5, rr + 1), (u + n) % SLOTS, KQ, KK, from_x(ckT))

            def head_v(h):
                gg = h // 2
                n, rr = KQ + 3 * gg + 1 + h % 2, KQ + 7 * gg + 1 + 3 * (h % 2)
                tiles(bank_for(5, rr + 2), (u + n) % SLOTS, KQ + KK, KK, from_x(ckT)).then_inc(unit_done, 1)

            rope_unit(0)
            norm_mean(10, QR)
            norm_spread(10)
            head_qk(0)
            head_v(0)
            value_transposes(HEADS, r + KQ + 4)
            for h in range(HEADS):
                nxt = h + 1 < HEADS
                scores(HEADS + h, ROPE * (h % 2))
                if nxt:
                    if h % 2:
                        rope_unit((h + 1) // 2)
                    head_qk(h + 1)
                    head_v(h + 1)
                prob_transposes(HEADS + h)
                if h == 0:
                    pe.wait_ge(r_ready, 11)
                values(HEADS + h)
                if nxt:
                    value_transposes(HEADS + h + 1,
                                     r + KQ + 7 * ((h + 1) // 2) + 4 + 3 * ((h + 1) % 2))
            out_proj(5, u + KQ + 12, KQ + 28)
            norm_mean(11, D)
            norm_spread(11)
            ffn(6, XG0[X_MLA], 12, 13)
            for k in range(KD):
                pe.wait_ge(x_ready, KD * X_F3 + k + 1)
                if k == 0:
                    pe.wait_ge(evacuated, R0[6] + results[6])
                if k == 7:
                    pe.wait_ge(out_copied, 1)
                for c in range(TS):
                    ins = t.transpose((sco + acc)[k % 7][:, c * P:(c + 1) * P], xT[:, k, c * P:(c + 1) * P],
                                      ident[:])
                ins.then_inc(x_psum, 1)


_INS = ["x", "norm_gains", "ffn_w1", "ffn_w3", "ffn_w2", "moba_w_qkv", "moba_w_o", "mla_w_dq", "mla_q_norm",
        "mla_w_uq", "mla_w_o", "kv_in_norm", "w_dkv_kr", "kv_norm", "w_ukv"]


def _rope_table(seq, dim, copies):
    import numpy as np

    inv = (np.float32(1.0) / np.float32(10000.0) ** (np.arange(0, dim, 2, dtype=np.float32) / np.float32(dim)))
    ang = np.arange(seq, dtype=np.float32)[:, None] * inv.astype(np.float32)[None, :]
    cos, sin = np.cos(ang).T, np.sin(ang).T
    return np.ascontiguousarray(np.stack([np.concatenate([cos, cos] * copies), np.concatenate([sin, -sin] * copies)])
                                ).astype(np.float32)


def kernel(**inputs):
    import numpy as _np
    import concourse.bacc as _bacc
    from concourse import mybir as _mybir
    from concourse.bass_utils import run_bass_kernel_spmd as _run

    nc = _bacc.Bacc("TRN2", target_bir_lowering=False, num_devices=1)
    arrays, args = {}, []
    for name in _INS:
        arrays[f"in_{name}_dram"] = _np.ascontiguousarray(inputs[name])
    seq = inputs["x"].shape[1]
    arrays["in_rope_a_dram"] = _rope_table(seq, 128, 1)
    arrays["in_rope_r_dram"] = _rope_table(seq, 64, 2)
    for name, a in arrays.items():
        args.append(nc.dram_tensor(name, a.shape, _mybir.dt.from_np(a.dtype), kind="ExternalInput").ap())
    shape = inputs["x"].shape
    args.append(nc.dram_tensor("out_0_dram", shape, _mybir.dt.float32, kind="ExternalOutput").ap())
    yoco_kernel(nc, *args)
    r = _run(nc, [arrays], core_ids=[0])
    return r.results[0]["out_0_dram"]
```

```python
from contextlib import ExitStack

import concourse.bass as bass
from concourse import mybir

ALU = mybir.AluOpType
ACT = mybir.ActivationFunctionType
F32 = mybir.dt.float32
F32R = mybir.dt.float32r
AX_X = mybir.AxisListType.X

P = 128
SLOTS = 4
UT = 8
NEG = -3.0e38


def yoco_kernel(nc: bass.Bass, x, norm_gains, ffn_w1, ffn_w3, ffn_w2, moba_w_qkv, moba_w_o, mla_w_dq,
                mla_q_norm, mla_w_uq, mla_w_o, kv_in_norm, w_dkv_kr, kv_norm, w_ukv,
                rope_a, rope_r, out):
    _, S, D = x.shape
    L, _, _, FF = ffn_w1.shape
    KD = D // P
    KF = FF // P
    TS = S // P
    HEADS = moba_w_o.shape[1] // P
    QR = mla_w_dq.shape[2]
    KQ = QR // P
    KVR = kv_norm.shape[0]
    KK = KVR // P
    ROPE = w_dkv_kr.shape[1] - KVR
    HQ = P + ROPE
    A_SCALE = float(P) ** -0.5
    B_SCALE = float(HQ) ** -0.5
    EPS = 1e-6
    DOWN = [min(UT, KF - s) for s in range(0, KF, UT)]
    ND = len(DOWN)
    assert KD == UT and KF == 22 and ND == 3 and TS == 4 and HEADS == 8 and ROPE == 64 and KQ == 4 and KK == 2

    FFN_U = [(UT, 1)] * (2 * KF) + [(n, 1) for n in DOWN] * KD
    MOBA_U = [(UT, 1)] * (3 * HEADS + KD)
    KV_U = [(UT, 1)] * KK + [(UT // 2, 2)] * 2
    MLA_U = [(UT, 1)] * KQ + [(KQ, 2), (UT, 3), (UT, 3)] * (HEADS // 2) + [(UT, 1)] * KD
    stages = [FFN_U, MOBA_U, FFN_U, KV_U, FFN_U, MLA_U, FFN_U]
    FFN_R, WO_R = 2 * KF + KD + 1, KD + 2
    results = [FFN_R, 3 * HEADS + WO_R, FFN_R, KK + 1, FFN_R, KQ + 7 * (HEADS // 2) + WO_R, FFN_R]
    units = [u for s in stages for u in s]
    NU = len(units)
    U0 = [sum(len(s) for s in stages[:i]) for i in range(len(stages))]
    R0 = [sum(results[:i]) for i in range(len(stages))]
    assert all(u % SLOTS == 0 for u in U0)
    landed = []
    for u, (_, dmas) in enumerate(units):
        landed.append((landed[u - SLOTS] if u >= SLOTS else 0) + 16 * dmas)
    FFN_STAGE = {0: 0, 2: 1, 4: 2, 6: 3}

    (N_PRE0, N_F0, N_PRE1, N_MOBA, N_PRE2, N_F1, N_PRE3, N_CKV, N_F2, N_PRE4, N_CQ, N_MLA, N_PRE5, N_F3) = range(14)
    POST_FFN, POST_WO = (N_F0, N_F1, N_F2, N_F3), (N_MOBA, N_MLA)
    NORM_TILES = [KD] * 14
    NORM_TILES[N_CKV], NORM_TILES[N_CQ] = KK, KQ
    for n in POST_FFN + POST_WO:
        NORM_TILES[n] = KD - (1 if n in POST_FFN else 2)
    A0 = [sum(n - 1 for n in NORM_TILES[:i]) for i in range(len(NORM_TILES) + 1)]
    EV0 = [sum(2 if i in POST_FFN + POST_WO else 1 for i in range(n)) for n in range(len(NORM_TILES) + 1)]
    SPREAD0 = [EV0[n] - (n > N_CQ) for n in range(14)]
    LAST = [1 if n in POST_FFN else 2 if n in POST_WO else 0 for n in range(14)]
    SQ_LAST0 = [2 * sum(LAST[:n]) for n in range(14)]
    HALF0 = [sum(LAST[:n]) for n in range(14)]
    HALF = S // 2
    HT = TS // 2

    def half(e):
        return slice(e * HALF, (e + 1) * HALF)
    X_LOAD, X_F0, X_MOBA, X_F1, X_F2, X_MLA, X_F3 = range(7)
    X0 = [0] + [KD + 2 * KD * i for i in range(6)]
    XG0 = [0] + [KD + 2 * KD * i + (KD if i > 2 else 0) for i in range(6)]

    def gain(layer, s, k):
        return (layer * 6 + s) * KD + k
    G_KVIN = L * 6 * KD
    G_Q = G_KVIN + KD
    G_KV = G_Q + KQ
    NG = G_KV + KK

    with ExitStack() as ctx:
        base = [(nc.sbuf_base + 63) // 64 * 64]

        def at(name, shape, dt, offset):
            return nc.alloc_sbuf_tensor_at(name, shape, dt, offset=offset)

        def size(shape):
            n = 4
            for d in shape[1:]:
                n *= d
            return n

        def sb(name, shape, dt=F32):
            o = base[0]
            base[0] += (size(shape) + 31) // 32 * 32
            return at(name, shape, dt, o)

        xT = sb("xT", [P, KD, S])
        xg_base = base[0]
        xg = sb("xg", [P, 2, KD, S], F32R)
        y = at("y", [P, KD, S], F32, xg_base + 4 * KD * S)
        raw = sb("raw", [P, SLOTS, UT, P])
        wh = sb("wh", [P, SLOTS, UT, P], F32R)
        wl = sb("wl", [P, SLOTS, UT, P], F32R)
        h_base = base[0]
        hT = sb("hT", [P, 2, KF, S], F32R)
        ck = sb("ck", [P, KK + 1, S])
        Rb = sb("Rb", [P, S])
        sumsq = sb("sumsq", [P, S])
        T = [sb(f"tmp{i}", [P, S]) for i in range(4)]
        cosT = sb("cosT", [P, S])
        sinT = sb("sinT", [P, S])
        gains = sb("gains", [P, P])
        ident = sb("ident", [P, P])
        ones = sb("ones", [P, P])
        mean_w = {n: sb(f"mean_w{n}", [P, 1]) for n in (D, QR, KVR)}
        var = sb("var", [P, TS])
        neghalf = sb("neghalf", [P, TS])
        rtok = sb("rtok", [P, TS])
        mx = sb("mx", [P, 2, TS])
        nmx = sb("nmx", [P, TS])
        psums = sb("psums", [P, TS])
        rsums = sb("rsums", [P, TS])
        qscale = sb("qscale", [P, TS])
        assert base[0] <= nc.sbuf_usable_end, base[0]

        spot = [h_base]

        def over(name, shape, dt=F32):
            o = spot[0]
            spot[0] += size(shape)
            assert spot[0] <= h_base + 4 * 2 * KF * S
            return at(name, shape, dt, o)

        xin = at("xin", [P, TS, D], F32, h_base)
        gin = at("gin", [P, P], F32, h_base + 4 * TS * D)
        xout = at("xout", [P, 2, HT, D], F32, h_base)
        xkv = at("xkv", [P, 2, KD, S], F32R, h_base)
        ckv_diag = at("ckv_diag", [P, S], F32, h_base + 4 * S * (KF + KF - 4))
        cosR = over("cosR", [P, S])
        sinR = over("sinR", [P, S])
        qh = over("qh", [P, 2, S], F32R)
        kh = over("kh", [P, 2, S], F32R)
        vh_at = spot[0]
        vh = over("vh", [P, 2, 2, TS, P], F32R)
        POFF = [P * c * (c + 1) // 2 for c in range(TS + 1)]
        prob = over("prob", [P, POFF[TS]])
        TOFF = [sum((TS - i) * P for i in range(j)) for j in range(TS + 1)]
        probT = over("probT", [P, 2, TOFF[TS]], F32R)
        oT_at = spot[0]
        oT = over("oT", [P, 2, HEADS, S], F32R)
        cq = at("cq", [P, KQ, S], F32, oT_at)
        mask = over("mask", [P, P])
        krT = over("krT", [P, 2, S], F32R)
        qrT = over("qrT", [P, 2, S], F32R)
        ckT_at = spot[0]
        ckT = over("ckT", [P, 2, KK, S], F32R)
        prob_odd = [at(f"prob_odd{i}", [P, POFF[TS]], F32, o) for i, o in enumerate((ckT_at, vh_at))]

        BANK = [(0, 0), (0, P), (1, 0), (2, 0)]
        PIECES = [(TOFF[0], TOFF[1]), (TOFF[1], TOFF[2]), (TOFF[2], TOFF[4])]

        acc = [ctx.enter_context(nc.psum_tensor(f"acc{i}", [P, S], F32)) for i in range(4)]
        aux = ctx.enter_context(nc.psum_tensor("aux", [P, S], F32))
        sco = [ctx.enter_context(nc.psum_tensor(f"sco{i}", [P, S], F32)) for i in range(3)]
        norm_bank = (aux, sco[0])
        piece_bank = (acc[2], acc[3], acc[2])
        out_bank = (acc[1], acc[2], sco[1], sco[2])

        def square_buf(n, i):
            return T[0] if n in POST_FFN else T[(i - 1) % 3]

        def vT_bank(n):
            return acc[3] if n else aux

        def last_banks(n):
            return (acc[0],) if n == N_F1 else (sco[1], sco[2])

        def att_bank(rr):
            return acc[rr] if rr < 4 else acc[rr % 2]

        def sem(name):
            return ctx.enter_context(nc.semaphore(name))

        raw_full = [sem(f"raw_full{i}") for i in range(SLOTS)]
        w_hi = sem("w_hi")
        w_lo = sem("w_lo")
        unit_done = sem("unit_done")
        head_psum = sem("head_psum")
        half_psum = sem("half_psum")
        evacuated = sem("evacuated")
        const_ready = sem("const_ready")
        gains_in = sem("gains_in")
        gains_psum = sem("gains_psum")
        gains_ready = sem("gains_ready")
        x_in = [sem(f"x_in{k}") for k in range(KD)]
        x_psum = sem("x_psum")
        x_ready = sem("x_ready")
        xhi_ready = sem("xhi_ready")
        xg_ready = sem("xg_ready")
        y0_ready = sem("y0_ready")
        yr_ready = sem("yr_ready")
        sq_ready = sem("sq_ready")
        sq_last = sem("sq_last")
        sumsq_added = sem("sumsq_added")
        var_psum = sem("var_psum")
        var_ready = sem("var_ready")
        rtok_ready = sem("rtok_ready")
        diag_ready = sem("diag_ready")
        r_psum = sem("r_psum")
        r_ready = sem("r_ready")
        silu_ready = sem("silu_ready")
        hid_ready = sem("hid_ready")
        hid_hi = sem("hid_hi")
        hid_lo = sem("hid_lo")
        table_in = sem("table_in")
        mask_ready = sem("mask_ready")
        table_ready = sem("table_ready")
        swapped = sem("swapped")
        roped = sem("roped")
        part_hi = sem("part_hi")
        part_lo = sem("part_lo")
        vT_psum = sem("vT_psum")
        v_hi = sem("v_hi")
        v_lo = sem("v_lo")
        score_psum = sem("score_psum")
        softmax_step = sem("softmax_step")
        nmx_ready = sem("nmx_ready")
        exp_ready = sem("exp_ready")
        prob_ready = sem("prob_ready")
        probT_psum = sem("probT_psum")
        probT_hi = sem("probT_hi")
        probT_lo = sem("probT_lo")
        pv_psum = sem("pv_psum")
        o_hi = sem("o_hi")
        o_lo = sem("o_lo")
        cq_hi = sem("cq_hi")
        cq_lo = sem("cq_lo")
        out_copied = sem("out_copied")
        stored = sem("stored")

        block = ctx.enter_context(nc.Block())

        def f32(ap):
            return ap.bitcast(F32)

        def prob_of(n, c, j=None):
            buf = prob_odd[n // HEADS] if n % 2 else prob
            return buf[:, POFF[c]:POFF[c + 1]] if j is None else buf[:, POFF[c] + j * P:POFF[c] + (j + 1) * P]

        def values_of(n):
            if n < HEADS:
                return vh[:, n % 2, 0], vh[:, n % 2, 1]
            return tuple(xg[:, a, KQ + n % 2].rearrange("p (t d) -> p t d", d=P) for a in range(2))

        mla_rr = {("k", 0): KQ, ("v", 0): KQ + 1, ("r", 0): KQ + 2, ("q", 0): KQ + 3}
        for h in range(1, HEADS):
            for a in ("r",) * (h % 2 == 0) + ("q", "k", "v"):
                mla_rr[a, h // 2 if a == "r" else h] = KQ + len(mla_rr)

        def mla_unit(gg, h=None):
            return U0[5] + KQ + 3 * gg + (0 if h is None else 1 + h % 2)

        def head_result(a, h):
            if h == 0:
                return {"k": (head_psum, 1), "v": (head_psum, 2), "q": (unit_done, mla_unit(0, 0) + 1)}[a]
            return {"q": (head_psum, 2 * h + 1), "k": (head_psum, 2 * h + 2),
                    "v": (unit_done, mla_unit(h // 2, h) + 1)}[a]

        @block.sync
        def _(sp):
            def slot_free(u):
                if isinstance(u, int) and u < SLOTS:
                    return
                sp.wait_ge(w_lo, u - SLOTS + 1)

            def load(slot, j, src):
                n, w = src.shape[1], src.shape[2]
                sp.dma_start(raw[:, slot, j:j + n, 0:w], src).then_inc(raw_full[slot], 16)

            def kpn(w):
                return w.rearrange("(k p) n -> p k n", p=P)

            def ffn(st, layer, i):
                w1, w3 = kpn(ffn_w1[layer, i]), kpn(ffn_w3[layer, i])
                w2 = kpn(ffn_w2[layer, i])

                def up(it):
                    for j in range(2):
                        for a, w in enumerate((w1, w3)):
                            slot_free(U0[st] + 4 * it + 2 * j + a)
                            load(2 * j + a, 0, w[:, :, bass.ds((2 * it + j) * P, P)])

                up(0)
                with sp.Fori(1, KF // 2) as it:
                    up(it)
                with sp.Fori(0, KD // 4) as it:
                    for m in range(4):
                        for s in range(ND):
                            u = ND * m + s
                            slot_free(U0[st] + 2 * KF + 4 * ND * it + u)
                            load(u % SLOTS, 0, w2[:, UT * s:UT * s + DOWN[s], bass.ds((4 * it + m) * P, P)])

            def plain(u0, w, cols):
                for n, c in enumerate(cols):
                    slot_free(u0 + n)
                    load((u0 + n) % SLOTS, 0, w[:, :, c:c + P])

            for k in range(0, KD, 2):
                sp.dma_start(xin[:, :, k * P:(k + 1) * P],
                             x[0].rearrange("(c p) d -> p c d", p=P)[:, :, k * P:(k + 1) * P]
                             ).then_inc(x_in[k], 16)
            ffn(0, 0, 0)
            qkv = kpn(moba_w_qkv[0])
            plain(U0[1], qkv, [HEADS * P * a + P * h for h in range(HEADS) for a in range(3)])
            plain(U0[1] + 3 * HEADS, kpn(moba_w_o[0]), range(0, D, P))
            ffn(2, 0, 1)
            dkv = kpn(w_dkv_kr)
            plain(U0[3], dkv, range(0, KVR, P))
            for part in range(2):
                u = U0[3] + KK + part
                slot_free(u)
                for c in range(2):
                    sp.dma_start(raw[:, u % SLOTS, 0:UT // 2, c * ROPE:(c + 1) * ROPE],
                                 dkv[:, part * UT // 2:(part + 1) * UT // 2, KVR:KVR + ROPE]
                                 ).then_inc(raw_full[u % SLOTS], 16)
            ffn(4, 1, 0)
            plain(U0[5], kpn(mla_w_dq[0]), range(0, QR, P))
            uq, ukv = kpn(mla_w_uq[0]), kpn(w_ukv)
            u = U0[5] + KQ
            for g in range(HEADS // 2):
                slot_free(u)
                for c in range(2):
                    r = HQ * (2 * g + c) + P
                    sp.dma_start(raw[:, u % SLOTS, 0:KQ, c * ROPE:(c + 1) * ROPE],
                                 uq[:, :, r:r + ROPE]).then_inc(raw_full[u % SLOTS], 16)
                u += 1
                for h in (2 * g, 2 * g + 1):
                    slot_free(u)
                    load(u % SLOTS, 0, uq[:, :, HQ * h:HQ * h + P])
                    load(u % SLOTS, KQ, ukv[:, :, 2 * P * h:2 * P * h + P])
                    load(u % SLOTS, KQ + KK, ukv[:, :, 2 * P * h + P:2 * P * (h + 1)])
                    u += 1
            plain(u, kpn(mla_w_o[0]), range(0, D, P))
            ffn(6, 1, 1)
            ov = out[0].rearrange("(e c p) d -> p e c d", p=P, c=HT)
            for e in range(2):
                for q in range(KD // 2):
                    sp.wait_ge(out_copied, KD // 2 * e + q + 1)
                    sp.dma_start(ov[:, e, :, 2 * P * q:2 * P * (q + 1)], xout[:, e, :, 2 * P * q:2 * P * (q + 1)]
                                 ).then_inc(stored, 16)
            sp.wait_ge(stored, 16 * KD)

        @block.gpsimd
        def _(pool):
            g = nc.gpsimd
            g.memset(ident[:], 0.0).then_inc(const_ready, 1)
            pool.wait_ge(const_ready, 1)
            g.affine_select(out=ident[:], in_=ident[:], compare_op=ALU.not_equal, fill=1.0, base=0,
                            pattern=[[-1, P]], channel_multiplier=1).then_inc(const_ready, 1)
            g.memset(ones[:], 1.0)
            for n, t in mean_w.items():
                g.memset(t[:], 1.0 / n)
            g.memset(neghalf[:], -0.5).then_inc(const_ready, 1)

            def rsqrt(ev, cols=slice(0, TS)):
                pool.wait_ge(var_ready, ev + 1)
                g.tensor_tensor(rtok[:, cols], var[:, cols], neghalf[:, cols], ALU.pow).then_inc(rtok_ready, 1)

            def post_norm(n):
                for e in range(2):
                    rsqrt(EV0[n] + e, slice(HT * e, HT * (e + 1)))
                    pool.wait_ge(r_ready, EV0[n] + e + 1)
                    for m in range(1, KD):
                        g.tensor_tensor(y[:, m, half(e)], y[:, m, half(e)], Rb[:, half(e)], ALU.mult
                                        ).then_inc(yr_ready, 1)

            def split_two(u):
                for w in (u + 2, u + 3):
                    pool.wait_ge(w_hi, w + 1)
                    g.tensor_tensor(wl[:, w % SLOTS], raw[:, w % SLOTS], f32(wh[:, w % SLOTS]), ALU.subtract
                                    ).then_inc(w_lo, 1)

            def rope_add(count, dst):
                pool.wait_ge(swapped, count)
                g.tensor_tensor(dst, T[0][:], T[2][:], ALU.add).then_inc(roped, 1)

            def causal_mask(count, free_after):
                pool.wait_ge(unit_done, free_after)
                g.memset(mask[:], 0.0).then_inc(mask_ready, 1)
                pool.wait_ge(mask_ready, count)
                g.affine_select(out=mask[:], in_=mask[:], compare_op=ALU.is_ge, fill=NEG, base=0,
                                pattern=[[-1, P]], channel_multiplier=1).then_inc(mask_ready, 1)

            split_two(U0[0])
            rsqrt(EV0[N_PRE0])
            post_norm(N_F0)
            split_two(U0[1])
            causal_mask(1, U0[1])
            rsqrt(EV0[N_PRE1])
            for h in range(HEADS):
                rope_add(4 * h + 2, T[3][:])
                rope_add(4 * h + 4, T[3][:])
            post_norm(N_MOBA)
            split_two(U0[2])
            rsqrt(EV0[N_PRE2])
            post_norm(N_F1)
            rsqrt(EV0[N_PRE3])
            rope_add(4 * HEADS + 4, ck[:, KK])
            rsqrt(EV0[N_CKV])
            post_norm(N_F2)
            split_two(U0[5])
            causal_mask(3, U0[5])
            rsqrt(EV0[N_PRE4])
            rope_add(4 * HEADS + 8, T[3][:])
            rsqrt(EV0[N_CQ])
            for gg in range(1, HEADS // 2):
                rope_add(4 * HEADS + 4 * (gg + 2), T[3][:])
            post_norm(N_MLA)
            split_two(U0[6])
            rsqrt(EV0[N_PRE5])
            post_norm(N_F3)

        @block.scalar
        def _(act):
            s = nc.scalar
            COPY, SQUARE, EXP, SILU = ACT.Copy, ACT.Square, ACT.Exp, ACT.Silu

            def split_hi(slot, tiles, u, count):
                act.wait_ge(raw_full[slot], count)
                if not (isinstance(u, int) and u < SLOTS):
                    act.wait_ge(unit_done, u - SLOTS + 1)
                s.activation(wh[:, slot, 0:tiles], raw[:, slot, 0:tiles], COPY).then_inc(w_hi, 1)

            def split(u):
                if u < NU:
                    split_hi(u % SLOTS, units[u][0], u, landed[u])

            def square(n, i, src):
                bufs = 1 if n in POST_FFN else 3
                if i == 0 and n:
                    act.wait_ge(var_psum, EV0[n])
                if i > bufs:
                    act.wait_ge(sumsq_added, A0[n] + i - bufs)
                s.activation((square_buf(n, i) if i else sumsq)[:], src, SQUARE).then_inc(sq_ready, 1)

            def x_update(t, targets, before_second=()):
                for a, (gcol, dst) in enumerate(targets):
                    for e in range(2 if a == 0 else 1):
                        if e == 1:
                            for u in before_second:
                                split(u)
                        for m in range(KD):
                            if a == 0:
                                act.wait_ge(x_ready, X0[t] + KD * e + m + 1)
                            cols = half(e) if a == 0 else slice(0, S)
                            s.activation(dst[:, 0, m, cols], xT[:, m, cols], COPY,
                                         scale=gains[:, gcol + m:gcol + m + 1]).then_inc(xhi_ready, 1)

            def x_squares(n):
                for m in range(KD):
                    square(n, m, xT[:, m])

            def ffn(st, n_post):
                F0 = KF * FFN_STAGE[st]

                def up(it, first=0):
                    for j in range(2):
                        for a in range(2):
                            v = 2 * j + a + 2
                            if v >= first:
                                split_hi(v % SLOTS, UT, U0[st] + 4 * it + v, landed[U0[st] + v] + 16 * it)
                        act.wait_ge(evacuated, R0[st] + 4 * it + 2 * j + 1)
                        s.activation(T[1][:], T[0][:], SILU).then_inc(silu_ready, 1)
                        act.wait_ge(hid_ready, F0 + 2 * it + j + 1)
                        s.activation(hT[:, 0, bass.ds(2 * it + j, 1)].rearrange("p a s -> p (a s)"),
                                     T[3][:], COPY).then_inc(hid_hi, 1)

                up(0, first=4)
                with act.Fori(1, KF // 2) as it:
                    up(it)
                d0 = U0[st] + 2 * KF
                for m in range(KD - 1):
                    for v in range(ND * m + 2, ND * m + 2 + ND):
                        split(d0 + v)
                    act.wait_ge(evacuated, R0[st] + 2 * KF + m + 1)
                    square(n_post, m, y[:, m])
                split(d0 + ND * KD - 1)
                split(d0 + ND * KD)
                split(d0 + ND * KD + 1)

            def exchange(products, count, width):
                act.wait_ge(products, count)
                for b in range(0, P, 2 * width):
                    for i, o in ((b + width, b), (b, b + width)):
                        s.activation(T[2][o:o + width], T[1][i:i + width], COPY).then_inc(swapped, 1)

            def part(dst, src=T[3][:]):
                s.activation(dst, src, COPY).then_inc(part_hi, 1)

            def softmax_exp(n):
                act.wait_ge(nmx_ready, n + 1)
                if n > 1:
                    act.wait_ge(probT_psum, 3 * (n - 1))
                for c in range(TS):
                    bank, o = BANK[c]
                    s.activation(prob_of(n, c), sco[bank][:, o:o + (c + 1) * P], EXP,
                                 bias=nmx[:, c:c + 1], scale=A_SCALE if n < HEADS else qscale[:, c:c + 1],
                                 accum_out=psums[:, c:c + 1]).then_inc(exp_ready, 1)

            def probT_split(n, pieces):
                for b in pieces:
                    lo, hi = PIECES[b]
                    act.wait_ge(probT_psum, 3 * n + b + 1)
                    s.activation(probT[:, 0, lo:hi], piece_bank[b][:, 0:hi - lo], COPY).then_inc(probT_hi, 1)

            def o_split(n):
                act.wait_ge(pv_psum, n + 1)
                s.activation(oT[:, 0, n % HEADS], aux[:], COPY).then_inc(o_hi, 1)

            def v_split(n):
                act.wait_ge(vT_psum, n + 1)
                s.activation(values_of(n)[0], vT_bank(n)[:].rearrange("p (t d) -> p t d", d=P), COPY
                             ).then_inc(v_hi, 1)

            def out_proj(u, r, n):
                for m in range(KD - 2):
                    split(u + m + 2)
                    act.wait_ge(evacuated, r + m + 1)
                    square(n, m, y[:, m])
                split(u + KD)
                split(u + KD + 1)

            s.dma_start(gin[0:G_KVIN], norm_gains.rearrange("l s (k f) -> (l s k) f", f=P)).then_inc(gains_in, 16)
            s.dma_start(gin[G_KVIN:G_Q], kv_in_norm.rearrange("(k f) -> k f", f=P)).then_inc(gains_in, 16)
            s.dma_start(gin[G_Q:G_KV], mla_q_norm.rearrange("a (k f) -> (a k) f", f=P)).then_inc(gains_in, 16)
            s.dma_start(gin[G_KV:NG], kv_norm.rearrange("(k f) -> k f", f=P)).then_inc(gains_in, 16)
            for k in range(1, KD, 2):
                s.dma_start(xin[:, :, k * P:(k + 1) * P],
                            x[0].rearrange("(c p) d -> p c d", p=P)[:, :, k * P:(k + 1) * P]
                            ).then_inc(x_in[k], 16)
            s.dma_start(cosT[:], rope_a[0]).then_inc(table_in, 16)
            s.dma_start(sinT[:], rope_a[1]).then_inc(table_in, 16)
            split(0)
            split(1)
            act.wait_ge(gains_ready, 1)
            for m in range(KD):
                act.wait_ge(x_ready, m + 1)
                s.activation(xg[:, 0, m], xT[:, m], COPY, scale=gains[:, gain(0, 0, m):gain(0, 0, m) + 1]
                             ).then_inc(xhi_ready, 1)
            split(2)
            split(3)
            x_squares(N_PRE0)
            ffn(0, N_F0)

            u, r = U0[1], R0[1]
            x_update(X_F0, [(gain(0, 2, 0), xg)], before_second=(u + 2,))
            split(u + 3)
            x_squares(N_PRE1)
            split(u + 4)
            split(u + 5)

            def qk(h, i, between=lambda: None):
                exchange(evacuated, r + 3 * h + i + 1, P // 2)
                between()
                act.wait_ge(roped, 2 * h + i + 1)
                part((qh, kh)[i][:, 0])

            def split_next(w):
                if w < u + 3 * HEADS + 2:
                    split(w)

            qk(0, 0)
            qk(0, 1)
            v_split(0)
            for h in range(HEADS):
                nxt = h + 1 < HEADS
                split_next(u + 3 * h + 6)
                if h:
                    probT_split(h - 1, (0, 1))
                softmax_exp(h)
                if nxt:
                    qk(h + 1, 0, lambda: probT_split(h - 1, (2,) if h else ()))
                    split_next(u + 3 * h + 7)
                    qk(h + 1, 1, lambda: split_next(u + 3 * h + 8))
                else:
                    probT_split(h - 1, (2,))
                if h:
                    o_split(h - 1)
                if nxt:
                    v_split(h + 1)
            probT_split(HEADS - 1, (0, 1, 2))
            o_split(HEADS - 1)
            s.dma_start(cosT[:], rope_r[0]).then_inc(table_in, 16)
            s.dma_start(sinT[:], rope_r[1]).then_inc(table_in, 16)
            out_proj(u + 3 * HEADS, r + 3 * HEADS, N_MOBA)
            x_update(X_MOBA, [(gain(0, 4, 0), xg)], before_second=(U0[2] + 2, U0[2] + 3))
            x_squares(N_PRE2)
            ffn(2, N_F1)

            u, r = U0[3], R0[3]
            x_update(X_F1, [(G_KVIN, xkv), (gain(1, 0, 0), xg)], before_second=(u + 2, u + 3))
            split(u + 4)
            split(u + 5)
            x_squares(N_PRE3)
            split(u + 6)
            for i in range(KK):
                act.wait_ge(evacuated, r + i + 1)
                square(N_CKV, i, ck[:, i])
            exchange(table_ready, 3, ROPE // 2)
            split(u + 7)
            ffn(4, N_F2)

            u, r = U0[5], R0[5]
            x_update(X_F2, [(gain(1, 2, 0), xg)], before_second=(u + 2,))
            split(u + 3)
            x_squares(N_PRE4)
            for i in range(KK):
                s.activation(ckT[:, 0, i], ck[:, i], COPY).then_inc(cq_hi, 1)
            s.activation(krT[:, 0], ck[:, KK], COPY).then_inc(cq_hi, 1)
            split(u + 4)
            split(u + 5)
            for m in range(KQ):
                act.wait_ge(evacuated, r + m + 1)
                if m == 0:
                    act.wait_ge(unit_done, u + KQ)
                s.activation(xg[:, 0, m], cq[:, m], COPY, scale=gains[:, G_Q + m:G_Q + m + 1]
                             ).then_inc(cq_hi, 1)
            for m in range(KQ):
                square(N_CQ, m, cq[:, m])

            def rotated(gg):
                exchange(evacuated, r + mla_rr["r", gg] + 1, ROPE // 2)
                act.wait_ge(roped, 2 * HEADS + 2 + gg)
                part(qrT[:, 0])

            def direct(a, h, dst):
                act.wait_ge(*head_result(a, h))
                part(dst, att_bank(mla_rr[a, h])[:])

            direct("k", 0, kh[:, 0])
            v_split(HEADS)
            rotated(0)
            direct("q", 0, qh[:, 0])
            split(u + 6)
            split(u + 7)
            for h in range(HEADS):
                nxt = h + 1 < HEADS
                n = HEADS + h
                gg = (h + 1) // 2
                nu = u + KQ + 3 * gg + 1 + (h + 1) % 2
                if nxt and h % 2:
                    split(nu + 1)
                if h:
                    probT_split(n - 1, (0, 1))
                softmax_exp(n)
                if nxt:
                    if h % 2:
                        rotated(gg)
                    split(nu + 2)
                    direct("q", h + 1, qh[:, 0])
                if h:
                    probT_split(n - 1, (2,))
                if nxt:
                    direct("k", h + 1, kh[:, 0])
                if h:
                    o_split(n - 1)
                if nxt:
                    v_split(n + 1)
            probT_split(2 * HEADS - 1, (0, 1, 2))
            o_split(2 * HEADS - 1)
            out_proj(u + KQ + 12, r + KQ + 28, N_MLA)
            x_update(X_MLA, [(gain(1, 4, 0), xg)], before_second=(U0[6] + 2, U0[6] + 3))
            x_squares(N_PRE5)
            ffn(6, N_F3)

        @block.vector
        def _(dve):
            v = nc.vector

            def split_lo(slot, tiles, u):
                dve.wait_ge(w_hi, u + 1)
                v.tensor_tensor(wl[:, slot, 0:tiles], raw[:, slot, 0:tiles], f32(wh[:, slot, 0:tiles]),
                                ALU.subtract).then_inc(w_lo, 1)

            def split(u):
                if u < NU:
                    split_lo(u % SLOTS, units[u][0], u)

            def add_square(n, i):
                dve.wait_ge(sq_ready, sum(NORM_TILES[:n]) + i + 1)
                dve.wait_ge(sumsq_added, A0[n] + i - 1)
                v.tensor_tensor(sumsq[:], sumsq[:], square_buf(n, i)[:], ALU.add).then_inc(sumsq_added, 1)

            def norm_diag(n, e, factor, diag, cols=slice(0, TS)):
                ev = EV0[n] + e
                dve.wait_ge(var_psum, ev + 1)
                v.tensor_scalar(var[:, cols], norm_bank[e][:, cols], EPS, None, ALU.add).then_inc(var_ready, 1)
                dve.wait_ge(rtok_ready, ev + 1)
                w = cols.stop - cols.start
                v.scalar_tensor_tensor(out=diag[:, cols.start * P:cols.stop * P].rearrange("p (t q) -> p t q", q=P),
                                       in0=ident[:].unsqueeze(1).broadcast_to([P, w, P]), scalar=factor,
                                       in1=rtok[:, cols].unsqueeze(2).broadcast_to([P, w, P]),
                                       op0=ALU.mult, op1=ALU.mult).then_inc(diag_ready, 1)

            def norm_factor(n, diag=T[3]):
                norm_diag(n, 0, 1.0, diag)
                dve.wait_ge(r_psum, SPREAD0[n] + 1)
                v.tensor_copy(Rb[:], aux[:]).then_inc(r_ready, 1)
                dve.wait_ge(r_ready, EV0[n] + 1)

            def gated_split(t, nth, m, gcol, dst, cols):
                dve.wait_ge(xhi_ready, XG0[t] + nth + 1)
                v.scalar_tensor_tensor(out=dst[:, 1, m, cols], in0=xT[:, m, cols],
                                       scalar=gains[:, gcol + m:gcol + m + 1], in1=f32(dst[:, 0, m, cols]),
                                       op0=ALU.mult, op1=ALU.subtract).then_inc(xg_ready, 1)

            def last_tiles(n, e, tiles, r_count):
                for m, bank, done, count in tiles:
                    dve.wait_ge(done, count)
                    v.tensor_copy(y[:, m, half(e)], bank[:, half(e)]).then_inc(evacuated, 1)
                dve.wait_ge(evacuated, r_count)
                dve.wait_ge(sumsq_added, A0[n + 1])
                for i, (m, *_) in enumerate(tiles):
                    v.tensor_tensor(T[1 + i][:, half(e)], y[:, m, half(e)], y[:, m, half(e)], ALU.mult
                                    ).then_inc(sq_last, 1)

            def x_update(t, n, factor, g_post, targets, lasts, next_unit=None):
                last_tiles(n, 0, *lasts[0])

                def diag(e):
                    norm_diag(n, e, factor, T[3], slice(HT * e, HT * (e + 1)))

                def first(e):
                    dve.wait_ge(r_psum, SPREAD0[n] + e + 1)
                    v.tensor_tensor(T[2][:, half(e)], y[:, 0, half(e)], norm_bank[e][:, half(e)], ALU.mult
                                    ).then_inc(y0_ready, 1)
                    v.tensor_copy(Rb[:, half(e)], norm_bank[e][:, half(e)]).then_inc(r_ready, 1)

                diag(0)
                if next_unit is not None:
                    split(next_unit)
                first(0)
                for e in range(2):
                    for m in range(KD + 1):
                        if m < KD:
                            if m == 0:
                                dve.wait_ge(y0_ready, 2 * (t - 1) + e + 1)
                                src = T[2][:, half(e)]
                            else:
                                dve.wait_ge(yr_ready, 2 * (KD - 1) * (t - 1) + (KD - 1) * e + m)
                                src = y[:, m, half(e)]
                            v.scalar_tensor_tensor(out=xT[:, m, half(e)], in0=src,
                                                   scalar=gains[:, g_post + m:g_post + m + 1],
                                                   in1=xT[:, m, half(e)], op0=ALU.mult, op1=ALU.add
                                                   ).then_inc(x_ready, 1)
                        if m and targets:
                            dve.wait_ge(x_ready, X0[t] + KD * e + m)
                            gated_split(t, KD * e + m - 1, m - 1, *targets[0], half(e))
                        if e == 0 and m == 2:
                            last_tiles(n, 1, *lasts[1])
                        if e == 0 and m == 4:
                            diag(1)
                        if e == 0 and m == 6:
                            first(1)

            def x_squares(n):
                for m in range(1, KD):
                    add_square(n, m)

            def ffn(st, n_pre, n_post, middle=None):
                F0 = KF * FFN_STAGE[st]

                def up(it, first=0, pre=False):
                    for j in range(2):
                        for a in range(2):
                            w = 2 * j + a + 2
                            if w >= first:
                                split_lo(w % SLOTS, UT, U0[st] + 4 * it + w)
                        if pre and j == 0 and n_pre is not None:
                            norm_factor(n_pre)
                            dve.wait_ge(w_lo, U0[st] + 4)
                        f = F0 + 2 * it + j
                        dve.wait_ge(unit_done, U0[st] + 4 * it + 2 * j + 1)
                        v.tensor_tensor(T[0][:], acc[2 * j][:], Rb[:], ALU.mult).then_inc(evacuated, 1)
                        dve.wait_ge(unit_done, U0[st] + 4 * it + 2 * j + 2)
                        v.tensor_tensor(T[2][:], acc[2 * j + 1][:], Rb[:], ALU.mult).then_inc(evacuated, 1)
                        dve.wait_ge(evacuated, R0[st] + 4 * it + 2 * j + 2)
                        dve.wait_ge(silu_ready, f + 1)
                        v.tensor_tensor(T[3][:], T[1][:], T[2][:], ALU.mult).then_inc(hid_ready, 1)
                        dve.wait_ge(hid_ready, f + 1)
                        dve.wait_ge(hid_hi, f + 1)
                        at_ = bass.ds(2 * it + j, 1)
                        v.tensor_tensor(hT[:, 1, at_].rearrange("p a s -> p (a s)"), T[3][:],
                                        f32(hT[:, 0, at_].rearrange("p a s -> p (a s)")),
                                        ALU.subtract).then_inc(hid_lo, 1)
                        if pre and j == 0 and middle is not None:
                            middle()

                up(0, first=4, pre=True)
                with dve.Fori(1, KF // 2) as it:
                    up(it)
                d0, r0 = U0[st] + 2 * KF, R0[st] + 2 * KF
                for m in range(KD - 1):
                    for w in range(ND * m + 2, ND * m + 2 + ND):
                        split(d0 + w)
                    dve.wait_ge(unit_done, d0 + ND * (m + 1))
                    v.tensor_copy(y[:, m], acc[m % 4][:]).then_inc(evacuated, 1)
                    if m:
                        add_square(n_post, m)
                split(d0 + ND * KD - 1)
                split(d0 + ND * KD)
                return (([(KD - 1, acc[3], half_psum, HALF0[n_post] + 1)], r0 + KD),
                        ([(KD - 1, last_banks(n_post)[0], unit_done, d0 + ND * KD)], r0 + KD + 1))

            def rope_products(u_count, bank, cos, sin):
                dve.wait_ge(unit_done, u_count)
                v.tensor_tensor(T[1][:], bank, sin[:], ALU.mult)
                v.tensor_tensor(T[0][:], bank, cos[:], ALU.mult).then_inc(evacuated, 1)

            def part(n, dst):
                dve.wait_ge(part_hi, n + 1)
                v.tensor_tensor(dst[:, 1], T[3][:], f32(dst[:, 0]), ALU.subtract).then_inc(part_lo, 1)

            steps = [0]

            def step(ins):
                steps[0] += 1
                ins.then_inc(softmax_step, 1)
                dve.wait_ge(softmax_step, steps[0])

            def softmax_max(n):
                dve.wait_ge(score_psum, 3 * (n + 1))
                if n % HEADS == 0:
                    dve.wait_ge(mask_ready, 2 * (n // HEADS + 1))
                for c in range(TS):
                    bank, o = BANK[c]
                    diag = sco[bank][:, o + c * P:o + (c + 1) * P]
                    ins = v.tensor_tensor(diag, diag, mask[:], ALU.add)
                step(ins)
                for c in range(TS):
                    bank, o = BANK[c]
                    ins = v.tensor_reduce(mx[:, 0, c:c + 1], sco[bank][:, o:o + (c + 1) * P], AX_X, ALU.max)
                step(ins)
                if n < HEADS:
                    v.tensor_scalar(nmx[:], mx[:, 0], -A_SCALE, None, ALU.mult).then_inc(nmx_ready, 1)
                else:
                    v.scalar_tensor_tensor(out=nmx[:], in0=mx[:, 0], scalar=-1.0, in1=qscale[:],
                                           op0=ALU.mult, op1=ALU.mult).then_inc(nmx_ready, 1)

            def softmax_norm(n):
                dve.wait_ge(exp_ready, TS * (n + 1))
                step(v.reciprocal(rsums[:], psums[:]))
                for c in range(TS):
                    pc = prob_of(n, c)
                    v.tensor_scalar(pc, pc, rsums[:, c:c + 1], None, ALU.mult).then_inc(prob_ready, 1)

            def probT_split(n, pieces):
                for b in pieces:
                    lo, hi = PIECES[b]
                    dve.wait_ge(probT_hi, 3 * n + b + 1)
                    v.tensor_tensor(probT[:, 1, lo:hi], piece_bank[b][:, 0:hi - lo], f32(probT[:, 0, lo:hi]),
                                    ALU.subtract).then_inc(probT_lo, 1)

            def o_split(n):
                dve.wait_ge(o_hi, n + 1)
                v.tensor_tensor(oT[:, 1, n % HEADS], aux[:], f32(oT[:, 0, n % HEADS]),
                                ALU.subtract).then_inc(o_lo, 1)

            def v_split(n):
                dve.wait_ge(v_hi, n + 1)
                v_h, v_l = values_of(n)
                v.tensor_tensor(v_l, vT_bank(n)[:].rearrange("p (t d) -> p t d", d=P), f32(v_h),
                                ALU.subtract).then_inc(v_lo, 1)

            def out_proj(u, r, n):
                for m in range(KD - 2):
                    split(u + m + 2)
                    dve.wait_ge(unit_done, u + m + 1)
                    v.tensor_copy(y[:, m], acc[m % 4][:]).then_inc(evacuated, 1)
                    if m:
                        add_square(n, m)
                split(u + KD)
                split(u + KD + 1)
                return (([(KD - 2, acc[2], half_psum, HALF0[n] + 1), (KD - 1, acc[3], half_psum, HALF0[n] + 2)],
                         r + KD),
                        ([(KD - 2 + i, last_banks(n)[i], unit_done, u + KD - 1 + i) for i in range(2)],
                         r + KD + 2))

            split(0)
            split(1)
            dve.wait_ge(gains_psum, 1)
            v.tensor_copy(gains[:, 0:NG], aux[:, 0:NG]).then_inc(gains_ready, 1)
            for m in range(KD + 1):
                if m < KD:
                    dve.wait_ge(x_psum, m + 1)
                    v.tensor_copy(xT[:, m], (sco + acc)[m % 7][:]).then_inc(x_ready, 1)
                if m:
                    dve.wait_ge(x_ready, m)
                    if m == 1:
                        dve.wait_ge(gains_ready, 1)
                    gated_split(X_LOAD, m - 1, m - 1, gain(0, 0, 0), xg, slice(0, S))
            x_squares(N_PRE0)
            lasts = ffn(0, N_PRE0, N_F0)
            x_update(X_F0, N_F0, 0.5, gain(0, 1, 0), [(gain(0, 2, 0), xg)], lasts, U0[1] + 1)

            u, r = U0[1], R0[1]
            x_squares(N_PRE1)
            dve.wait_ge(w_lo, u + 4)
            split(u + 4)
            split(u + 5)
            norm_factor(N_PRE1)
            dve.wait_ge(table_in, 32)
            v.tensor_tensor(cosR[:], cosT[:], Rb[:], ALU.mult).then_inc(table_ready, 1)
            v.tensor_tensor(sinR[:], sinT[:], Rb[:], ALU.mult).then_inc(table_ready, 1)
            dve.wait_ge(table_ready, 2)

            def evac_v(u_count, bank):
                dve.wait_ge(unit_done, u_count)
                v.tensor_tensor(T[0][:], bank, Rb[:], ALU.mult).then_inc(evacuated, 1)

            def qk(h, i, between=lambda: None):
                rope_products(u + 3 * h + i + 1, att_bank(3 * h + i)[:], cosR, sinR)
                between()
                part(2 * h + i, (qh, kh)[i])

            def split_next(w):
                if w < u + 3 * HEADS + 2:
                    split(w)

            qk(0, 0)
            qk(0, 1)
            evac_v(u + 3, acc[2][:])
            v_split(0)
            for h in range(HEADS):
                nxt = h + 1 < HEADS
                softmax_max(h)
                split_next(u + 3 * h + 6)
                if h:
                    probT_split(h - 1, (0, 1))
                softmax_norm(h)
                if nxt:
                    qk(h + 1, 0, lambda: probT_split(h - 1, (2,) if h else ()))
                    split_next(u + 3 * h + 7)
                    qk(h + 1, 1, lambda: split_next(u + 3 * h + 8))
                else:
                    probT_split(h - 1, (2,))
                if h:
                    o_split(h - 1)
                if nxt:
                    evac_v(u + 3 * h + 6, att_bank(3 * h + 5)[:])
                    v_split(h + 1)
            probT_split(HEADS - 1, (0, 1, 2))
            o_split(HEADS - 1)
            lasts = out_proj(u + 3 * HEADS, r + 3 * HEADS, N_MOBA)
            x_update(X_MOBA, N_MOBA, 1.0, gain(0, 3, 0), [(gain(0, 4, 0), xg)], lasts)
            x_squares(N_PRE2)
            lasts = ffn(2, N_PRE2, N_F1)

            u, r = U0[3], R0[3]
            x_update(X_F1, N_F1, 0.5, gain(0, 5, 0), [(G_KVIN, xkv)], lasts, u + 1)
            split(u + 2)
            split(u + 3)
            for m in range(KD):
                gated_split(X_F1, 2 * KD + m, m, gain(1, 0, 0), xg, slice(0, S))
            split(u + 4)
            split(u + 5)
            x_squares(N_PRE3)
            split(u + 6)
            norm_factor(N_PRE3)
            for m in range(KK):
                dve.wait_ge(unit_done, u + m + 1)
                v.tensor_tensor(ck[:, m], sco[1 + m][:], Rb[:], ALU.mult).then_inc(evacuated, 1)
            dve.wait_ge(unit_done, u + KK + 2)
            v.tensor_tensor(T[3][:], acc[3][:], Rb[:], ALU.mult).then_inc(evacuated, 1)
            dve.wait_ge(evacuated, r + KK + 1)
            for i in range(1, KK):
                add_square(N_CKV, i)
            dve.wait_ge(sumsq_added, A0[N_CKV + 1])
            dve.wait_ge(table_in, 64)
            v.tensor_tensor(T[1][:], T[3][:], sinT[:], ALU.mult)
            v.tensor_tensor(T[0][:], T[3][:], cosT[:], ALU.mult).then_inc(table_ready, 1)
            split(u + 7)
            dve.wait_ge(roped, 2 * HEADS + 1)

            def ck_scale():
                norm_diag(N_CKV, 0, 1.0, ckv_diag)
                dve.wait_ge(r_psum, SPREAD0[N_CKV] + 1)
                for i in range(KK):
                    v.scalar_tensor_tensor(out=ck[:, i], in0=ck[:, i], scalar=gains[:, G_KV + i:G_KV + i + 1],
                                           in1=aux[:], op0=ALU.mult, op1=ALU.mult
                                           ).then_inc(r_ready if i == KK - 1 else table_ready, 1)

            lasts = ffn(4, None, N_F2, middle=ck_scale)
            x_update(X_F2, N_F2, 0.5, gain(1, 1, 0), [(gain(1, 2, 0), xg)], lasts, U0[5] + 1)

            u, r = U0[5], R0[5]
            x_squares(N_PRE4)
            dve.wait_ge(w_lo, u + 4)
            for i in range(KK):
                dve.wait_ge(cq_hi, i + 1)
                v.tensor_tensor(ckT[:, 1, i], ck[:, i], f32(ckT[:, 0, i]), ALU.subtract).then_inc(cq_lo, 1)
            dve.wait_ge(cq_hi, KK + 1)
            v.tensor_tensor(krT[:, 1], ck[:, KK], f32(krT[:, 0]), ALU.subtract).then_inc(cq_lo, 1)
            norm_factor(N_PRE4)
            split(u + 4)
            split(u + 5)
            for m in range(KQ):
                dve.wait_ge(unit_done, u + m + 1)
                v.tensor_tensor(cq[:, m], acc[m][:], Rb[:], ALU.mult).then_inc(evacuated, 1)
            dve.wait_ge(evacuated, r + KQ)
            for m in range(KQ):
                dve.wait_ge(cq_hi, KK + 1 + m + 1)
                v.scalar_tensor_tensor(out=xg[:, 1, m], in0=cq[:, m], scalar=gains[:, G_Q + m:G_Q + m + 1],
                                       in1=f32(xg[:, 0, m]), op0=ALU.mult, op1=ALU.subtract).then_inc(cq_lo, 1)
            for m in range(1, KQ):
                add_square(N_CQ, m)

            def direct(a, h, dst):
                dve.wait_ge(*head_result(a, h))
                dve.wait_ge(part_hi, parts[0] + 1)
                v.tensor_tensor(dst[:, 1], att_bank(mla_rr[a, h])[:], f32(dst[:, 0]), ALU.subtract
                                ).then_inc(evacuated, 1)
                parts[0] += 1

            def copy_v(h):
                dve.wait_ge(*head_result("v", h))
                v.tensor_copy(T[0][:], att_bank(mla_rr["v", h])[:]).then_inc(evacuated, 1)

            def rotated(gg, u_count):
                rope_products(u_count, att_bank(mla_rr["r", gg])[:], cosT, sinT)
                dve.wait_ge(part_hi, parts[0] + 1)
                v.tensor_tensor(qrT[:, 1], T[3][:], f32(qrT[:, 0]), ALU.subtract).then_inc(part_lo, 1)
                parts[0] += 1

            parts = [2 * HEADS]
            direct("k", 0, kh)
            dve.wait_ge(sumsq_added, A0[N_CQ + 1])
            copy_v(0)
            v_split(HEADS)
            rotated(0, u + KQ + 1)
            direct("q", 0, qh)
            split(u + 6)
            split(u + 7)
            dve.wait_ge(var_psum, EV0[N_CQ] + 1)
            v.tensor_scalar(var[:], norm_bank[0][:, 0:TS], EPS, None, ALU.add).then_inc(var_ready, 1)
            dve.wait_ge(rtok_ready, EV0[N_CQ] + 1)
            v.tensor_scalar(qscale[:], rtok[:], B_SCALE, None, ALU.mult).then_inc(r_ready, 1)
            dve.wait_ge(r_ready, EV0[N_CQ] + 1)
            for h in range(HEADS):
                nxt = h + 1 < HEADS
                n = HEADS + h
                gg = (h + 1) // 2
                nu = u + KQ + 3 * gg + 1 + (h + 1) % 2
                softmax_max(n)
                if nxt and h % 2:
                    split(nu + 1)
                if h:
                    probT_split(n - 1, (0, 1))
                softmax_norm(n)
                if nxt:
                    if h % 2:
                        rotated(gg, nu)
                    split(nu + 2)
                    direct("q", h + 1, qh)
                if h:
                    probT_split(n - 1, (2,))
                if nxt:
                    direct("k", h + 1, kh)
                if h:
                    o_split(n - 1)
                if nxt:
                    copy_v(h + 1)
                    v_split(n + 1)
            probT_split(2 * HEADS - 1, (0, 1, 2))
            o_split(2 * HEADS - 1)
            lasts = out_proj(u + KQ + 12, r + KQ + 28, N_MLA)
            x_update(X_MLA, N_MLA, 1.0, gain(1, 3, 0), [(gain(1, 4, 0), xg)], lasts)
            x_squares(N_PRE5)
            lasts = ffn(6, N_PRE5, N_F3)
            x_update(X_F3, N_F3, 0.5, gain(1, 5, 0), [], lasts)
            for i in range(KD):
                dve.wait_ge(x_psum, KD + i + 1)
                e, q = divmod(i, KD // 2)
                v.tensor_copy(xout[:, e, :, 2 * P * q:2 * P * (q + 1)],
                              out_bank[i % 4][:].rearrange("p (c f) -> p c f", c=HT)).then_inc(out_copied, 1)

        @block.tensor
        def _(pe):
            t = nc.tensor

            def product(dst, w_h, w_l, m_h, m_l, start, stop, **kw):
                t.matmul(dst, w_h, m_h, start=start, stop=False, **kw)
                t.matmul(dst, w_h, m_l, start=False, stop=False, **kw)
                return t.matmul(dst, w_l, m_h, start=False, stop=stop, **kw)

            def tiles(dst, slot, first, n, moving, start=True, stop=True, before=None, k0=0):
                for k in range(k0, n):
                    if before is not None:
                        before(k)
                    m_h, m_l = moving(k)
                    ins = product(dst, wh[:, slot, first + k], wl[:, slot, first + k], m_h, m_l,
                                  start and k == k0, stop and k == n - 1)
                return ins

            def from_x(buf, cols=slice(0, S)):
                return lambda k: (buf[:, 0, k, cols], buf[:, 1, k, cols])

            def mean(n, e=0, width=D, cols=range(TS), last=()):
                pe.wait_ge(sumsq_added, A0[n + 1])
                if last:
                    pe.wait_ge(sq_last, SQ_LAST0[n] + len(last) * (e + 1))
                if EV0[n]:
                    pe.wait_ge(r_ready, EV0[n])
                for c in cols:
                    parts = [sumsq, *last]
                    for i, src in enumerate(parts):
                        ins = t.matmul(norm_bank[e][:, c:c + 1], src[:, c * P:(c + 1) * P], mean_w[width][:],
                                       start=i == 0, stop=i == len(parts) - 1)
                ins.then_inc(var_psum, 1)

            def spread(n, e=0, cols=slice(0, S), diag=T[3]):
                pe.wait_ge(diag_ready, SPREAD0[n] + e + 1)
                t.matmul(norm_bank[e][:, cols], ones[:], diag[:, cols], start=True, stop=True).then_inc(r_psum, 1)

            def post_mean(n, e):
                mean(n, e, D, range(HT * e, HT * (e + 1)), T[1:1 + LAST[n]])

            def post_spread(n, e):
                spread(n, e, half(e))

            def unit(u, dst, moving, n=UT, **kw):
                pe.wait_ge(w_lo, u + 1)
                tiles(dst, u % SLOTS, 0, n, moving, **kw).then_inc(unit_done, 1)

            def pair(u, banks, buf, xg0, by_halves, after=None):
                pe.wait_ge(w_lo, u + 2)
                cols = [half(0), half(1)] if by_halves else [slice(0, S)]
                for e, cs in enumerate(cols):
                    for k in range(UT):
                        pe.wait_ge(xg_ready, xg0 + KD * e + k + 1)
                        for a in range(2):
                            ins = product(banks[a][:, cs], wh[:, (u + a) % SLOTS, k], wl[:, (u + a) % SLOTS, k],
                                          buf[:, 0, k, cs], buf[:, 1, k, cs], k == 0, k == UT - 1)
                            if k == UT - 1 and e == len(cols) - 1:
                                ins.then_inc(unit_done, 1)
                        if after is not None:
                            after(e, k)

            def second_norm(n):
                def after(e, k):
                    if e == 0 and k == 1:
                        post_mean(n, 1)
                    if e == 0 and k == 3:
                        post_spread(n, 1)
                return after

            def norm_among(n, at_mean, at_spread):
                def before(k):
                    if k == at_mean:
                        mean(n)
                    if k == at_spread:
                        spread(n)
                return before

            def norm_over_two(u, n):
                unit(u + 2, acc[2][:], from_x(xg), before=norm_among(n, 6, None))
                unit(u + 3, acc[3][:], from_x(xg), before=norm_among(n, None, 3))

            def shared_norm(k):
                if k == 3:
                    mean(N_CKV, width=KVR)
                if k == 7:
                    spread(N_CKV, diag=ckv_diag)

            def ffn(st, xg0, by_halves, after, n_pre, n_post):
                F0 = KF * FFN_STAGE[st]
                u, r = U0[st], R0[st]
                pair(u, (acc[0], acc[1]), xg, xg0, by_halves, after)
                if st == 4:
                    pe.wait_ge(evacuated, r)
                    unit(u + 2, acc[2][:], from_x(xg))
                    unit(u + 3, acc[3][:], from_x(xg), before=shared_norm)
                else:
                    norm_over_two(u, n_pre)
                with pe.Fori(1, KF // 2) as it:
                    for a in range(4):
                        pe.wait_ge(w_lo, u + 4 * it + a + 1)
                        pe.wait_ge(evacuated, r + 4 * it + a - 3)
                        tiles(acc[a][:], a, 0, UT, from_x(xg)).then_inc(unit_done, 1)
                d0, r0 = u + 2 * KF, r + 2 * KF

                def hidden(s, cols=slice(0, S)):
                    return lambda k: (hT[:, 0, UT * s + k, cols], hT[:, 1, UT * s + k, cols])

                for m in range(KD - 1):
                    pe.wait_ge(evacuated, r0 + m - 3)
                    for s in range(ND):
                        def late(k, s=s):
                            pe.wait_ge(hid_lo, F0 + UT * s + k + 1)
                        unit(d0 + ND * m + s, acc[m % 4][:], hidden(s), DOWN[s], start=s == 0, stop=s == ND - 1,
                             before=late if m == 0 else None)
                m = KD - 1
                pe.wait_ge(evacuated, r0 + m - 3)
                for s in range(ND):
                    w = d0 + ND * m + s
                    pe.wait_ge(w_lo, w + 1)
                    ins = tiles(acc[3][:, half(0)], w % SLOTS, 0, DOWN[s], hidden(s, half(0)),
                                start=s == 0, stop=s == ND - 1)
                ins.then_inc(half_psum, 1)
                if n_post == N_F1:
                    pe.wait_ge(evacuated, r0 + 5)
                for s in range(ND):
                    unit(d0 + ND * m + s, last_banks(n_post)[0][:, half(1)], hidden(s, half(1)),
                         DOWN[s],
                         start=s == 0, stop=s == ND - 1)
                    if s == 0:
                        post_mean(n_post, 0)
                    if s == 1:
                        post_spread(n_post, 0)

            def att_dst(st, rr):
                if rr >= 4:
                    pe.wait_ge(evacuated, R0[st] + (rr - 3 if rr < 6 else rr - 1))
                return att_bank(rr)[:]

            def scores(n, rope_rows=None):
                if n:
                    pe.wait_ge(exp_ready, TS * n)
                for c in range(TS):
                    bank, o = BANK[c]
                    dst = sco[bank][:, o:o + (c + 1) * P]
                    ins = product(dst, qh[:, 0, c * P:(c + 1) * P], qh[:, 1, c * P:(c + 1) * P],
                                  kh[:, 0, 0:(c + 1) * P], kh[:, 1, 0:(c + 1) * P], True, rope_rows is None)
                    if rope_rows is not None:
                        rr = slice(rope_rows, rope_rows + ROPE)
                        ins = product(dst, qrT[rr, 0, c * P:(c + 1) * P], qrT[rr, 1, c * P:(c + 1) * P],
                                      krT[rr, 0, 0:(c + 1) * P], krT[rr, 1, 0:(c + 1) * P], False, True)
                    if c:
                        ins.then_inc(score_psum, 1)

            def prob_transposes(n, pieces):
                pe.wait_ge(prob_ready, TS * (n + 1))
                for b in pieces:
                    if b == 1 and (n + 1) % HEADS:
                        pe.wait_ge(v_lo, n + 2)
                    if b == 2:
                        pe.wait_ge(probT_lo, 3 * n + 1)
                    for j in ((0,), (1,), (2, 3))[b]:
                        for c in range(j, TS):
                            o = TOFF[j] - PIECES[b][0] + (c - j) * P
                            ins = t.transpose(piece_bank[b][:, o:o + P],
                                              prob_of(n, c, j), ident[:])
                    ins.then_inc(probT_psum, 1)

            def values(n):
                if n:
                    pe.wait_ge(o_lo, n)
                pe.wait_ge(v_lo, n + 1)
                v_h, v_l = values_of(n)
                for j in range(TS):
                    if j < 3:
                        pe.wait_ge(probT_lo, 3 * n + j + 1)
                    ins = product(aux[:, j * P:S], v_h[:, j], v_l[:, j], probT[:, 0, TOFF[j]:TOFF[j + 1]],
                                  probT[:, 1, TOFF[j]:TOFF[j + 1]], j == 0, j == TS - 1)
                ins.then_inc(pv_psum, 1)

            def value_transposes(n, r_count):
                pe.wait_ge(evacuated, r_count)
                for j in range(TS):
                    ins = t.transpose(vT_bank(n)[:, j * P:(j + 1) * P], T[0][:, j * P:(j + 1) * P], ident[:])
                ins.then_inc(vT_psum, 1)

            def out_proj(st, u, r, n, heads):
                att = R0[st] + r
                last = heads + HEADS - 1
                pe.wait_ge(evacuated, att)
                for m in range(2):
                    pe.wait_ge(w_lo, u + m + 1)
                    if m == 0:
                        pe.wait_ge(o_lo, last)
                    tiles(acc[m][:], (u + m) % SLOTS, 0, UT - 1, from_x(oT), stop=False)
                    if m == 0:
                        prob_transposes(last, (0, 1, 2))
                    else:
                        values(last)
                for m in range(2, 4):
                    pe.wait_ge(w_lo, u + m + 1)
                    if m == 2:
                        pe.wait_ge(o_lo, last + 1)
                        for b in range(2):
                            tiles(acc[b][:], (u + b) % SLOTS, 0, UT, from_x(oT), start=False, k0=UT - 1
                                  ).then_inc(unit_done, 1)
                    unit(u + m, acc[m][:], from_x(oT))
                for m in range(4, KD - 2):
                    pe.wait_ge(evacuated, att + m - 3)
                    unit(u + m, acc[m % 4][:], from_x(oT))
                for m in (KD - 2, KD - 1):
                    pe.wait_ge(evacuated, att + m - 3)
                    pe.wait_ge(w_lo, u + m + 1)
                    tiles(acc[m % 4][:, half(0)], (u + m) % SLOTS, 0, UT, from_x(oT, half(0))
                          ).then_inc(half_psum, 1)
                for m in (KD - 2, KD - 1):
                    unit(u + m, last_banks(n)[m % 2][:, half(1)], from_x(oT, half(1)),
                         before=(lambda k: post_mean(n, 0) if k == 4 else None) if m == KD - 2 else None)
                    if m == KD - 2:
                        post_spread(n, 0)

            pe.wait_ge(const_ready, 3)
            for k in range(KD):
                pe.wait_ge(x_in[k], 16)
                if k == 7:
                    pe.wait_ge(x_ready, 1)
                for c in range(TS):
                    ins = t.transpose((sco + acc)[k % 7][:, c * P:(c + 1) * P], xin[:, c, k * P:(k + 1) * P],
                                      ident[:])
                ins.then_inc(x_psum, 1)
                if k == 0:
                    pe.wait_ge(gains_in, 64)
                    t.transpose(aux[:, 0:NG], gin[0:NG, :], ident[0:NG, 0:NG]).then_inc(gains_psum, 1)
            pe.wait_ge(x_ready, KD)
            ffn(0, XG0[X_LOAD], False, None, N_PRE0, N_F0)

            u, r = U0[1], R0[1]
            pair(u, (acc[0], acc[1]), xg, XG0[X_F0], True, second_norm(N_F0))
            norm_over_two(u, N_PRE1)

            def qkv_unit(rr):
                unit(u + rr, att_dst(1, rr), from_x(xg))

            qkv_unit(4)
            qkv_unit(5)
            value_transposes(0, r + 3)
            for h in range(HEADS):
                nxt = h + 1 < HEADS
                pe.wait_ge(part_lo, 2 * (h + 1))
                scores(h)
                if h:
                    prob_transposes(h - 1, (0, 1))
                if nxt and h:
                    qkv_unit(3 * h + 4)
                if h:
                    prob_transposes(h - 1, (2,))
                if nxt and h:
                    qkv_unit(3 * h + 5)
                if h:
                    values(h - 1)
                if h + 2 < HEADS:
                    qkv_unit(3 * h + 6)
                if nxt:
                    value_transposes(h + 1, r + 3 * h + 6)
            out_proj(1, u + 3 * HEADS, 3 * HEADS, N_MOBA, 0)
            ffn(2, XG0[X_MOBA], True, second_norm(N_MOBA), N_PRE2, N_F1)

            u, r = U0[3], R0[3]
            pair(u, (sco[1], sco[2]), xkv, XG0[X_F1], True, second_norm(N_F1))
            unit(u + 2, acc[3][:], from_x(xkv), UT // 2, stop=False)
            unit(u + 3, acc[3][:], lambda k: (xkv[:, 0, UT // 2 + k], xkv[:, 1, UT // 2 + k]), UT // 2, start=False)

            pre = norm_among(N_PRE3, 4, 6)
            ffn(4, XG0[X_F1] + 2 * KD, False, lambda e, k: pre(k), N_CKV, N_F2)

            u, r = U0[5], R0[5]
            pair(u, (acc[0], acc[1]), xg, XG0[X_F2], True, second_norm(N_F2))
            norm_over_two(u, N_PRE4)

            def head_part(a, h, before=None):
                first, n = {"q": (0, KQ), "k": (KQ, KK), "v": (KQ + KK, KK)}[a]
                w = mla_unit(h // 2, h)
                pe.wait_ge(w_lo, w + 1)
                return tiles(att_dst(5, mla_rr[a, h]), w % SLOTS, first, n, from_x(xg if a == "q" else ckT),
                             before=before)

            pe.wait_ge(cq_lo, KK + 1)
            head_part("k", 0).then_inc(head_psum, 1)
            head_part("v", 0).then_inc(head_psum, 1)
            unit(mla_unit(0), att_dst(5, mla_rr["r", 0]), from_x(xg), KQ,
                 before=lambda k: pe.wait_ge(cq_lo, KK + 1 + k + 1))
            value_transposes(HEADS, r + mla_rr["v", 0] + 1)
            head_part("q", 0).then_inc(unit_done, 1)
            mean(N_CQ, width=QR)
            for h in range(HEADS):
                nxt = h + 1 < HEADS
                n = HEADS + h
                gg = (h + 1) // 2
                pe.wait_ge(evacuated, r + max(mla_rr["q", h], mla_rr["k", h]) + 1)
                pe.wait_ge(part_lo, 2 * HEADS + h // 2 + 1)
                scores(n, ROPE * (h % 2))
                if h:
                    prob_transposes(n - 1, (0, 1))
                if nxt:
                    if h % 2:
                        unit(mla_unit(gg), att_dst(5, mla_rr["r", gg]), from_x(xg), KQ)
                    head_part("q", h + 1).then_inc(head_psum, 1)
                if h:
                    prob_transposes(n - 1, (2,))
                if nxt:
                    head_part("k", h + 1).then_inc(head_psum, 1)
                if h:
                    values(n - 1)
                if nxt:
                    head_part("v", h + 1).then_inc(unit_done, 1)
                    value_transposes(n + 1, r + mla_rr["v", h + 1] + 1)
            out_proj(5, u + KQ + 12, KQ + 28, N_MLA, HEADS)
            ffn(6, XG0[X_MLA], True, second_norm(N_MLA), N_PRE5, N_F3)

            post_mean(N_F3, 1)
            pe.wait_ge(evacuated, R0[6] + results[6])
            for e in range(2):
                for q in range(KD // 2):
                    i = KD // 2 * e + q
                    if i >= 4:
                        pe.wait_ge(out_copied, i - 3)
                    if i == 1:
                        post_spread(N_F3, 1)
                    for k in (2 * q, 2 * q + 1):
                        pe.wait_ge(x_ready, X0[X_F3] + KD * e + k + 1)
                        for c in range(HT):
                            o = 2 * P * c + P * (k % 2)
                            ins = t.transpose(out_bank[i % 4][:, o:o + P],
                                              xT[:, k, (HT * e + c) * P:(HT * e + c + 1) * P], ident[:])
                    ins.then_inc(x_psum, 1)


_INS = ["x", "norm_gains", "ffn_w1", "ffn_w3", "ffn_w2", "moba_w_qkv", "moba_w_o", "mla_w_dq", "mla_q_norm",
        "mla_w_uq", "mla_w_o", "kv_in_norm", "w_dkv_kr", "kv_norm", "w_ukv"]


def _rope_table(seq, dim, copies):
    import numpy as np

    inv = (np.float32(1.0) / np.float32(10000.0) ** (np.arange(0, dim, 2, dtype=np.float32) / np.float32(dim)))
    ang = np.arange(seq, dtype=np.float32)[:, None] * inv.astype(np.float32)[None, :]
    cos, sin = np.cos(ang).T, np.sin(ang).T
    return np.ascontiguousarray(np.stack([np.concatenate([cos, cos] * copies), np.concatenate([sin, -sin] * copies)])
                                ).astype(np.float32)


def kernel(**inputs):
    import numpy as _np
    import concourse.bacc as _bacc
    from concourse import mybir as _mybir
    from concourse.bass_utils import run_bass_kernel_spmd as _run

    nc = _bacc.Bacc("TRN2", target_bir_lowering=False, num_devices=1)
    arrays, args = {}, []
    for name in _INS:
        arrays[f"in_{name}_dram"] = _np.ascontiguousarray(inputs[name])
    seq = inputs["x"].shape[1]
    arrays["in_rope_a_dram"] = _rope_table(seq, 128, 1)
    arrays["in_rope_r_dram"] = _rope_table(seq, 64, 2)
    for name, a in arrays.items():
        args.append(nc.dram_tensor(name, a.shape, _mybir.dt.from_np(a.dtype), kind="ExternalInput").ap())
    shape = inputs["x"].shape
    args.append(nc.dram_tensor("out_0_dram", shape, _mybir.dt.float32, kind="ExternalOutput").ap())
    yoco_kernel(nc, *args)
    r = _run(nc, [arrays], core_ids=[0])
    return r.results[0]["out_0_dram"]
```

```python
from contextlib import ExitStack

import concourse.bass as bass
from concourse import mybir

ALU = mybir.AluOpType
ACT = mybir.ActivationFunctionType
F32 = mybir.dt.float32
F32R = mybir.dt.float32r
AX_X = mybir.AxisListType.X

P = 128
SLOTS = 4
UT = 8
NEG = -3.0e38


def yoco_kernel(nc: bass.Bass, x, norm_gains, ffn_w1, ffn_w3, ffn_w2, moba_w_qkv, moba_w_o, mla_w_dq,
                mla_q_norm, mla_w_uq, mla_w_o, kv_in_norm, w_dkv_kr, kv_norm, w_ukv,
                rope_a, rope_r, out):
    _, S, D = x.shape
    L, _, _, FF = ffn_w1.shape
    KD = D // P
    KF = FF // P
    TS = S // P
    HEADS = moba_w_o.shape[1] // P
    QR = mla_w_dq.shape[2]
    KQ = QR // P
    KVR = kv_norm.shape[0]
    KK = KVR // P
    ROPE = w_dkv_kr.shape[1] - KVR
    HQ = P + ROPE
    A_SCALE = float(P) ** -0.5
    B_SCALE = float(HQ) ** -0.5
    EPS = 1e-6
    DOWN = [min(UT, KF - s) for s in range(0, KF, UT)]
    ND = len(DOWN)
    assert KD == UT and KF == 22 and ND == 3 and TS == 4 and HEADS == 8 and ROPE == 64 and KQ == 4 and KK == 2

    FFN_U = [(UT, 1)] * (2 * KF) + [(n, 1) for n in DOWN] * KD
    MOBA_U = [(UT, 1)] * (3 * HEADS + KD)
    KV_U = [(UT, 1)] * KK + [(UT // 2, 2)] * 2
    MLA_U = [(UT, 1)] * KQ + [(KQ, 2), (UT, 3), (UT, 3)] * (HEADS // 2) + [(UT, 1)] * KD
    stages = [FFN_U, MOBA_U, FFN_U, KV_U, FFN_U, MLA_U, FFN_U]
    FFN_R, WO_R = 2 * KF + KD + 1, KD + 2
    results = [FFN_R, 3 * HEADS + WO_R, FFN_R, KK + 1, FFN_R, KQ + 7 * (HEADS // 2) + WO_R, FFN_R]
    units = [u for s in stages for u in s]
    NU = len(units)
    U0 = [sum(len(s) for s in stages[:i]) for i in range(len(stages))]
    R0 = [sum(results[:i]) for i in range(len(stages))]
    assert all(u % SLOTS == 0 for u in U0)
    landed = []
    for u, (_, dmas) in enumerate(units):
        landed.append((landed[u - SLOTS] if u >= SLOTS else 0) + 16 * dmas)
    FFN_STAGE = {0: 0, 2: 1, 4: 2, 6: 3}

    (N_PRE0, N_F0, N_PRE1, N_MOBA, N_PRE2, N_F1, N_PRE3, N_CKV, N_F2, N_PRE4, N_CQ, N_MLA, N_PRE5, N_F3) = range(14)
    POST_FFN, POST_WO = (N_F0, N_F1, N_F2, N_F3), (N_MOBA, N_MLA)
    NORM_TILES = [KD] * 14
    NORM_TILES[N_CKV], NORM_TILES[N_CQ] = KK, KQ
    for n in POST_FFN + POST_WO:
        NORM_TILES[n] = KD - (1 if n in POST_FFN else 2)
    A0 = [sum(n - 1 for n in NORM_TILES[:i]) for i in range(len(NORM_TILES) + 1)]
    EV0 = [sum(2 if i in POST_FFN + POST_WO else 1 for i in range(n)) for n in range(len(NORM_TILES) + 1)]
    SPREAD0 = [EV0[n] - (n > N_CQ) for n in range(14)]
    LAST = [1 if n in POST_FFN else 2 if n in POST_WO else 0 for n in range(14)]
    SQ_LAST0 = [2 * sum(LAST[:n]) for n in range(14)]
    HALF0 = [sum(LAST[:n]) for n in range(14)]
    HALF = S // 2
    HT = TS // 2

    def half(e):
        return slice(e * HALF, (e + 1) * HALF)
    X_LOAD, X_F0, X_MOBA, X_F1, X_F2, X_MLA, X_F3 = range(7)
    X0 = [0] + [KD + 2 * KD * i for i in range(6)]
    XG0 = [0] + [KD + 2 * KD * i + (KD if i > 2 else 0) for i in range(6)]

    def gain(layer, s, k):
        return (layer * 6 + s) * KD + k
    G_KVIN = L * 6 * KD
    G_Q = G_KVIN + KD
    G_KV = G_Q + KQ
    NG = G_KV + KK

    with ExitStack() as ctx:
        base = [(nc.sbuf_base + 63) // 64 * 64]

        def at(name, shape, dt, offset):
            return nc.alloc_sbuf_tensor_at(name, shape, dt, offset=offset)

        def size(shape):
            n = 4
            for d in shape[1:]:
                n *= d
            return n

        def sb(name, shape, dt=F32):
            o = base[0]
            base[0] += (size(shape) + 31) // 32 * 32
            return at(name, shape, dt, o)

        xT = sb("xT", [P, KD, S])
        xg_base = base[0]
        xg = sb("xg", [P, 2, KD, S], F32R)
        y = at("y", [P, KD, S], F32, xg_base + 4 * KD * S)
        raw = sb("raw", [P, SLOTS, UT, P])
        wh = sb("wh", [P, SLOTS, UT, P], F32R)
        wl = sb("wl", [P, SLOTS, UT, P], F32R)
        h_base = base[0]
        hT = sb("hT", [P, 2, KF, S], F32R)
        ck = sb("ck", [P, KK + 1, S])
        Rb = sb("Rb", [P, S])
        sumsq = sb("sumsq", [P, S])
        T = [sb(f"tmp{i}", [P, S]) for i in range(4)]
        cosT = sb("cosT", [P, S])
        sinT = sb("sinT", [P, S])
        gains = sb("gains", [P, P])
        ident = sb("ident", [P, P])
        ones = sb("ones", [P, P])
        mean_w = {n: sb(f"mean_w{n}", [P, 1]) for n in (D, QR, KVR)}
        var = sb("var", [P, TS])
        neghalf = sb("neghalf", [P, TS])
        rtok = sb("rtok", [P, TS])
        mx = sb("mx", [P, TS])
        nmx = sb("nmx", [P, TS])
        psums = sb("psums", [P, TS])
        rsums = sb("rsums", [P, TS])
        qscale = sb("qscale", [P, TS])
        assert base[0] <= nc.sbuf_usable_end, base[0]

        spot = [h_base]

        def over(name, shape, dt=F32):
            o = spot[0]
            spot[0] += size(shape)
            assert spot[0] <= h_base + 4 * 2 * KF * S
            return at(name, shape, dt, o)

        xin = at("xin", [P, TS, D], F32, h_base)
        gin = at("gin", [P, P], F32, h_base + 4 * TS * D)
        xout = at("xout", [P, 2, HT, D], F32, h_base)
        xkv = at("xkv", [P, 2, KD, S], F32R, h_base)
        ckv_diag = at("ckv_diag", [P, S], F32, h_base + 4 * S * (KF + KF - 4))
        cosR = over("cosR", [P, S])
        sinR = over("sinR", [P, S])
        qh = over("qh", [P, 2, S], F32R)
        kh = over("kh", [P, 2, S], F32R)
        vh_at = spot[0]
        vh = over("vh", [P, 2, 2, TS, P], F32R)
        POFF = [P * c * (c + 1) // 2 for c in range(TS + 1)]
        prob = over("prob", [P, POFF[TS]])
        TOFF = [sum((TS - i) * P for i in range(j)) + P * (j == TS - 1) for j in range(TS)]
        probT = over("probT", [P, 2, TOFF[TS - 1] + P], F32R)
        oT_at = spot[0]
        oT = over("oT", [P, 2, HEADS, S], F32R)
        cq = at("cq", [P, KQ, S], F32, oT_at)
        mask = over("mask", [P, P])
        krT = over("krT", [P, 2, S], F32R)
        qrT = over("qrT", [P, 2, S], F32R)
        ckT_at = spot[0]
        ckT = over("ckT", [P, 2, KK, S], F32R)
        prob_odd = [at(f"prob_odd{i}", [P, POFF[TS]], F32, o) for i, o in enumerate((ckT_at, vh_at))]

        BANK = [(0, 2 * P), (0, 0), (1, 0), (2, 0)]
        PIECES = [(0,), (1,), (2, 3)]

        acc = [ctx.enter_context(nc.psum_tensor(f"acc{i}", [P, S], F32)) for i in range(4)]
        aux = ctx.enter_context(nc.psum_tensor("aux", [P, S], F32))
        sco = [ctx.enter_context(nc.psum_tensor(f"sco{i}", [P, S], F32)) for i in range(3)]
        norm_bank = (aux, sco[0])
        piece_bank = (acc[2], acc[3], acc[2])
        x_bank = (*sco, acc[2], acc[3])
        out_bank = (acc[1], acc[2], sco[1], sco[2])

        def square_buf(n, i):
            if n == N_CQ:
                return (cosR, sinR)[i % 2]
            return T[0] if n in POST_FFN else T[(i - 1) % 3]

        def vT_bank(n):
            return acc[3] if n else aux

        def last_banks(n):
            return (acc[0],) if n == N_F1 else (sco[1], sco[2])

        att_banks, att_free = {}, {}
        for st, special in ((1, {6: aux}), (5, {KQ: sco[1], KQ + 1: sco[2]})):
            att_banks[st] = [special.get(rr, acc[rr if rr < 4 else rr % 2]) for rr in range(results[st] - WO_R)]
            att_free[st] = [max([i + 1 for i in range(rr) if att_banks[st][i] is b], default=0)
                            for rr, b in enumerate(att_banks[st])]
        wo_bank = (acc[0], acc[1], sco[1], sco[2], acc[2], acc[3], acc[0], acc[1])

        def sem(name):
            return ctx.enter_context(nc.semaphore(name))

        raw_full = [sem(f"raw_full{i}") for i in range(SLOTS)]
        w_hi = sem("w_hi")
        w_lo = sem("w_lo")
        unit_done = sem("unit_done")
        head_psum = sem("head_psum")
        half_psum = sem("half_psum")
        evacuated = sem("evacuated")
        const_ready = sem("const_ready")
        gains_in = sem("gains_in")
        gains_psum = sem("gains_psum")
        gains_ready = sem("gains_ready")
        x_in = [sem(f"x_in{k}") for k in range(KD)]
        x_psum = sem("x_psum")
        x_ready = sem("x_ready")
        xhi_ready = sem("xhi_ready")
        xg_ready = sem("xg_ready")
        y0_ready = sem("y0_ready")
        yr_ready = sem("yr_ready")
        sq_ready = sem("sq_ready")
        sq_last = sem("sq_last")
        sumsq_added = sem("sumsq_added")
        var_psum = sem("var_psum")
        var_ready = sem("var_ready")
        rtok_ready = sem("rtok_ready")
        diag_ready = sem("diag_ready")
        r_psum = sem("r_psum")
        r_ready = sem("r_ready")
        silu_ready = sem("silu_ready")
        hid_ready = sem("hid_ready")
        hid_hi = sem("hid_hi")
        hid_lo = sem("hid_lo")
        table_in = sem("table_in")
        mask_ready = sem("mask_ready")
        table_ready = sem("table_ready")
        swapped = sem("swapped")
        roped = sem("roped")
        part_hi = sem("part_hi")
        part_lo = sem("part_lo")
        vT_psum = sem("vT_psum")
        v_hi = sem("v_hi")
        v_lo = sem("v_lo")
        score_psum = sem("score_psum")
        softmax_step = sem("softmax_step")
        nmx_ready = sem("nmx_ready")
        exp_ready = sem("exp_ready")
        prob_ready = sem("prob_ready")
        probT_psum = sem("probT_psum")
        probT_hi = sem("probT_hi")
        probT_lo = sem("probT_lo")
        pv_psum = sem("pv_psum")
        o_hi = sem("o_hi")
        o_lo = sem("o_lo")
        cq_hi = sem("cq_hi")
        cq_lo = sem("cq_lo")
        copied_act = sem("copied_act")
        copied_dve = sem("copied_dve")
        stored = sem("stored")

        block = ctx.enter_context(nc.Block())

        def f32(ap):
            return ap.bitcast(F32)

        def prob_of(n, c, j=None):
            buf = prob_odd[n // HEADS] if n % 2 else prob
            return buf[:, POFF[c]:POFF[c + 1]] if j is None else buf[:, POFF[c] + j * P:POFF[c] + (j + 1) * P]

        def piece_parts(b):
            parts, o = [], 0
            for j in PIECES[b]:
                w = (TS - j) * P
                parts.append((piece_bank[b][:, o:o + w], slice(TOFF[j], TOFF[j] + w)))
                o += w
            return parts

        def out_copy(i):
            e, q = divmod(i, KD // 2)
            return (xout[:, e, :, 2 * P * q:2 * P * (q + 1)],
                    out_bank[i % 4][:].rearrange("p (c f) -> p c f", c=HT))

        def out_done(i):
            return (copied_dve, (i - 2) // 2) if i in (4, 6) else (copied_act, i + 1 if i < 4 else (i + 5) // 2)

        def values_of(n):
            if n < HEADS:
                return vh[:, n % 2, 0], vh[:, n % 2, 1]
            return tuple(xg[:, a, KQ + n % 2].rearrange("p (t d) -> p t d", d=P) for a in range(2))

        mla_rr = {("k", 0): KQ, ("v", 0): KQ + 1, ("r", 0): KQ + 2, ("q", 0): KQ + 3}
        for h in range(1, HEADS):
            for a in ("r",) * (h % 2 == 0) + ("q", "k", "v"):
                mla_rr[a, h // 2 if a == "r" else h] = KQ + len(mla_rr)

        def mla_unit(gg, h=None):
            return U0[5] + KQ + 3 * gg + (0 if h is None else 1 + h % 2)

        def mla_splits(h):
            if h % 2 == 0:
                return [mla_unit((h + 2) // 2) + 2]
            return [mla_unit((h + 3) // 2) + i for i in range(2 if h + 1 < HEADS else 1)]

        def head_result(a, h):
            if h == 0:
                return {"k": (head_psum, 1), "v": (head_psum, 2), "q": (unit_done, mla_unit(0, 0) + 1)}[a]
            return {"q": (head_psum, 2 * h + 1), "k": (head_psum, 2 * h + 2),
                    "v": (unit_done, mla_unit(h // 2, h) + 1)}[a]

        @block.sync
        def _(sp):
            def slot_free(u):
                if isinstance(u, int) and u < SLOTS:
                    return
                sp.wait_ge(w_lo, u - SLOTS + 1)

            def load(slot, j, src):
                n, w = src.shape[1], src.shape[2]
                sp.dma_start(raw[:, slot, j:j + n, 0:w], src).then_inc(raw_full[slot], 16)

            def kpn(w):
                return w.rearrange("(k p) n -> p k n", p=P)

            def ffn(st, layer, i):
                w1, w3 = kpn(ffn_w1[layer, i]), kpn(ffn_w3[layer, i])
                w2 = kpn(ffn_w2[layer, i])

                def up(it):
                    for j in range(2):
                        for a, w in enumerate((w1, w3)):
                            slot_free(U0[st] + 4 * it + 2 * j + a)
                            load(2 * j + a, 0, w[:, :, bass.ds((2 * it + j) * P, P)])

                up(0)
                with sp.Fori(1, KF // 2) as it:
                    up(it)
                with sp.Fori(0, KD // 4) as it:
                    for m in range(4):
                        for s in range(ND):
                            u = ND * m + s
                            slot_free(U0[st] + 2 * KF + 4 * ND * it + u)
                            load(u % SLOTS, 0, w2[:, UT * s:UT * s + DOWN[s], bass.ds((4 * it + m) * P, P)])

            def plain(u0, w, cols):
                for n, c in enumerate(cols):
                    slot_free(u0 + n)
                    load((u0 + n) % SLOTS, 0, w[:, :, c:c + P])

            for k in range(0, KD, 2):
                sp.dma_start(xin[:, :, k * P:(k + 1) * P],
                             x[0].rearrange("(c p) d -> p c d", p=P)[:, :, k * P:(k + 1) * P]
                             ).then_inc(x_in[k], 16)
            ffn(0, 0, 0)
            qkv = kpn(moba_w_qkv[0])
            plain(U0[1], qkv, [HEADS * P * a + P * h for h in range(HEADS) for a in range(3)])
            plain(U0[1] + 3 * HEADS, kpn(moba_w_o[0]), range(0, D, P))
            ffn(2, 0, 1)
            dkv = kpn(w_dkv_kr)
            plain(U0[3], dkv, range(0, KVR, P))
            for part in range(2):
                u = U0[3] + KK + part
                slot_free(u)
                for c in range(2):
                    sp.dma_start(raw[:, u % SLOTS, 0:UT // 2, c * ROPE:(c + 1) * ROPE],
                                 dkv[:, part * UT // 2:(part + 1) * UT // 2, KVR:KVR + ROPE]
                                 ).then_inc(raw_full[u % SLOTS], 16)
            ffn(4, 1, 0)
            plain(U0[5], kpn(mla_w_dq[0]), range(0, QR, P))
            uq, ukv = kpn(mla_w_uq[0]), kpn(w_ukv)
            u = U0[5] + KQ
            for g in range(HEADS // 2):
                slot_free(u)
                for c in range(2):
                    r = HQ * (2 * g + c) + P
                    sp.dma_start(raw[:, u % SLOTS, 0:KQ, c * ROPE:(c + 1) * ROPE],
                                 uq[:, :, r:r + ROPE]).then_inc(raw_full[u % SLOTS], 16)
                u += 1
                for h in (2 * g, 2 * g + 1):
                    slot_free(u)
                    load(u % SLOTS, 0, uq[:, :, HQ * h:HQ * h + P])
                    load(u % SLOTS, KQ, ukv[:, :, 2 * P * h:2 * P * h + P])
                    load(u % SLOTS, KQ + KK, ukv[:, :, 2 * P * h + P:2 * P * (h + 1)])
                    u += 1
            plain(u, kpn(mla_w_o[0]), range(0, D, P))
            ffn(6, 1, 1)
            ov = out[0].rearrange("(e c p) d -> p e c d", p=P, c=HT)
            for e in range(2):
                for q in range(KD // 2):
                    sp.wait_ge(*out_done(KD // 2 * e + q))
                    sp.dma_start(ov[:, e, :, 2 * P * q:2 * P * (q + 1)], xout[:, e, :, 2 * P * q:2 * P * (q + 1)]
                                 ).then_inc(stored, 16)
            sp.wait_ge(stored, 16 * KD)

        @block.gpsimd
        def _(pool):
            g = nc.gpsimd
            g.memset(ident[:], 0.0).then_inc(const_ready, 1)
            pool.wait_ge(const_ready, 1)
            g.affine_select(out=ident[:], in_=ident[:], compare_op=ALU.not_equal, fill=1.0, base=0,
                            pattern=[[-1, P]], channel_multiplier=1).then_inc(const_ready, 1)
            g.memset(ones[:], 1.0)
            for n, t in mean_w.items():
                g.memset(t[:], 1.0 / n)
            g.memset(neghalf[:], -0.5).then_inc(const_ready, 1)

            def rsqrt(ev, cols=slice(0, TS)):
                pool.wait_ge(var_ready, ev + 1)
                g.tensor_tensor(rtok[:, cols], var[:, cols], neghalf[:, cols], ALU.pow).then_inc(rtok_ready, 1)

            def post_norm(n):
                for e in range(2):
                    rsqrt(EV0[n] + e, slice(HT * e, HT * (e + 1)))
                    pool.wait_ge(r_ready, EV0[n] + e + 1)
                    for m in range(1, KD):
                        g.tensor_tensor(y[:, m, half(e)], y[:, m, half(e)], Rb[:, half(e)], ALU.mult
                                        ).then_inc(yr_ready, 1)

            def split_two(u):
                for w in (u + 2, u + 3):
                    pool.wait_ge(w_hi, w + 1)
                    n = units[w][0]
                    g.tensor_tensor(wl[:, w % SLOTS, 0:n], raw[:, w % SLOTS, 0:n], f32(wh[:, w % SLOTS, 0:n]),
                                    ALU.subtract).then_inc(w_lo, 1)

            def rope_add(count, dst):
                pool.wait_ge(swapped, count)
                g.tensor_tensor(dst, T[0][:], T[2][:], ALU.add).then_inc(roped, 1)

            def causal_mask(count, free_after):
                pool.wait_ge(unit_done, free_after)
                g.memset(mask[:], 0.0).then_inc(mask_ready, 1)
                pool.wait_ge(mask_ready, count)
                g.affine_select(out=mask[:], in_=mask[:], compare_op=ALU.is_ge, fill=NEG, base=0,
                                pattern=[[-1, P]], channel_multiplier=1).then_inc(mask_ready, 1)

            split_two(U0[0])
            rsqrt(EV0[N_PRE0])
            post_norm(N_F0)
            split_two(U0[1])
            causal_mask(1, U0[1])
            rsqrt(EV0[N_PRE1])
            for h in range(HEADS):
                rope_add(4 * h + 2, T[3][:])
                rope_add(4 * h + 4, T[3][:])
            post_norm(N_MOBA)
            split_two(U0[2])
            rsqrt(EV0[N_PRE2])
            post_norm(N_F1)
            split_two(U0[3])
            rsqrt(EV0[N_PRE3])
            rope_add(4 * HEADS + 4, ck[:, KK])
            rsqrt(EV0[N_CKV])
            post_norm(N_F2)
            split_two(U0[5])
            causal_mask(3, U0[5])
            rsqrt(EV0[N_PRE4])
            rope_add(4 * HEADS + 8, T[3][:])
            rsqrt(EV0[N_CQ])
            for gg in range(1, HEADS // 2):
                rope_add(4 * HEADS + 4 * (gg + 2), T[3][:])
            post_norm(N_MLA)
            split_two(U0[6])
            rsqrt(EV0[N_PRE5])
            post_norm(N_F3)

        @block.scalar
        def _(act):
            s = nc.scalar
            COPY, SQUARE, EXP, SILU = ACT.Copy, ACT.Square, ACT.Exp, ACT.Silu

            def split_hi(slot, tiles, u, count):
                act.wait_ge(raw_full[slot], count)
                if not (isinstance(u, int) and u < SLOTS):
                    act.wait_ge(unit_done, u - SLOTS + 1)
                s.activation(wh[:, slot, 0:tiles], raw[:, slot, 0:tiles], COPY).then_inc(w_hi, 1)

            def split(u):
                if u < NU:
                    split_hi(u % SLOTS, units[u][0], u, landed[u])

            def square(n, i, src):
                bufs = 1 if n in POST_FFN else 2 if n == N_CQ else 3
                if i == 0 and n:
                    act.wait_ge(var_psum, EV0[n])
                if i > bufs:
                    act.wait_ge(sumsq_added, A0[n] + i - bufs)
                s.activation((square_buf(n, i) if i else sumsq)[:], src, SQUARE).then_inc(sq_ready, 1)

            def x_update(t, targets, before_second=(), middle=()):
                for a, (gcol, dst) in enumerate(targets):
                    for e in range(2 if a == 0 else 1):
                        if e == 1:
                            for u in before_second:
                                split(u)
                        for m in range(KD):
                            if a == 0:
                                act.wait_ge(x_ready, X0[t] + KD * e + m + 1)
                            if a == 1 and m == KD // 2:
                                for u in middle:
                                    split(u)
                            cols = half(e) if a == 0 else slice(0, S)
                            s.activation(dst[:, 0, m, cols], xT[:, m, cols], COPY,
                                         scale=gains[:, gcol + m:gcol + m + 1]).then_inc(xhi_ready, 1)

            def x_squares(n):
                for m in range(KD):
                    square(n, m, xT[:, m])

            def ffn(st, n_post):
                F0 = KF * FFN_STAGE[st]

                def up(it, peeled=False):
                    for j in range(2):
                        for v in ((2 * j + 2, 2 * j + 3), (4, 5) if j == 0 else ())[peeled]:
                            split_hi(v % SLOTS, UT, U0[st] + 4 * it + v, landed[U0[st] + v] + 16 * it)
                        act.wait_ge(evacuated, R0[st] + 4 * it + 2 * j + 1)
                        s.activation(T[1][:], T[0][:], SILU).then_inc(silu_ready, 1)
                        act.wait_ge(hid_ready, F0 + 2 * it + j + 1)
                        s.activation(hT[:, 0, bass.ds(2 * it + j, 1)].rearrange("p a s -> p (a s)"),
                                     T[3][:], COPY).then_inc(hid_hi, 1)

                up(0, peeled=True)
                with act.Fori(1, KF // 2) as it:
                    up(it)
                d0 = U0[st] + 2 * KF
                for m in range(KD - 1):
                    for v in range(ND * m + 2, ND * m + 2 + ND):
                        split(d0 + v)
                    act.wait_ge(evacuated, R0[st] + 2 * KF + m + 1)
                    square(n_post, m, y[:, m])
                split(d0 + ND * KD - 1)
                split(d0 + ND * KD)
                split(d0 + ND * KD + 1)

            def exchange(products, count, width):
                act.wait_ge(products, count)
                for b in range(0, P, 2 * width):
                    for i, o in ((b + width, b), (b, b + width)):
                        s.activation(T[2][o:o + width], T[1][i:i + width], COPY).then_inc(swapped, 1)

            def part(dst, src=T[3][:]):
                s.activation(dst, src, COPY).then_inc(part_hi, 1)

            def softmax_exp(n):
                act.wait_ge(nmx_ready, n + 1)
                if n > 1:
                    act.wait_ge(probT_psum, 3 * (n - 1))
                for c in range(TS):
                    bank, o = BANK[c]
                    s.activation(prob_of(n, c), sco[bank][:, o:o + (c + 1) * P], EXP,
                                 bias=nmx[:, c:c + 1], scale=A_SCALE if n < HEADS else qscale[:, c:c + 1],
                                 accum_out=psums[:, c:c + 1]).then_inc(exp_ready, 1)

            def probT_split(n, pieces):
                for b in pieces:
                    act.wait_ge(probT_psum, 3 * n + b + 1)
                    for src, at_ in piece_parts(b):
                        ins = s.activation(probT[:, 0, at_], src, COPY)
                    ins.then_inc(probT_hi, 1)

            def probT_zeros():
                s.activation(probT[:, :, TOFF[TS - 1] - P:TOFF[TS - 1]],
                             ident[:].unsqueeze(1).broadcast_to([P, 2, P]), COPY, scale=0.0)

            def o_split(n):
                act.wait_ge(pv_psum, n + 1)
                s.activation(oT[:, 0, n % HEADS], aux[:], COPY).then_inc(o_hi, 1)

            def v_split(n):
                act.wait_ge(vT_psum, n + 1)
                s.activation(values_of(n)[0], vT_bank(n)[:].rearrange("p (t d) -> p t d", d=P), COPY
                             ).then_inc(v_hi, 1)

            def out_proj(u, r, n):
                for m in range(KD - 1):
                    if m < KD - 2:
                        split(u + m + 4)
                    if m:
                        act.wait_ge(evacuated, r + m)
                        square(n, m - 1, y[:, m - 1])

            s.dma_start(gin[0:G_KVIN], norm_gains.rearrange("l s (k f) -> (l s k) f", f=P)).then_inc(gains_in, 16)
            s.dma_start(gin[G_KVIN:G_Q], kv_in_norm.rearrange("(k f) -> k f", f=P)).then_inc(gains_in, 16)
            s.dma_start(gin[G_Q:G_KV], mla_q_norm.rearrange("a (k f) -> (a k) f", f=P)).then_inc(gains_in, 16)
            s.dma_start(gin[G_KV:NG], kv_norm.rearrange("(k f) -> k f", f=P)).then_inc(gains_in, 16)
            for k in range(1, KD, 2):
                s.dma_start(xin[:, :, k * P:(k + 1) * P],
                            x[0].rearrange("(c p) d -> p c d", p=P)[:, :, k * P:(k + 1) * P]
                            ).then_inc(x_in[k], 16)
            s.dma_start(cosT[:], rope_a[0]).then_inc(table_in, 16)
            s.dma_start(sinT[:], rope_a[1]).then_inc(table_in, 16)
            split(0)
            split(1)
            act.wait_ge(gains_ready, 1)
            for m in range(KD):
                act.wait_ge(x_ready, m + 1)
                s.activation(xg[:, 0, m], xT[:, m], COPY, scale=gains[:, gain(0, 0, m):gain(0, 0, m) + 1]
                             ).then_inc(xhi_ready, 1)
            split(2)
            split(3)
            x_squares(N_PRE0)
            ffn(0, N_F0)

            u, r = U0[1], R0[1]
            x_update(X_F0, [(gain(0, 2, 0), xg)], before_second=(u + 2,))
            split(u + 3)
            x_squares(N_PRE1)
            for w in (4, 5, 6):
                split(u + w)

            def exchanged(h, i):
                exchange(evacuated, r + 3 * h + i + 1, P // 2)

            def rotated(h, i):
                act.wait_ge(roped, 2 * h + i + 1)
                if h:
                    act.wait_ge(score_psum, 3 * h)
                part((qh, kh)[i][:, 0])

            probT_zeros()
            for i in range(2):
                exchanged(0, i)
                rotated(0, i)
            v_split(0)
            exchanged(1, 0)
            rotated(1, 0)
            exchanged(1, 1)
            split(u + 7)
            rotated(1, 1)
            softmax_exp(0)
            v_split(1)
            split(u + 8)
            split(u + 9)
            for h in range(1, HEADS - 1):
                exchanged(h + 1, 0)
                probT_split(h - 1, (0, 1))
                rotated(h + 1, 0)
                split(u + 3 * h + 7)
                softmax_exp(h)
                exchanged(h + 1, 1)
                probT_split(h - 1, (2,))
                split(u + 3 * h + 8)
                rotated(h + 1, 1)
                o_split(h - 1)
                split(u + 3 * h + 9)
                v_split(h + 1)
            probT_split(HEADS - 2, (0, 1, 2))
            softmax_exp(HEADS - 1)
            o_split(HEADS - 2)
            probT_split(HEADS - 1, (0, 1, 2))
            o_split(HEADS - 1)
            s.dma_start(cosT[:], rope_r[0]).then_inc(table_in, 16)
            s.dma_start(sinT[:], rope_r[1]).then_inc(table_in, 16)
            out_proj(u + 3 * HEADS, r + 3 * HEADS, N_MOBA)
            x_update(X_MOBA, [(gain(0, 4, 0), xg)], before_second=(U0[2] + 2, U0[2] + 3))
            x_squares(N_PRE2)
            ffn(2, N_F1)

            u, r = U0[3], R0[3]
            x_update(X_F1, [(G_KVIN, xkv), (gain(1, 0, 0), xg)], before_second=(u + 2, u + 3),
                     middle=(u + 4, u + 5))
            x_squares(N_PRE3)
            split(u + 6)
            split(u + 7)
            for i in range(KK):
                act.wait_ge(evacuated, r + i + 1)
                square(N_CKV, i, ck[:, i])
            exchange(table_ready, 3, ROPE // 2)
            ffn(4, N_F2)

            u, r = U0[5], R0[5]
            x_update(X_F2, [(gain(1, 2, 0), xg)], before_second=(u + 2,))
            split(u + 3)
            x_squares(N_PRE4)
            for i in range(KK):
                s.activation(ckT[:, 0, i], ck[:, i], COPY).then_inc(cq_hi, 1)
            s.activation(krT[:, 0], ck[:, KK], COPY).then_inc(cq_hi, 1)
            for w in (4, 5, 6):
                split(u + w)
            for m in range(KQ):
                act.wait_ge(evacuated, r + m + 1)
                if m == 0:
                    act.wait_ge(unit_done, u + KQ)
                s.activation(xg[:, 0, m], cq[:, m], COPY, scale=gains[:, G_Q + m:G_Q + m + 1]
                             ).then_inc(cq_hi, 1)

            def exchanged(gg):
                exchange(evacuated, r + mla_rr["r", gg] + 1, ROPE // 2)

            def rotated(gg):
                act.wait_ge(roped, 2 * HEADS + 2 + gg)
                part(qrT[:, 0])

            def direct(a, h, dst):
                act.wait_ge(*head_result(a, h))
                part(dst, att_banks[5][mla_rr[a, h]][:])

            direct("k", 0, kh[:, 0])
            probT_zeros()
            for m in range(KQ):
                square(N_CQ, m, cq[:, m])
            v_split(HEADS)
            exchanged(0)
            direct("q", 0, qh[:, 0])
            rotated(0)
            split(u + 7)
            split(u + 8)
            for h in range(HEADS):
                nxt = h + 1 < HEADS
                n = HEADS + h
                turn = nxt and h % 2
                if h:
                    probT_split(n - 1, (0,))
                act.wait_ge(score_psum, 3 * (n + 1))
                if nxt:
                    direct("q", h + 1, qh[:, 0])
                if h:
                    probT_split(n - 1, (1, 2))
                if turn:
                    exchanged((h + 1) // 2)
                if nxt:
                    direct("k", h + 1, kh[:, 0])
                if turn:
                    rotated((h + 1) // 2)
                softmax_exp(n)
                for w in mla_splits(h):
                    split(w)
                if h:
                    o_split(n - 1)
                if nxt:
                    v_split(n + 1)
            probT_split(2 * HEADS - 1, (0, 1, 2))
            o_split(2 * HEADS - 1)
            out_proj(u + KQ + 12, r + KQ + 28, N_MLA)
            x_update(X_MLA, [(gain(1, 4, 0), xg)], before_second=(U0[6] + 2, U0[6] + 3))
            x_squares(N_PRE5)
            ffn(6, N_F3)
            for i in (0, 1, 2, 3, 5, 7):
                act.wait_ge(x_psum, KD + i + 1)
                s.activation(*out_copy(i), COPY).then_inc(copied_act, 1)

        @block.vector
        def _(dve):
            v = nc.vector

            def split_lo(slot, tiles, u):
                dve.wait_ge(w_hi, u + 1)
                v.tensor_tensor(wl[:, slot, 0:tiles], raw[:, slot, 0:tiles], f32(wh[:, slot, 0:tiles]),
                                ALU.subtract).then_inc(w_lo, 1)

            def split(u):
                if u < NU:
                    split_lo(u % SLOTS, units[u][0], u)

            def add_square(n, i):
                dve.wait_ge(sq_ready, sum(NORM_TILES[:n]) + i + 1)
                dve.wait_ge(sumsq_added, A0[n] + i - 1)
                v.tensor_tensor(sumsq[:], sumsq[:], square_buf(n, i)[:], ALU.add).then_inc(sumsq_added, 1)

            def norm_diag(n, e, factor, diag, cols=slice(0, TS)):
                ev = EV0[n] + e
                dve.wait_ge(var_psum, ev + 1)
                v.tensor_scalar(var[:, cols], norm_bank[e][:, cols], EPS, None, ALU.add).then_inc(var_ready, 1)
                dve.wait_ge(rtok_ready, ev + 1)
                w = cols.stop - cols.start
                v.scalar_tensor_tensor(out=diag[:, cols.start * P:cols.stop * P].rearrange("p (t q) -> p t q", q=P),
                                       in0=ident[:].unsqueeze(1).broadcast_to([P, w, P]), scalar=factor,
                                       in1=rtok[:, cols].unsqueeze(2).broadcast_to([P, w, P]),
                                       op0=ALU.mult, op1=ALU.mult).then_inc(diag_ready, 1)

            def norm_factor(n, with_diag=True):
                if with_diag:
                    norm_diag(n, 0, 1.0, T[3])
                dve.wait_ge(r_psum, SPREAD0[n] + 1)
                v.tensor_copy(Rb[:], aux[:]).then_inc(r_ready, 1)
                dve.wait_ge(r_ready, EV0[n] + 1)

            def gated_split(t, nth, m, gcol, dst, cols):
                dve.wait_ge(xhi_ready, XG0[t] + nth + 1)
                v.scalar_tensor_tensor(out=dst[:, 1, m, cols], in0=xT[:, m, cols],
                                       scalar=gains[:, gcol + m:gcol + m + 1], in1=f32(dst[:, 0, m, cols]),
                                       op0=ALU.mult, op1=ALU.subtract).then_inc(xg_ready, 1)

            def last_tiles(n, e, tiles, r_count):
                for m, bank, done, count in tiles:
                    dve.wait_ge(done, count)
                    v.tensor_copy(y[:, m, half(e)], bank[:, half(e)]).then_inc(evacuated, 1)
                dve.wait_ge(evacuated, r_count)
                dve.wait_ge(sumsq_added, A0[n + 1])
                for i, (m, *_) in enumerate(tiles):
                    v.tensor_tensor(T[1 + i][:, half(e)], y[:, m, half(e)], y[:, m, half(e)], ALU.mult
                                    ).then_inc(sq_last, 1)

            def x_update(t, n, factor, g_post, targets, lasts, next_unit=None):
                last_tiles(n, 0, *lasts[0])

                def diag(e):
                    norm_diag(n, e, factor, T[3], slice(HT * e, HT * (e + 1)))

                def first(e):
                    dve.wait_ge(r_psum, SPREAD0[n] + e + 1)
                    v.tensor_tensor(T[2][:, half(e)], y[:, 0, half(e)], norm_bank[e][:, half(e)], ALU.mult
                                    ).then_inc(y0_ready, 1)
                    v.tensor_copy(Rb[:, half(e)], norm_bank[e][:, half(e)]).then_inc(r_ready, 1)

                diag(0)
                if next_unit is not None:
                    split(next_unit)
                first(0)
                for e in range(2):
                    for m in range(KD + 1):
                        if m < KD:
                            if m == 0:
                                dve.wait_ge(y0_ready, 2 * (t - 1) + e + 1)
                                src = T[2][:, half(e)]
                            else:
                                dve.wait_ge(yr_ready, 2 * (KD - 1) * (t - 1) + (KD - 1) * e + m)
                                src = y[:, m, half(e)]
                            v.scalar_tensor_tensor(out=xT[:, m, half(e)], in0=src,
                                                   scalar=gains[:, g_post + m:g_post + m + 1],
                                                   in1=xT[:, m, half(e)], op0=ALU.mult, op1=ALU.add
                                                   ).then_inc(x_ready, 1)
                        if m and targets:
                            dve.wait_ge(x_ready, X0[t] + KD * e + m)
                            gated_split(t, KD * e + m - 1, m - 1, *targets[0], half(e))
                        if e == 0 and m == 2:
                            last_tiles(n, 1, *lasts[1])
                        if e == 0 and m == 4:
                            diag(1)
                        if e == 0 and m == 6:
                            first(1)

            def x_squares(n):
                for m in range(1, KD):
                    add_square(n, m)

            def ffn(st, n_pre, n_post, middle=None):
                F0 = KF * FFN_STAGE[st]

                def up(it, peeled=False):
                    for j in range(2):
                        if peeled and j == 0:
                            dve.wait_ge(w_lo, U0[st] + 4)
                        for w in ((2 * j + 2, 2 * j + 3), (4, 5) if j == 0 else ())[peeled]:
                            split_lo(w % SLOTS, UT, U0[st] + 4 * it + w)
                        if peeled and j == 0 and n_pre is not None:
                            norm_factor(n_pre)
                        f = F0 + 2 * it + j
                        dve.wait_ge(unit_done, U0[st] + 4 * it + 2 * j + 1)
                        v.tensor_tensor(T[0][:], acc[2 * j][:], Rb[:], ALU.mult).then_inc(evacuated, 1)
                        dve.wait_ge(unit_done, U0[st] + 4 * it + 2 * j + 2)
                        v.tensor_tensor(T[2][:], acc[2 * j + 1][:], Rb[:], ALU.mult).then_inc(evacuated, 1)
                        dve.wait_ge(evacuated, R0[st] + 4 * it + 2 * j + 2)
                        dve.wait_ge(silu_ready, f + 1)
                        v.tensor_tensor(T[3][:], T[1][:], T[2][:], ALU.mult).then_inc(hid_ready, 1)
                        dve.wait_ge(hid_ready, f + 1)
                        dve.wait_ge(hid_hi, f + 1)
                        at_ = bass.ds(2 * it + j, 1)
                        v.tensor_tensor(hT[:, 1, at_].rearrange("p a s -> p (a s)"), T[3][:],
                                        f32(hT[:, 0, at_].rearrange("p a s -> p (a s)")),
                                        ALU.subtract).then_inc(hid_lo, 1)
                        if peeled and j == 0 and middle is not None:
                            middle()

                up(0, peeled=True)
                with dve.Fori(1, KF // 2) as it:
                    up(it)
                d0, r0 = U0[st] + 2 * KF, R0[st] + 2 * KF
                for m in range(KD - 1):
                    for w in range(ND * m + 2, ND * m + 2 + ND):
                        split(d0 + w)
                    dve.wait_ge(unit_done, d0 + ND * (m + 1))
                    v.tensor_copy(y[:, m], acc[m % 4][:]).then_inc(evacuated, 1)
                    if m:
                        add_square(n_post, m)
                split(d0 + ND * KD - 1)
                split(d0 + ND * KD)
                return (([(KD - 1, acc[3], half_psum, HALF0[n_post] + 1)], r0 + KD),
                        ([(KD - 1, last_banks(n_post)[0], unit_done, d0 + ND * KD)], r0 + KD + 1))

            def rope_products(u_count, bank, cos, sin):
                dve.wait_ge(unit_done, u_count)
                v.tensor_tensor(T[1][:], bank, sin[:], ALU.mult)
                v.tensor_tensor(T[0][:], bank, cos[:], ALU.mult).then_inc(evacuated, 1)

            def part(n, dst):
                dve.wait_ge(part_hi, n + 1)
                v.tensor_tensor(dst[:, 1], T[3][:], f32(dst[:, 0]), ALU.subtract).then_inc(part_lo, 1)

            steps = [0]

            def step(ins):
                steps[0] += 1
                ins.then_inc(softmax_step, 1)
                dve.wait_ge(softmax_step, steps[0])

            def softmax_max(n):
                dve.wait_ge(score_psum, 3 * (n + 1))
                if n % HEADS == 0:
                    dve.wait_ge(mask_ready, 2 * (n // HEADS + 1))
                for c in range(TS):
                    bank, o = BANK[c]
                    diag = sco[bank][:, o + c * P:o + (c + 1) * P]
                    ins = v.tensor_tensor(diag, diag, mask[:], ALU.add)
                step(ins)
                for c in range(TS):
                    bank, o = BANK[c]
                    ins = v.tensor_reduce(mx[:, c:c + 1], sco[bank][:, o:o + (c + 1) * P], AX_X, ALU.max)
                step(ins)
                if n < HEADS:
                    v.tensor_scalar(nmx[:], mx[:], -A_SCALE, None, ALU.mult).then_inc(nmx_ready, 1)
                else:
                    v.scalar_tensor_tensor(out=nmx[:], in0=mx[:], scalar=-1.0, in1=qscale[:],
                                           op0=ALU.mult, op1=ALU.mult).then_inc(nmx_ready, 1)

            def softmax_norm(n):
                dve.wait_ge(exp_ready, TS * (n + 1))
                step(v.reciprocal(rsums[:], psums[:]))
                for c in range(TS):
                    pc = prob_of(n, c)
                    v.tensor_scalar(pc, pc, rsums[:, c:c + 1], None, ALU.mult).then_inc(prob_ready, 1)

            def probT_split(n, pieces):
                for b in pieces:
                    dve.wait_ge(probT_hi, 3 * n + b + 1)
                    for src, at_ in piece_parts(b):
                        ins = v.tensor_tensor(probT[:, 1, at_], src, f32(probT[:, 0, at_]), ALU.subtract)
                    ins.then_inc(probT_lo, 1)

            def o_split(n):
                dve.wait_ge(o_hi, n + 1)
                v.tensor_tensor(oT[:, 1, n % HEADS], aux[:], f32(oT[:, 0, n % HEADS]),
                                ALU.subtract).then_inc(o_lo, 1)

            def v_split(n):
                dve.wait_ge(v_hi, n + 1)
                v_h, v_l = values_of(n)
                v.tensor_tensor(v_l, vT_bank(n)[:].rearrange("p (t d) -> p t d", d=P), f32(v_h),
                                ALU.subtract).then_inc(v_lo, 1)

            def out_proj(u, r, n):
                for m in range(KD - 2):
                    split(u + m + 4)
                    dve.wait_ge(unit_done, u + m + 1)
                    v.tensor_copy(y[:, m], wo_bank[m][:]).then_inc(evacuated, 1)
                    if m > 1:
                        add_square(n, m - 1)
                add_square(n, KD - 3)
                return (([(KD - 2 + i, wo_bank[KD - 2 + i], half_psum, HALF0[n] + 1 + i) for i in range(2)], r + KD),
                        ([(KD - 2 + i, last_banks(n)[i], unit_done, u + KD - 1 + i) for i in range(2)], r + KD + 2))

            split(0)
            split(1)
            dve.wait_ge(gains_psum, 1)
            v.tensor_copy(gains[:, 0:NG], aux[:, 0:NG]).then_inc(gains_ready, 1)
            for m in range(KD + 1):
                if m < KD:
                    dve.wait_ge(x_psum, m + 1)
                    v.tensor_copy(xT[:, m], x_bank[m % 5][:]).then_inc(x_ready, 1)
                if m:
                    dve.wait_ge(x_ready, m)
                    if m == 1:
                        dve.wait_ge(gains_ready, 1)
                    gated_split(X_LOAD, m - 1, m - 1, gain(0, 0, 0), xg, slice(0, S))
            x_squares(N_PRE0)
            lasts = ffn(0, N_PRE0, N_F0)
            x_update(X_F0, N_F0, 0.5, gain(0, 1, 0), [(gain(0, 2, 0), xg)], lasts, U0[1] + 1)

            u, r = U0[1], R0[1]
            x_squares(N_PRE1)
            dve.wait_ge(w_lo, u + 4)
            split(u + 4)
            norm_diag(N_PRE1, 0, 1.0, T[3])
            split(u + 5)
            split(u + 6)
            norm_factor(N_PRE1, with_diag=False)
            dve.wait_ge(table_in, 32)
            v.tensor_tensor(cosR[:], cosT[:], Rb[:], ALU.mult).then_inc(table_ready, 1)
            v.tensor_tensor(sinR[:], sinT[:], Rb[:], ALU.mult).then_inc(table_ready, 1)
            dve.wait_ge(table_ready, 2)

            def evac_v(u_count, bank):
                dve.wait_ge(unit_done, u_count)
                v.tensor_tensor(T[0][:], bank, Rb[:], ALU.mult).then_inc(evacuated, 1)

            def products(h, i):
                rope_products(u + 3 * h + i + 1, att_banks[1][3 * h + i][:], cosR, sinR)

            def rotated(h, i):
                part(2 * h + i, (qh, kh)[i])

            for i in range(2):
                products(0, i)
                rotated(0, i)
            evac_v(u + 3, acc[2][:])
            v_split(0)
            products(1, 0)
            softmax_max(0)
            rotated(1, 0)
            products(1, 1)
            split(u + 7)
            rotated(1, 1)
            evac_v(u + 6, att_banks[1][5][:])
            softmax_norm(0)
            v_split(1)
            split(u + 8)
            split(u + 9)
            for h in range(1, HEADS - 1):
                products(h + 1, 0)
                softmax_max(h)
                probT_split(h - 1, (0, 1))
                rotated(h + 1, 0)
                split(u + 3 * h + 7)
                softmax_norm(h)
                products(h + 1, 1)
                probT_split(h - 1, (2,))
                split(u + 3 * h + 8)
                rotated(h + 1, 1)
                o_split(h - 1)
                split(u + 3 * h + 9)
                evac_v(u + 3 * h + 6, att_banks[1][3 * h + 5][:])
                v_split(h + 1)
            probT_split(HEADS - 2, (0, 1, 2))
            softmax_max(HEADS - 1)
            softmax_norm(HEADS - 1)
            o_split(HEADS - 2)
            probT_split(HEADS - 1, (0, 1, 2))
            o_split(HEADS - 1)
            lasts = out_proj(u + 3 * HEADS, r + 3 * HEADS, N_MOBA)
            x_update(X_MOBA, N_MOBA, 1.0, gain(0, 3, 0), [(gain(0, 4, 0), xg)], lasts)
            x_squares(N_PRE2)
            lasts = ffn(2, N_PRE2, N_F1)

            u, r = U0[3], R0[3]
            x_update(X_F1, N_F1, 0.5, gain(0, 5, 0), [(G_KVIN, xkv)], lasts, u + 1)
            for m in range(KD):
                if m == KD // 2:
                    dve.wait_ge(w_lo, u + 4)
                    split(u + 4)
                    split(u + 5)
                gated_split(X_F1, 2 * KD + m, m, gain(1, 0, 0), xg, slice(0, S))
            x_squares(N_PRE3)
            split(u + 6)
            split(u + 7)
            norm_factor(N_PRE3)
            for m in range(KK):
                dve.wait_ge(unit_done, u + m + 1)
                v.tensor_tensor(ck[:, m], sco[1 + m][:], Rb[:], ALU.mult).then_inc(evacuated, 1)
            dve.wait_ge(unit_done, u + KK + 2)
            v.tensor_tensor(T[3][:], acc[3][:], Rb[:], ALU.mult).then_inc(evacuated, 1)
            dve.wait_ge(evacuated, r + KK + 1)
            for i in range(1, KK):
                add_square(N_CKV, i)
            dve.wait_ge(sumsq_added, A0[N_CKV + 1])
            dve.wait_ge(table_in, 64)
            v.tensor_tensor(T[1][:], T[3][:], sinT[:], ALU.mult)
            v.tensor_tensor(T[0][:], T[3][:], cosT[:], ALU.mult).then_inc(table_ready, 1)
            norm_diag(N_CKV, 0, 1.0, ckv_diag)
            dve.wait_ge(roped, 2 * HEADS + 1)

            def ck_scale():
                dve.wait_ge(r_psum, SPREAD0[N_CKV] + 1)
                for i in range(KK):
                    v.scalar_tensor_tensor(out=ck[:, i], in0=ck[:, i], scalar=gains[:, G_KV + i:G_KV + i + 1],
                                           in1=aux[:], op0=ALU.mult, op1=ALU.mult
                                           ).then_inc(r_ready if i == KK - 1 else table_ready, 1)

            lasts = ffn(4, None, N_F2, middle=ck_scale)
            x_update(X_F2, N_F2, 0.5, gain(1, 1, 0), [(gain(1, 2, 0), xg)], lasts, U0[5] + 1)

            u, r = U0[5], R0[5]
            x_squares(N_PRE4)
            dve.wait_ge(w_lo, u + 4)
            for i in range(KK):
                dve.wait_ge(cq_hi, i + 1)
                v.tensor_tensor(ckT[:, 1, i], ck[:, i], f32(ckT[:, 0, i]), ALU.subtract).then_inc(cq_lo, 1)
            dve.wait_ge(cq_hi, KK + 1)
            v.tensor_tensor(krT[:, 1], ck[:, KK], f32(krT[:, 0]), ALU.subtract).then_inc(cq_lo, 1)
            norm_diag(N_PRE4, 0, 1.0, T[3])
            for w in (4, 5, 6):
                split(u + w)
            norm_factor(N_PRE4, with_diag=False)
            for m in range(KQ):
                dve.wait_ge(unit_done, u + m + 1)
                v.tensor_tensor(cq[:, m], acc[m][:], Rb[:], ALU.mult).then_inc(evacuated, 1)
            dve.wait_ge(evacuated, r + KQ)
            for m in range(KQ):
                dve.wait_ge(cq_hi, KK + 1 + m + 1)
                v.scalar_tensor_tensor(out=xg[:, 1, m], in0=cq[:, m], scalar=gains[:, G_Q + m:G_Q + m + 1],
                                       in1=f32(xg[:, 0, m]), op0=ALU.mult, op1=ALU.subtract).then_inc(cq_lo, 1)
            def direct(a, h, dst):
                dve.wait_ge(*head_result(a, h))
                dve.wait_ge(part_hi, parts[0] + 1)
                v.tensor_tensor(dst[:, 1], att_banks[5][mla_rr[a, h]][:], f32(dst[:, 0]), ALU.subtract
                                ).then_inc(evacuated, 1)
                parts[0] += 1

            def copy_v(h):
                dve.wait_ge(*head_result("v", h))
                v.tensor_copy(T[0][:], att_banks[5][mla_rr["v", h]][:]).then_inc(evacuated, 1)

            def products(gg):
                rope_products(mla_unit(gg) + 1, att_banks[5][mla_rr["r", gg]][:], cosT, sinT)

            def rotated():
                dve.wait_ge(part_hi, parts[0] + 1)
                v.tensor_tensor(qrT[:, 1], T[3][:], f32(qrT[:, 0]), ALU.subtract).then_inc(part_lo, 1)
                parts[0] += 1

            parts = [2 * HEADS]
            direct("k", 0, kh)
            copy_v(0)
            for m in range(1, KQ):
                add_square(N_CQ, m)
            dve.wait_ge(vT_psum, HEADS + 1)
            products(0)
            v_split(HEADS)
            direct("q", 0, qh)
            rotated()
            split(u + 7)
            split(u + 8)
            dve.wait_ge(var_psum, EV0[N_CQ] + 1)
            v.tensor_scalar(var[:], norm_bank[0][:, 0:TS], EPS, None, ALU.add).then_inc(var_ready, 1)
            dve.wait_ge(rtok_ready, EV0[N_CQ] + 1)
            v.tensor_scalar(qscale[:], rtok[:], B_SCALE, None, ALU.mult).then_inc(r_ready, 1)
            dve.wait_ge(r_ready, EV0[N_CQ] + 1)
            for h in range(HEADS):
                nxt = h + 1 < HEADS
                n = HEADS + h
                turn = nxt and h % 2
                if h:
                    probT_split(n - 1, (0,))
                if turn:
                    products((h + 1) // 2)
                if nxt:
                    direct("q", h + 1, qh)
                if h:
                    probT_split(n - 1, (1, 2))
                softmax_max(n)
                if nxt:
                    direct("k", h + 1, kh)
                if turn:
                    rotated()
                if nxt:
                    copy_v(h + 1)
                softmax_norm(n)
                for w in mla_splits(h):
                    split(w)
                if h:
                    o_split(n - 1)
                if nxt:
                    v_split(n + 1)
            probT_split(2 * HEADS - 1, (0, 1, 2))
            o_split(2 * HEADS - 1)
            lasts = out_proj(u + KQ + 12, r + KQ + 28, N_MLA)
            x_update(X_MLA, N_MLA, 1.0, gain(1, 3, 0), [(gain(1, 4, 0), xg)], lasts)
            x_squares(N_PRE5)
            lasts = ffn(6, N_PRE5, N_F3)
            x_update(X_F3, N_F3, 0.5, gain(1, 5, 0), [], lasts)
            for i in (4, 6):
                dve.wait_ge(x_psum, KD + i + 1)
                v.tensor_copy(*out_copy(i)).then_inc(copied_dve, 1)

        @block.tensor
        def _(pe):
            t = nc.tensor

            def product(dst, w_h, w_l, m_h, m_l, start, stop):
                t.matmul(dst, w_h, m_h, start=start, stop=False)
                t.matmul(dst, w_h, m_l, start=False, stop=False)
                return t.matmul(dst, w_l, m_h, start=False, stop=stop)

            def tiles(dst, slot, first, n, moving, start=True, stop=True, before=None, k0=0):
                for k in range(k0, n):
                    if before is not None:
                        before(k)
                    m_h, m_l = moving(k)
                    ins = product(dst, wh[:, slot, first + k], wl[:, slot, first + k], m_h, m_l,
                                  start and k == k0, stop and k == n - 1)
                return ins

            def from_x(buf, cols=slice(0, S)):
                return lambda k: (buf[:, 0, k, cols], buf[:, 1, k, cols])

            def mean(n, e=0, width=D, cols=range(TS), last=()):
                pe.wait_ge(sumsq_added, A0[n + 1])
                if last:
                    pe.wait_ge(sq_last, SQ_LAST0[n] + len(last) * (e + 1))
                if EV0[n]:
                    pe.wait_ge(r_ready, EV0[n])
                for c in cols:
                    parts = [sumsq, *last]
                    for i, src in enumerate(parts):
                        ins = t.matmul(norm_bank[e][:, c:c + 1], src[:, c * P:(c + 1) * P], mean_w[width][:],
                                       start=i == 0, stop=i == len(parts) - 1)
                ins.then_inc(var_psum, 1)

            def spread(n, e=0, cols=slice(0, S), diag=T[3]):
                pe.wait_ge(diag_ready, SPREAD0[n] + e + 1)
                t.matmul(norm_bank[e][:, cols], ones[:], diag[:, cols], start=True, stop=True).then_inc(r_psum, 1)

            def post_mean(n, e):
                mean(n, e, D, range(HT * e, HT * (e + 1)), T[1:1 + LAST[n]])

            def post_spread(n, e):
                spread(n, e, half(e))

            def unit(u, dst, moving, n=UT, **kw):
                pe.wait_ge(w_lo, u + 1)
                tiles(dst, u % SLOTS, 0, n, moving, **kw).then_inc(unit_done, 1)

            def pair(u, banks, buf, xg0, by_halves, after=None):
                pe.wait_ge(w_lo, u + 2)
                cols = [half(0), half(1)] if by_halves else [slice(0, S)]
                for e, cs in enumerate(cols):
                    for k in range(UT):
                        pe.wait_ge(xg_ready, xg0 + KD * e + k + 1)
                        for a in range(2):
                            ins = product(banks[a][:, cs], wh[:, (u + a) % SLOTS, k], wl[:, (u + a) % SLOTS, k],
                                          buf[:, 0, k, cs], buf[:, 1, k, cs], k == 0, k == UT - 1)
                            if k == UT - 1 and e == len(cols) - 1:
                                ins.then_inc(unit_done, 1)
                        if after is not None:
                            after(e, k)

            def second_norm(n):
                def after(e, k):
                    if e == 0 and k == 1:
                        post_mean(n, 1)
                    if e == 0 and k == 3:
                        post_spread(n, 1)
                return after

            def norm_among(n, at_mean, at_spread):
                def before(k):
                    if k == at_mean:
                        mean(n)
                    if k == at_spread:
                        spread(n)
                return before

            def norm_over_two(u, n):
                unit(u + 2, acc[2][:], from_x(xg))
                unit(u + 3, acc[3][:], from_x(xg), before=norm_among(n, 0, 4))

            def shared_norm(k):
                if k == 0:
                    mean(N_CKV, width=KVR)
                if k == 7:
                    spread(N_CKV, diag=ckv_diag)

            def ffn(st, xg0, by_halves, after, n_pre, n_post):
                F0 = KF * FFN_STAGE[st]
                u, r = U0[st], R0[st]
                pair(u, (acc[0], acc[1]), xg, xg0, by_halves, after)
                if st == 4:
                    unit(u + 2, acc[2][:], from_x(xg))
                    pe.wait_ge(evacuated, r)
                    unit(u + 3, acc[3][:], from_x(xg), before=shared_norm)
                else:
                    norm_over_two(u, n_pre)
                with pe.Fori(1, KF // 2) as it:
                    for a in range(4):
                        pe.wait_ge(w_lo, u + 4 * it + a + 1)
                        pe.wait_ge(evacuated, r + 4 * it + a - 3)
                        tiles(acc[a][:], a, 0, UT, from_x(xg)).then_inc(unit_done, 1)
                d0, r0 = u + 2 * KF, r + 2 * KF

                def hidden(s, cols=slice(0, S)):
                    return lambda k: (hT[:, 0, UT * s + k, cols], hT[:, 1, UT * s + k, cols])

                for m in range(KD - 1):
                    pe.wait_ge(evacuated, r0 + m - 3)
                    for s in range(ND):
                        def late(k, s=s):
                            pe.wait_ge(hid_lo, F0 + UT * s + k + 1)
                        unit(d0 + ND * m + s, acc[m % 4][:], hidden(s), DOWN[s], start=s == 0, stop=s == ND - 1,
                             before=late if m == 0 else None)
                m = KD - 1
                pe.wait_ge(evacuated, r0 + m - 3)
                for s in range(ND):
                    w = d0 + ND * m + s
                    pe.wait_ge(w_lo, w + 1)
                    ins = tiles(acc[3][:, half(0)], w % SLOTS, 0, DOWN[s], hidden(s, half(0)),
                                start=s == 0, stop=s == ND - 1)
                ins.then_inc(half_psum, 1)
                if n_post == N_F1:
                    pe.wait_ge(evacuated, r0 + 5)
                for s in range(ND):
                    def first_norm(k, s=s):
                        if (s, k) == (0, 4):
                            post_mean(n_post, 0)
                        if (s, k) == (1, 2):
                            post_spread(n_post, 0)
                    unit(d0 + ND * m + s, last_banks(n_post)[0][:, half(1)], hidden(s, half(1)), DOWN[s],
                         start=s == 0, stop=s == ND - 1, before=first_norm)

            def att_dst(st, rr):
                if att_free[st][rr]:
                    pe.wait_ge(evacuated, R0[st] + att_free[st][rr])
                return att_banks[st][rr][:]

            def scores(n, rope_rows=None):
                if n:
                    pe.wait_ge(exp_ready, TS * n)
                for c in range(TS):
                    bank, o = BANK[c]
                    w = max(c + 1, 2) * P
                    dst = sco[bank][:, o:o + w]
                    ins = product(dst, qh[:, 0, c * P:(c + 1) * P], qh[:, 1, c * P:(c + 1) * P],
                                  kh[:, 0, 0:w], kh[:, 1, 0:w], True, rope_rows is None)
                    if rope_rows is not None:
                        rr = slice(rope_rows, rope_rows + ROPE)
                        ins = product(dst, qrT[rr, 0, c * P:(c + 1) * P], qrT[rr, 1, c * P:(c + 1) * P],
                                      krT[rr, 0, 0:w], krT[rr, 1, 0:w], False, True)
                    if c:
                        ins.then_inc(score_psum, 1)

            def prob_transposes(n, pieces):
                pe.wait_ge(prob_ready, TS * (n + 1))
                for b in pieces:
                    if b == 1 and (n + 1) % HEADS:
                        pe.wait_ge(v_lo, n + 2)
                    if b == 2:
                        pe.wait_ge(probT_lo, 3 * n + 1)
                    o = 0
                    for j in PIECES[b]:
                        for c in range(j, TS):
                            ins = t.transpose(piece_bank[b][:, o:o + P], prob_of(n, c, j), ident[:])
                            o += P
                    ins.then_inc(probT_psum, 1)

            def values(n):
                if n:
                    pe.wait_ge(o_lo, n)
                else:
                    pe.wait_ge(evacuated, R0[1] + 7)
                pe.wait_ge(v_lo, n + 1)
                v_h, v_l = values_of(n)
                for j in range(TS):
                    if j < 3:
                        pe.wait_ge(probT_lo, 3 * n + j + 1)
                    w = max(TS - j, 2) * P
                    end = TOFF[j] + (TS - j) * P
                    ins = product(aux[:, S - w:S], v_h[:, j], v_l[:, j], probT[:, 0, end - w:end],
                                  probT[:, 1, end - w:end], j == 0, j == TS - 1)
                ins.then_inc(pv_psum, 1)

            def value_transposes(n, r_count):
                pe.wait_ge(evacuated, r_count)
                for j in range(TS):
                    ins = t.transpose(vT_bank(n)[:, j * P:(j + 1) * P], T[0][:, j * P:(j + 1) * P], ident[:])
                ins.then_inc(vT_psum, 1)

            def out_proj(st, u, r, n, heads, last_scores):
                att = R0[st] + r
                last = heads + HEADS - 1

                def heads_done(m, first, end):
                    if first == 0:
                        pe.wait_ge(w_lo, u + m + 1)
                    return tiles(wo_bank[m][:], (u + m) % SLOTS, 0, end, from_x(oT), start=first == 0,
                                 stop=end == HEADS, k0=first)

                pe.wait_ge(evacuated, att - 1)
                pe.wait_ge(o_lo, last - 2)
                heads_done(0, 0, HEADS - 3)
                value_transposes(last, att)
                prob_transposes(last - 1, (0,))
                last_scores()
                prob_transposes(last - 1, (1,))
                pe.wait_ge(o_lo, last - 1)
                heads_done(0, HEADS - 3, HEADS - 2)
                prob_transposes(last - 1, (2,))
                pe.wait_ge(evacuated, att)
                heads_done(1, 0, HEADS - 2)
                values(last - 1)
                pe.wait_ge(exp_ready, TS * (last + 1))
                heads_done(2, 0, HEADS - 2)
                prob_transposes(last, (0, 1))
                heads_done(3, 0, HEADS - 2)
                prob_transposes(last, (2,))
                values(last)
                for m in range(4):
                    heads_done(m, HEADS - 2, HEADS - 1)
                pe.wait_ge(o_lo, last + 1)
                for m in range(4):
                    heads_done(m, HEADS - 1, HEADS).then_inc(unit_done, 1)
                for m in range(4, KD - 2):
                    unit(u + m, wo_bank[m][:], from_x(oT))
                for m in (KD - 2, KD - 1):
                    pe.wait_ge(evacuated, att + m - (KD - 2) + 1)
                    pe.wait_ge(w_lo, u + m + 1)
                    tiles(wo_bank[m][:, half(0)], (u + m) % SLOTS, 0, UT, from_x(oT, half(0))
                          ).then_inc(half_psum, 1)
                for m in (KD - 2, KD - 1):
                    pe.wait_ge(evacuated, att + m - (KD - 2) + 3)
                    unit(u + m, last_banks(n)[m % 2][:, half(1)], from_x(oT, half(1)),
                         before=(lambda k: post_mean(n, 0) if k == 4 else None) if m == KD - 2 else None)
                    if m == KD - 2:
                        post_spread(n, 0)

            pe.wait_ge(const_ready, 3)
            for k in range(KD):
                pe.wait_ge(x_in[k], 16)
                if k >= 5:
                    pe.wait_ge(x_ready, k - 4)
                for c in range(TS):
                    ins = t.transpose(x_bank[k % 5][:, c * P:(c + 1) * P], xin[:, c, k * P:(k + 1) * P],
                                      ident[:])
                ins.then_inc(x_psum, 1)
                if k == 0:
                    pe.wait_ge(gains_in, 64)
                    t.transpose(aux[:, 0:NG], gin[0:NG, :], ident[0:NG, 0:NG]).then_inc(gains_psum, 1)
            ffn(0, XG0[X_LOAD], False, None, N_PRE0, N_F0)

            u, r = U0[1], R0[1]
            pair(u, (acc[0], acc[1]), xg, XG0[X_F0], True, second_norm(N_F0))
            norm_over_two(u, N_PRE1)

            def qkv_unit(rr):
                unit(u + rr, att_dst(1, rr), from_x(xg))

            qkv_unit(4)
            qkv_unit(5)
            value_transposes(0, r + 3)
            def moba_scores(h):
                pe.wait_ge(part_lo, 2 * (h + 1))
                scores(h)

            for h in range(HEADS - 1):
                moba_scores(h)
                if h:
                    prob_transposes(h - 1, (0, 1))
                    qkv_unit(3 * h + 4)
                    prob_transposes(h - 1, (2,))
                    qkv_unit(3 * h + 5)
                    values(h - 1)
                if h + 2 < HEADS:
                    if h == 0:
                        pe.wait_ge(v_lo, 1)
                    qkv_unit(3 * h + 6)
                if h + 2 < HEADS:
                    value_transposes(h + 1, r + 3 * h + 6)
            out_proj(1, u + 3 * HEADS, 3 * HEADS, N_MOBA, 0, lambda: moba_scores(HEADS - 1))
            ffn(2, XG0[X_MOBA], True, second_norm(N_MOBA), N_PRE2, N_F1)

            u, r = U0[3], R0[3]
            pair(u, (sco[1], sco[2]), xkv, XG0[X_F1], True, second_norm(N_F1))
            unit(u + 2, acc[3][:], from_x(xkv), UT // 2, stop=False)
            unit(u + 3, acc[3][:], lambda k: (xkv[:, 0, UT // 2 + k], xkv[:, 1, UT // 2 + k]), UT // 2, start=False)

            pre = norm_among(N_PRE3, 4, 7)
            ffn(4, XG0[X_F1] + 2 * KD, False, lambda e, k: pre(k), N_CKV, N_F2)

            u, r = U0[5], R0[5]
            pair(u, (acc[0], acc[1]), xg, XG0[X_F2], True, second_norm(N_F2))
            norm_over_two(u, N_PRE4)

            def head_part(a, h, before=None):
                first, n = {"q": (0, KQ), "k": (KQ, KK), "v": (KQ + KK, KK)}[a]
                w = mla_unit(h // 2, h)
                pe.wait_ge(w_lo, w + 1)
                return tiles(att_dst(5, mla_rr[a, h]), w % SLOTS, first, n, from_x(xg if a == "q" else ckT),
                             before=before)

            pe.wait_ge(cq_lo, KK + 1)
            head_part("k", 0).then_inc(head_psum, 1)
            head_part("v", 0).then_inc(head_psum, 1)
            unit(mla_unit(0), att_dst(5, mla_rr["r", 0]), from_x(xg), KQ,
                 before=lambda k: pe.wait_ge(cq_lo, KK + 1 + k + 1))
            value_transposes(HEADS, r + mla_rr["v", 0] + 1)
            head_part("q", 0).then_inc(unit_done, 1)
            head_part("q", 1).then_inc(head_psum, 1)
            mean(N_CQ, width=QR)

            def mla_scores(h):
                pe.wait_ge(evacuated, r + max(mla_rr["q", h], mla_rr["k", h]) + 1)
                pe.wait_ge(part_lo, 2 * HEADS + h // 2 + 1)
                scores(HEADS + h, ROPE * (h % 2))

            for h in range(HEADS - 1):
                n = HEADS + h
                if h:
                    prob_transposes(n - 1, (0,))
                mla_scores(h)
                if h:
                    prob_transposes(n - 1, (1, 2))
                head_part("k", h + 1).then_inc(head_psum, 1)
                head_part("v", h + 1).then_inc(unit_done, 1)
                if h:
                    values(n - 1)
                if h + 2 < HEADS:
                    if h % 2 == 0:
                        gg = (h + 2) // 2
                        unit(mla_unit(gg), att_dst(5, mla_rr["r", gg]), from_x(xg), KQ)
                    head_part("q", h + 2).then_inc(head_psum, 1)
                if h + 2 < HEADS:
                    value_transposes(n + 1, r + mla_rr["v", h + 1] + 1)
            out_proj(5, u + KQ + 12, KQ + 28, N_MLA, HEADS, lambda: mla_scores(HEADS - 1))
            ffn(6, XG0[X_MLA], True, second_norm(N_MLA), N_PRE5, N_F3)

            post_mean(N_F3, 1)
            pe.wait_ge(evacuated, R0[6] + results[6])
            for e in range(2):
                for q in range(KD // 2):
                    i = KD // 2 * e + q
                    if i >= 4:
                        pe.wait_ge(*out_done(i - 4))
                    if i == 1:
                        post_spread(N_F3, 1)
                    for k in (2 * q, 2 * q + 1):
                        pe.wait_ge(x_ready, X0[X_F3] + KD * e + k + 1)
                        for c in range(HT):
                            o = 2 * P * c + P * (k % 2)
                            ins = t.transpose(out_bank[i % 4][:, o:o + P],
                                              xT[:, k, (HT * e + c) * P:(HT * e + c + 1) * P], ident[:])
                    ins.then_inc(x_psum, 1)


_INS = ["x", "norm_gains", "ffn_w1", "ffn_w3", "ffn_w2", "moba_w_qkv", "moba_w_o", "mla_w_dq", "mla_q_norm",
        "mla_w_uq", "mla_w_o", "kv_in_norm", "w_dkv_kr", "kv_norm", "w_ukv"]


def _rope_table(seq, dim, copies):
    import numpy as np

    inv = (np.float32(1.0) / np.float32(10000.0) ** (np.arange(0, dim, 2, dtype=np.float32) / np.float32(dim)))
    ang = np.arange(seq, dtype=np.float32)[:, None] * inv.astype(np.float32)[None, :]
    cos, sin = np.cos(ang).T, np.sin(ang).T
    return np.ascontiguousarray(np.stack([np.concatenate([cos, cos] * copies), np.concatenate([sin, -sin] * copies)])
                                ).astype(np.float32)


def kernel(**inputs):
    import numpy as _np
    import concourse.bacc as _bacc
    from concourse import mybir as _mybir
    from concourse.bass_utils import run_bass_kernel_spmd as _run

    nc = _bacc.Bacc("TRN2", target_bir_lowering=False, num_devices=1)
    arrays, args = {}, []
    for name in _INS:
        arrays[f"in_{name}_dram"] = _np.ascontiguousarray(inputs[name])
    seq = inputs["x"].shape[1]
    arrays["in_rope_a_dram"] = _rope_table(seq, 128, 1)
    arrays["in_rope_r_dram"] = _rope_table(seq, 64, 2)
    for name, a in arrays.items():
        args.append(nc.dram_tensor(name, a.shape, _mybir.dt.from_np(a.dtype), kind="ExternalInput").ap())
    shape = inputs["x"].shape
    args.append(nc.dram_tensor("out_0_dram", shape, _mybir.dt.float32, kind="ExternalOutput").ap())
    yoco_kernel(nc, *args)
    r = _run(nc, [arrays], core_ids=[0])
    return r.results[0]["out_0_dram"]
```
